# Optimizing a Trainium2 kernel written in Bass

```python
import math
import jax
import jax.numpy as jnp
from jax import lax
import numpy as np

D_MODEL = 2048
BATCH = 1
SEQ = 512
DEPTH = 2
DEC_BATCH = 8
DEC_SEQ = 1
PAST_LEN = 512
PAGE_SIZE = 128

N_META = 16
NORM_EPS = 1e-6
POOL_WIDTH = D_MODEL // 2
POOL_WINDOWS = (2, 4, 8, 16)
POOL_GROUP = POOL_WIDTH // len(POOL_WINDOWS)
POOL_CTX = max(POOL_WINDOWS) - 1
ATTN_WIDTH = D_MODEL // 2
DA_HEADS = 8
DA_VDIM = ATTN_WIDTH // DA_HEADS
DA_QKDIM = DA_VDIM // 2
DA_SCALE = DA_QKDIM ** -0.5
ROT_DIM = DA_QKDIM // 4
ROPE_THETA = 500000.0
LAMBDA_INIT = 0.8 - 0.6 * math.exp(-0.3 * 0)
Q_BLOCK = 128
EVEN_SPLITS = [POOL_WIDTH, 2 * POOL_WIDTH, 2 * POOL_WIDTH + ATTN_WIDTH,
               2 * POOL_WIDTH + 2 * ATTN_WIDTH, 2 * POOL_WIDTH + 3 * ATTN_WIDTH]
EVEN_IN = 2 * POOL_WIDTH + 4 * ATTN_WIDTH
GLA_HEADS = 4
GLA_KW = D_MODEL // 2
GLA_VW = D_MODEL
GLA_KDIM = GLA_KW // GLA_HEADS
GLA_VDIM = GLA_VW // GLA_HEADS
GLA_RANK = 16
GLA_TAU = 16.0
GLA_CHUNK = 64
ODD_SPLITS = [GLA_KW, 2 * GLA_KW, 2 * GLA_KW + GLA_VW, 2 * GLA_KW + 2 * GLA_VW]
ODD_IN = 2 * GLA_KW + 2 * GLA_VW + GLA_RANK

kernel_name = 'meta_pool_diffattn_gla_decode_step'

def rms_norm(x, g):
    xf = x.astype(jnp.float32)
    y = xf * lax.rsqrt(jnp.mean(xf * xf, axis=-1, keepdims=True) + NORM_EPS)
    return (y * g.astype(jnp.float32)).astype(x.dtype)

def partial_rope(x, positions):
    half = ROT_DIM // 2
    inv = jnp.power(ROPE_THETA, -jnp.arange(half, dtype=jnp.float32) * 2.0 / ROT_DIM)
    ang = positions.astype(jnp.float32)[:, None] * inv[None, :]
    cos = jnp.cos(ang)[None, :, None, None, :]
    sin = jnp.sin(ang)[None, :, None, None, :]
    xf = x.astype(jnp.float32)
    x1 = xf[..., :half]
    x2 = xf[..., half:ROT_DIM]
    out = jnp.concatenate([x1 * cos - x2 * sin, x2 * cos + x1 * sin, xf[..., ROT_DIM:]], axis=-1)
    return out.astype(x.dtype)

def multiscale_pool(u, prev, positions):
    T = u.shape[1]
    ext = jnp.concatenate([prev.astype(u.dtype), u], axis=1)
    cs = jnp.cumsum(ext.astype(jnp.float32), axis=1)
    cs = jnp.pad(cs, ((0, 0), (1, 0), (0, 0)))
    means = []
    for gi, w in enumerate(POOL_WINDOWS):
        c0, c1 = gi * POOL_GROUP, (gi + 1) * POOL_GROUP
        hi = cs[:, POOL_CTX + 1:POOL_CTX + 1 + T, c0:c1]
        lo = cs[:, POOL_CTX + 1 - w:POOL_CTX + 1 - w + T, c0:c1]
        cnt = jnp.minimum(w, positions + 1).astype(jnp.float32)
        means.append((hi - lo) / cnt[None, :, None])
    mean = jnp.concatenate(means, axis=-1)
    return (mean - u.astype(jnp.float32)).astype(u.dtype), ext[:, -POOL_CTX:]

def diff_attn_prompt(q, k, v, lam):
    B, L = q.shape[0], q.shape[1]
    n_blk = -(-L // Q_BLOCK)
    pad = n_blk * Q_BLOCK - L
    qb = jnp.pad(q, ((0, 0), (0, pad), (0, 0), (0, 0), (0, 0)))
    qb = qb.reshape(B, n_blk, Q_BLOCK, DA_HEADS, 2, DA_QKDIM).transpose(1, 0, 2, 3, 4, 5)
    starts = jnp.arange(n_blk, dtype=jnp.int32) * Q_BLOCK
    key_pos = jnp.arange(L, dtype=jnp.int32)

    def block(args):
        q_blk, start = args
        q_pos = start + jnp.arange(Q_BLOCK, dtype=jnp.int32)
        s = jnp.einsum('bqhmd,bkhmd->bhmqk', q_blk, k).astype(jnp.float32) * DA_SCALE
        s = jnp.where(key_pos[None, :] <= q_pos[:, None], s, -jnp.inf)
        p = jax.nn.softmax(s, axis=-1)
        pd = p[:, :, 0] - lam * p[:, :, 1]
        return jnp.einsum('bhqk,bkhe->bqhe', pd.astype(v.dtype), v)

    o = lax.map(block, (qb, starts))
    return o.transpose(1, 0, 2, 3, 4).reshape(B, n_blk * Q_BLOCK, DA_HEADS, DA_VDIM)[:, :L]

def diff_attn_sample(q, k, v, k_past, v_past, lam):
    S = q.shape[1]
    P = k_past.shape[1]
    s_past = jnp.einsum('bqhmd,bkhmd->bhmqk', q, k_past).astype(jnp.float32)
    s_new = jnp.einsum('bqhmd,bkhmd->bhmqk', q, k).astype(jnp.float32)
    s_new = jnp.where(jnp.tril(jnp.ones((S, S), dtype=bool)), s_new, -jnp.inf)
    p = jax.nn.softmax(jnp.concatenate([s_past, s_new], axis=-1) * DA_SCALE, axis=-1)
    pd = (p[:, :, 0] - lam * p[:, :, 1]).astype(v.dtype)
    return (jnp.einsum('bhqk,bkhe->bqhe', pd[..., :P], v_past)
            + jnp.einsum('bhqk,bkhe->bqhe', pd[..., P:], v))

def even_layer(h, positions, pool_prev, kv_past, pre_g, post_g, w_in, pool_w, pool_scale,
               lq1, lk1, lq2, lk2, subln_g, w_out):
    B, T, _ = h.shape
    z = rms_norm(h, pre_g) @ w_in
    u, pool_gate, q, k, v, attn_gate = jnp.split(z, EVEN_SPLITS, axis=-1)
    d, pool_state = multiscale_pool(u, pool_prev, positions)
    pool_out = jnp.einsum('btgc,gcd->btgd', d.reshape(B, T, len(POOL_WINDOWS), POOL_GROUP), pool_w)
    pool_out = pool_out.reshape(B, T, POOL_WIDTH) * pool_scale
    q = partial_rope(q.reshape(B, T, DA_HEADS, 2, DA_QKDIM), positions)
    k = partial_rope(k.reshape(B, T, DA_HEADS, 2, DA_QKDIM), positions)
    v = v.reshape(B, T, DA_HEADS, DA_VDIM)
    lam = (jnp.exp(jnp.sum(lq1.astype(jnp.float32) * lk1.astype(jnp.float32)))
           - jnp.exp(jnp.sum(lq2.astype(jnp.float32) * lk2.astype(jnp.float32))) + LAMBDA_INIT)
    if kv_past is None:
        o = diff_attn_prompt(q, k, v, lam)
    else:
        o = diff_attn_sample(q, k, v, kv_past[0], kv_past[1], lam)
    o = rms_norm(o, subln_g) * (1.0 - LAMBDA_INIT)
    mix = jnp.concatenate([pool_out * jax.nn.silu(pool_gate),
                           o.reshape(B, T, ATTN_WIDTH) * jax.nn.silu(attn_gate)], axis=-1)
    h = h + rms_norm(mix @ w_out, post_g)
    return h, k.reshape(B, T, DA_HEADS, 2 * DA_QKDIM), v, pool_state

def gla_scan(q, k, v, g, s0, chunk):
    B, T = q.shape[0], q.shape[1]
    n = T // chunk

    def to_chunks(a):
        return a.reshape(B, n, chunk, GLA_HEADS, a.shape[-1]).transpose(1, 0, 3, 2, 4)

    causal = jnp.tril(jnp.ones((chunk, chunk), dtype=bool))[:, :, None]

    def step(state, xs):
        qc, kc, vc, gc = xs
        b = jnp.cumsum(gc, axis=2)
        o_inter = jnp.einsum('bhtd,bhde->bhte', qc * jnp.exp(b), state)
        decay = jnp.exp(jnp.where(causal, b[:, :, :, None, :] - b[:, :, None, :, :], -jnp.inf))
        scores = jnp.einsum('bhtsd,bhsd->bhts', qc[:, :, :, None, :] * decay, kc)
        o = o_inter + jnp.einsum('bhts,bhse->bhte', scores, vc)
        b_last = b[:, :, -1:, :]
        state = (jnp.exp(b_last[:, :, 0, :])[..., None] * state
                 + jnp.einsum('bhsd,bhse->bhde', kc * jnp.exp(b_last - b), vc))
        return state, o

    state, o = lax.scan(step, s0.astype(jnp.float32),
                        (to_chunks(q), to_chunks(k), to_chunks(v), to_chunks(g)))
    o = o.transpose(1, 0, 3, 2, 4).reshape(B, T, GLA_HEADS, GLA_VDIM)
    return o, state

def odd_layer(h, s0, has_meta, pre_g, post_g, w_in, wa2, ba, norm_g, w_out):
    B, T, _ = h.shape
    z = rms_norm(h, pre_g) @ w_in
    q, k, v, gate, lr = jnp.split(z, ODD_SPLITS, axis=-1)
    q = q.reshape(B, T, GLA_HEADS, GLA_KDIM) * (GLA_KDIM ** -0.5)
    k = k.reshape(B, T, GLA_HEADS, GLA_KDIM)
    v = v.reshape(B, T, GLA_HEADS, GLA_VDIM)
    g = jax.nn.log_sigmoid((lr @ wa2 + ba).astype(jnp.float32)) / GLA_TAU
    g = g.reshape(B, T, GLA_HEADS, GLA_KDIM)
    if has_meta:
        o_m, st = gla_scan(q[:, :N_META], k[:, :N_META], v[:, :N_META], g[:, :N_META], s0, N_META)
        o_r, st = gla_scan(q[:, N_META:], k[:, N_META:], v[:, N_META:], g[:, N_META:], st, GLA_CHUNK)
        o = jnp.concatenate([o_m, o_r], axis=1)
    else:
        o, st = gla_scan(q, k, v, g, s0, T)
    o = rms_norm(o.astype(h.dtype), norm_g).reshape(B, T, GLA_VW) * jax.nn.silu(gate)
    h = h + rms_norm(o @ w_out, post_g)
    return h, st

def setup_inputs(seed: int = 0) -> dict:
    key = jax.random.key(seed)
    ks = jax.random.split(key, 32)
    f32 = jnp.float32
    n_pages = PAST_LEN // PAGE_SIZE
    n_used = DEC_BATCH * n_pages
    n_phys = n_used + max(1, n_used // 4)
    nrm = lambda i, shape, s: jax.random.normal(ks[i], shape, f32) * s
    gain = lambda i, n: 1.0 + 0.02 * jax.random.normal(ks[i], (n,), f32)
    page_table = jax.random.permutation(ks[6], n_phys)[:n_used].reshape(DEC_BATCH, n_pages).astype(jnp.int32)
    return {
        'x_prompt': nrm(0, (BATCH, SEQ, D_MODEL), 1.0),
        'x_sample': nrm(1, (DEC_BATCH, DEC_SEQ, D_MODEL), 1.0),
        'cache_k': nrm(2, (n_phys, PAGE_SIZE, DA_HEADS, 2 * DA_QKDIM), 1.0),
        'cache_v': nrm(3, (n_phys, PAGE_SIZE, DA_HEADS, DA_VDIM), 1.0),
        'state_pool': nrm(4, (DEC_BATCH, POOL_CTX, POOL_WIDTH), 1.0),
        'state_gla': nrm(5, (DEC_BATCH, GLA_HEADS, GLA_KDIM, GLA_VDIM), 1.0),
        'page_table': page_table,
        'meta_tokens': nrm(7, (N_META, D_MODEL), 1.0),
        'pre_norm_0': gain(8, D_MODEL),
        'post_norm_0': gain(9, D_MODEL),
        'w_in_0': nrm(10, (D_MODEL, EVEN_IN), D_MODEL ** -0.5),
        'pool_w_0': nrm(11, (len(POOL_WINDOWS), POOL_GROUP, POOL_GROUP), POOL_GROUP ** -0.5),
        'pool_scale_0': gain(12, POOL_WIDTH),
        'lambda_q1_0': nrm(13, (DA_QKDIM,), 0.1),
        'lambda_k1_0': nrm(14, (DA_QKDIM,), 0.1),
        'lambda_q2_0': nrm(15, (DA_QKDIM,), 0.1),
        'lambda_k2_0': nrm(16, (DA_QKDIM,), 0.1),
        'subln_0': gain(17, DA_VDIM),
        'w_out_0': nrm(18, (POOL_WIDTH + ATTN_WIDTH, D_MODEL), (POOL_WIDTH + ATTN_WIDTH) ** -0.5),
        'pre_norm_1': gain(19, D_MODEL),
        'post_norm_1': gain(20, D_MODEL),
        'w_in_1': nrm(21, (D_MODEL, ODD_IN), D_MODEL ** -0.5),
        'gla_wa2_1': nrm(22, (GLA_RANK, GLA_KW), GLA_RANK ** -0.5),
        'gla_ba_1': nrm(23, (GLA_KW,), 0.01),
        'gla_norm_1': gain(24, GLA_VDIM),
        'w_out_1': nrm(25, (GLA_VW, D_MODEL), GLA_VW ** -0.5),
    }

def reference(x_prompt, x_sample, cache_k, cache_v, state_pool, state_gla, page_table, meta_tokens,
              pre_norm_0, post_norm_0, w_in_0, pool_w_0, pool_scale_0, lambda_q1_0, lambda_k1_0,
              lambda_q2_0, lambda_k2_0, subln_0, w_out_0,
              pre_norm_1, post_norm_1, w_in_1, gla_wa2_1, gla_ba_1, gla_norm_1, w_out_1):
    B = x_prompt.shape[0]
    Bd, S = x_sample.shape[0], x_sample.shape[1]
    meta = jnp.broadcast_to(meta_tokens[None].astype(x_prompt.dtype), (B, N_META, D_MODEL))
    h_p = jnp.concatenate([meta, x_prompt], axis=1)
    L = h_p.shape[1]
    pos_p = jnp.arange(L, dtype=jnp.int32)
    pos_s = PAST_LEN + jnp.arange(S, dtype=jnp.int32)
    n_pages = page_table.shape[1]
    k_past = cache_k[page_table].reshape(Bd, n_pages * PAGE_SIZE, DA_HEADS, 2, DA_QKDIM)
    v_past = cache_v[page_table].reshape(Bd, n_pages * PAGE_SIZE, DA_HEADS, DA_VDIM)
    h_s = x_sample
    for layer in range(DEPTH):
        if layer % 2 == 0:
            pool_zero = jnp.zeros((B, POOL_CTX, POOL_WIDTH), h_p.dtype)
            h_p, k_new_p, v_new_p, pool_new_p = even_layer(
                h_p, pos_p, pool_zero, None, pre_norm_0, post_norm_0, w_in_0, pool_w_0, pool_scale_0,
                lambda_q1_0, lambda_k1_0, lambda_q2_0, lambda_k2_0, subln_0, w_out_0)
            h_s, k_new_s, v_new_s, pool_new_s = even_layer(
                h_s, pos_s, state_pool, (k_past, v_past), pre_norm_0, post_norm_0, w_in_0, pool_w_0,
                pool_scale_0, lambda_q1_0, lambda_k1_0, lambda_q2_0, lambda_k2_0, subln_0, w_out_0)
        else:
            s_zero = jnp.zeros((B, GLA_HEADS, GLA_KDIM, GLA_VDIM), jnp.float32)
            h_p, gla_new_p = odd_layer(h_p, s_zero, True, pre_norm_1, post_norm_1, w_in_1,
                                       gla_wa2_1, gla_ba_1, gla_norm_1, w_out_1)
            h_s, gla_new_s = odd_layer(h_s, state_gla, False, pre_norm_1, post_norm_1, w_in_1,
                                       gla_wa2_1, gla_ba_1, gla_norm_1, w_out_1)
    gla_new_p = gla_new_p.astype(state_gla.dtype)
    gla_new_s = gla_new_s.astype(state_gla.dtype)
    return (h_p[:, N_META:], h_s, k_new_p, v_new_p, pool_new_p, gla_new_p,
            k_new_s, v_new_s, pool_new_s, gla_new_s)


_drawn_inputs = setup_inputs


def setup_inputs(seed=0):
    import zlib

    import numpy as np

    out = dict(_drawn_inputs(seed))
    spreads = {}
    factors = {'post_norm_0': 2.733,
     'pool_scale_0': 3.887,
     'subln_0': 4.21,
     'post_norm_1': 4.969,
     'gla_ba_1': 8.0,
     'gla_norm_1': 5.005}
    for name, (base, spread) in spreads.items():
        noise = np.random.default_rng([zlib.crc32(name.encode()), seed]).standard_normal(out[name].shape)
        drawn = base * np.exp(spread * noise) if base else spread * noise
        out[name] = jnp.asarray(drawn.astype(out[name].dtype))
    for name, factor in factors.items():
        out[name] = (out[name] * factor).astype(out[name].dtype)
    return out
```

```python
from contextlib import ExitStack

import numpy as np

import concourse.bass as bass
from concourse import mybir

F32 = mybir.dt.float32
F32R = mybir.dt.float32r
I32 = mybir.dt.int32
ALU = mybir.AluOpType
ACT = mybir.ActivationFunctionType
AX = mybir.AxisListType

P = 128
D = 2048
KT = D // P
HC = KT // 2
META, SEQ, NB = 16, 512, 8
TP = META + SEQ
T = TP + NB
TH = T // 2
TT = 4
TAIL = TP - TT * P
TB = T - TT * P
EPS = 1e-6
NH, PAIRS = 8, 4
PAGE, NPG = 128, 4
SCALE = 64 ** -0.5
LAM_INIT = 0.2
CTX = 15
GH, GK, GV, RANK, TAU = 4, 256, 512, 16, 16.0
SUB = 32
PRE0, POST0, PRE1, POST1, PSC, BA, GN, SUBG, SUBG8 = 0, 16, 32, 48, 64, 72, 80, 84, 85
C_U, C_PG, C_Q, C_K, C_V, C_AG = (1024 * i for i in range(6))
G_Q, G_K, G_V, G_G, G_LR = 0, 1024, 2048, 4096, 6144
KOFF = [0, 32, 96, 192]
KLEN = 320
PHYS = 40


class Signal:

    def __init__(self, sem, phases, by=1):
        self.sem, self.by, self.start, self.names, start = sem, by, {}, {}, 0
        for phase, names, times in phases:
            self.start[phase], self.names[phase] = start, list(names)
            start += len(names) * times
        self.total = start * by

    def at(self, phase, name, i=0):
        names = self.names[phase]
        return self.sem, (i * len(names) + (self.start[phase] + names.index(name) + 1)) * self.by

    def before(self, phase, name, i=0):
        names = self.names[phase]
        return self.sem, (i * len(names) + (self.start[phase] + names.index(name))) * self.by


PAIR_TILES = ["qA", "kA", "vA", "gA", "qB", "kB", "vB", "gB", "u0", "u1", "p0", "p1"]
PAIR_PLAN = {
    2: "RQ0A RQ1A", 4: "RK0A RK1A", 5: "KT0A KT1A", 6: "VT0A VT1A",
    8: "S0A", 9: "PT0A S1A", 10: "PT1A O0A S2A RQ0B RQ1B", 11: "PT2A O1A S3A",
    12: "PT3A O2A S4A RK0B RK1B", 13: "PT4A O3A KT0B KT1B", 14: "O4A VT0B VT1B", 15: "SS0A SS1A",
    16: "S0B SG", 17: "PT0B S1B", 18: "PT1B O0B S2B", 19: "PT2B O1B S3B",
    20: "PT3B O2B S4B UT", 21: "PT4B O3B", 22: "O4B ST",
    23: "SS0B SS1B SD PO00 PO01 PO10 PO11 OS SN",
}
HEAD_LINKS = 21
HEAD_LINKS_ACT = 4
HEAD_TILES = ["q0", "q1", "k0", "k1", "v0", "v1", "v2", "v3", "g0", "g1", "g2", "g3"]
HEAD_PLAN = {
    0: "G00 G01", 1: "G10 G11", 10: "VT00 VT10", 12: "VT01 VT11", 14: "VT02 VT12",
    15: "SK0", 16: "VT03 VT13", 17: "OC0 SU00 SU01 SK1", 18: "OC1 SU10 SU11 SK2",
    19: "OC2 SU20 SU21 SK3 B0 B1", 20: "OC3 SU30 SU31 SK4 B2 B3", 21: "OC4 SU40 SU41 B4 B5",
    22: "B6 B7", 23: "SS0 SS1",
}
PAIR_OPS = [x for s in range(24) for x in PAIR_PLAN.get(s, "").split()]
HEAD_OPS = [x for s in range(24) for x in HEAD_PLAN.get(s, "").split()]
PAIR_JOBS = [x for x in PAIR_OPS if x not in [f"S{t}{h}" for t in range(5) for h in "AB"]]
HEAD_JOBS = [x for x in HEAD_OPS if x[0] != "B"]
JOBS = {"pair": PAIR_JOBS, "head": HEAD_JOBS}
BY_ACT = {"pair": [j for j in PAIR_JOBS if j[:2] in ("KT", "VT", "SS", "UT", "SN")],
          "head": [j for j in HEAD_JOBS if j[:2] in ("VT", "OC", "SS")]}
BY_DVE = {p: [j for j in JOBS[p] if j not in BY_ACT[p]] for p in JOBS}
ATTN = [f"{t}{h}" for h in "AB" for t in range(5)]
N_OUT0 = len(PAIR_TILES) * PAIRS
N_LR = N_OUT0 + KT
N_HEAD = N_LR + 1
N_OUT1 = N_HEAD + len(HEAD_TILES) * GH
N_END = N_OUT1 + KT
X_IN0, X_OUT0, X_IN1, X_OUT1 = 0, KT, 2 * KT, 3 * KT


def constants():
    ident = np.eye(P)
    causal = np.where(np.arange(P)[None, :] <= np.arange(P)[:, None], 0.0, -1e30)
    rot = np.zeros((P, P))
    rows = np.arange(P) % 64
    for r in range(P):
        if rows[r] < 8:
            rot[r + 8, r] = -1.0
        elif rows[r] < 16:
            rot[r - 8, r] = 1.0
    pos = np.concatenate([np.arange(TP), np.full(NB, 512)]).astype(np.float64)
    inv = 500000.0 ** (-(np.arange(8) * 2.0) / 16)
    ang = pos[None, :] * inv[rows % 8][:, None]
    on = (rows < 16)[:, None]
    cos, sin = np.where(on, np.cos(ang), 1.0), np.where(on, np.sin(ang), 0.0)
    tail = np.zeros((P, 16 + 16 + 2 + 16 + 2))
    for m in range(2):
        for t in range(TAIL):
            r = TAIL * m + t
            tail[r, t] = 1.0
            tail[r, 16:32] = np.where(np.arange(TAIL) <= t, 0.0, -1e30)
            tail[r, 32 + m] = 1.0
    for r in range(4 * NB):
        tail[r, 34 + r // 2] = 1.0
        tail[r, 50 + r % 2] = 1.0
    both = np.concatenate([ident, np.ones((P, P))], 1)
    first = np.concatenate([causal, rot, cos, sin, tail], 1)
    count = np.stack([1.0 / np.minimum(w, np.arange(16) + 1) for w in (2, 4, 8, 16)]).reshape(1, 64)
    first = np.concatenate([first, np.repeat(count, P, 0)], 1)
    lower = (np.arange(P)[:, None] <= np.arange(P)[None, :]).astype(float)
    return [np.ascontiguousarray(a, dtype=np.float32) for a in (both, first, lower)]


def build(nc, A, O, n_both, n_first, n_second):
    y_prompt, y_sample, k_prompt, v_prompt, pool_prompt, gla_prompt, k_sample, v_sample, pool_sample, gla_sample = O
    ctx = ExitStack()
    with ctx:
        def sb(name, shape, dt=F32, where=ctx):
            return where.enter_context(nc.sbuf_tensor(name, shape, dt))

        def sem(name):
            return ctx.enter_context(nc.semaphore(name))

        h_dram = nc.dram_tensor("h_residual", [2, KT, P, T], F32, kind="Internal").ap()
        q_dram = nc.dram_tensor("q_sample_rows", [PAIRS, NB, 2 * P], F32, kind="Internal").ap()
        sn_dram = nc.dram_tensor("new_key_scores", [PAIRS, NB, 4], F32, kind="Internal").ap()
        vs_dram = nc.dram_tensor("v_sample_rows", [GH, NB, GV], F32, kind="Internal").ap()

        xhi = sb("xhi", [P, KT, T], F32R)
        xlo = sb("xlo", [P, KT, T], F32R)
        mix = sb("mix", [P, KT, T])
        wraw = sb("wraw", [P, 2, HC, P])
        whi = sb("whi", [P, 4, HC, P], F32R)
        wlo = sb("wlo", [P, 4, HC, P], F32R)
        both = sb("both", [P, n_both])
        cols = sb("cols", [P, 96])
        rstd = sb("rstd", [P, 2, TH])
        tz = sb("tz", [P, 2, TH])
        te = sb("te", [P, 2, TH])
        stat = sb("stat", [P, 32])
        ident, ones = both[:, 0:P], both[:, P:2 * P]
        tzf = tz[:].rearrange("p a t -> p (a t)")
        tef = te[:].rearrange("p a t -> p (a t)")
        rstdf = rstd[:].rearrange("p a t -> p (a t)")

        proj = [ctx.enter_context(nc.psum_tensor(f"proj{i}", [P, 2, 512], F32)) for i in range(2)]
        score = ctx.enter_context(nc.psum_tensor("score", [P, 1024], F32))
        scratch = [ctx.enter_context(nc.psum_tensor(f"scratch{i}", [P, 512], F32)) for i in range(2)]
        banks = [proj[0][:, 0, :], proj[0][:, 1, :], proj[1][:, 0, :], proj[1][:, 1, :],
                 score[:, 0:512], score[:, 512:1024], scratch[0][:], scratch[1][:]]

        s_const = sem("s_const")
        s_xin = [sem(f"s_xin{i}") for i in range(5)]
        s_xt = sem("s_xt")
        s_xd, s_xa = sem("s_xd"), sem("s_xa")
        s_raw = [sem("s_raw0"), sem("s_raw1")]
        s_hi, s_lo = sem("s_hi"), sem("s_lo")
        s_tile = sem("s_tile")
        s_evac = sem("s_evac")
        s_xhi, s_x = sem("s_xhi"), sem("s_x")
        s_sq, s_acc = sem("s_sq"), sem("s_acc")
        s_ss, s_lnr, s_rstd = sem("s_ss"), sem("s_lnr"), sem("s_rstd")
        s_hst, s_hld = sem("s_hst"), [sem("s_hld0"), sem("s_hld1")]
        s_yt, s_hn = sem("s_yt"), sem("s_hn")
        s_ye = sem("s_ye")
        s_yout = [sem(f"s_yout{i}") for i in range(4)]
        s_fT, s_fd2, s_fa2 = sem("s_fT"), sem("s_fd2"), sem("s_fa2")
        s_lam, s_v = sem("s_lam"), sem("s_v")
        s_a, s_vc = sem("s_a"), sem("s_vc")
        s_full = sem("s_full")
        s_fd, s_fa = sem("s_fd"), sem("s_fa")
        s_store = sem("s_store")

        full = Signal(s_full, [("pair", PAIR_JOBS, PAIRS), ("head", HEAD_JOBS, GH)])
        free_d = Signal(s_fd, [("credit", "ab", 1), ("pair", BY_DVE["pair"], PAIRS), ("head", BY_DVE["head"], GH)])
        free_a = Signal(s_fa, [("credit", "ab", 1), ("pair", BY_ACT["pair"], PAIRS), ("head", BY_ACT["head"], GH)])

        def freed(phase, job, i):
            return (free_a if job in BY_ACT[phase] else free_d).at(phase, job, i)

        def freed_back(phase, job, i):
            sig = free_a if job in BY_ACT[phase] else free_d
            names = sig.names[phase]
            return sig.sem, i * len(names) + (sig.start[phase] + names.index(job) + 1 - len(names))

        def bank_of(phase, job):
            return scratch[JOBS[phase].index(job) % 2]

        class Chain:
            def __init__(self, sem, eng):
                self.sem, self.eng, self.base, self.n, self.i, self.per = sem, eng, 0, 0, None, 0

            def enter(self, i, per):
                self.base += self.n
                self.n, self.i, self.per = 0, i, per

            def leave(self, times):
                assert self.n == self.per, (self.n, self.per)
                self.base += self.per * times
                self.n, self.i = 0, None

            def link(self, ins):
                self.mark(ins)
                self.eng.wait_ge(self.sem, self.value())

            def mark(self, ins):
                ins.then_inc(self.sem, 1)
                self.n += 1

            def value(self):
                return self.base + self.n + (0 if self.i is None else self.i * self.per)


        sig = lambda name, *phases, by=1: Signal(sem(name), phases, by)
        score_ready = sig("scores_ready", ("pair", ATTN, PAIRS))
        max_ready = sig("max_ready", ("pair", ATTN + ["s"], PAIRS))
        exp_done = sig("exp_done", ("pair", ATTN + ["s"], PAIRS))
        pd_ready = sig("pd_ready", ("pair", ATTN + ["s"], PAIRS))
        rope_ready = sig("rope_ready", ("pair", ["qA", "kA", "qB", "kB"], PAIRS))
        osq_ready = sig("osq_ready", ("pair", ["A", "B", "s"], PAIRS))
        ro_ready = sig("ro_ready", ("pair", ["A", "B", "s"], PAIRS), ("head", ["o"], GH))
        gexp_ready = sig("gexp_ready", ("pair", ["gA", "gB", "p0", "p1"], PAIRS), ("head", ["g0", "g1", "g2", "g3"], GH))
        s_qk, s_kout = sem("s_qk"), sem("s_kout")
        s_vout = [sem("s_vout0"), sem("s_vout1")]
        s_sg, s_pw, s_uout = sem("s_sg"), sem("s_pw"), sem("s_uout")
        s_qb = [sem("s_qb0"), sem("s_qb1")]
        s_kv = [sem("s_kv0"), sem("s_kv1")]
        s_prod, s_kred, s_pv = sem("s_prod"), sem("s_kred"), sem("s_pv")
        s_snr, s_sns, s_sn = sem("s_snr"), sem("s_sns"), sem("s_sn")
        s_d, s_mix = sem("s_d"), sem("s_mix")
        s_init = sem("s_init")
        s_qblk = sem("s_qblk")
        s_c1 = sem("s_c1")
        s_lr = sem("s_lr")
        s_zg, s_ga, s_g = sem("s_zg"), sem("s_ga"), sem("s_g")
        s_b, s_refs, s_last = sem("s_b"), sem("s_refs"), sem("s_last")
        s_gqk = sem("s_gqk")
        chunks = [str(c) for c in range(5)]
        dq_ready = sig("dq_ready", ("head", chunks, GH))
        dec_ready = sig("decays_ready", ("head", chunks, GH))
        fac_ready = sig("factors_ready", ("head", chunks, GH))
        ed_exp = sig("ed_exp", ("head", chunks[1:], GH))
        ed_ready = sig("ed_ready", ("head", chunks[1:], GH))
        s_c0, s_wa2, s_cols = sem("s_c0"), sem("s_wa2"), sem("s_cols")
        s_vs, s_vb = sem("s_vs"), [sem("s_vb0"), sem("s_vb1")]
        s_st, s_sdec, s_snew = [sem("s_st0"), sem("s_st1")], sem("s_sdec"), sem("s_snew")
        s_so = sem("s_so")
        s_sout = [sem("s_sout0"), sem("s_sout1")]
        s_gout, s_gvout, s_osg = sem("s_gout"), sem("s_gvout"), sem("s_osg")
        s_gacc, s_gsq = sem("s_gacc"), sem("s_gsq")
        s_head = sem("s_head")

        stage = ExitStack()
        xin = [sb(f"xin{i}", [P, D], where=stage) for i in range(5)]
        acc0 = sb("acc0", [P, T], where=stage)
        rows = sb("rows", [85, P], where=stage)
        stage.close()
        stage = ExitStack()
        sb0 = lambda name, shape, dt=F32: sb(name, shape, dt, stage)
        first = sb0("first", [P, n_first])
        causal, rot = first[:, 0:P], first[:, P:2 * P]
        cos, sin = first[:, 256:256 + T], first[:, 256 + T:256 + 2 * T]
        o = 256 + 2 * T
        tsel, tmask, tmap = first[:, o:o + 16], first[:, o + 16:o + 32], first[:, o + 32:o + 34]
        ssel, smap = first[:, o + 34:o + 50], first[:, o + 50:o + 52]
        counts = first[:, o + 52:o + 116].rearrange("p (g t) -> p g t", g=4)
        qT = [sb0(f"qT{i}", [P, T]) for i in range(2)]
        kT = [sb0(f"kT{i}", [P, T]) for i in range(2)]
        qblk = sb0("qblk", [P, 2 * TAIL])
        ktok = sb0("ktok", [P, TT, P])
        qk_tok = sb0("qk_tok", [32, 2, 2, P])
        vtok = [sb0(f"vtok{i}", [P, TT + 1, P]) for i in range(2)]
        vs = sb0("vs", [P, 2, NB])
        probw = sb0("probw", [P, 2 * (16 + TP)])
        pd = sb0("pd", [P, T])
        pdT = [sb0(f"pdT{i}", [P, 512]) for i in range(2)]
        oT = sb0("oT", [P, T])
        kv = [sb0(f"kv{i}", [P, NPG, 2 * P]) for i in range(2)]
        qb = [sb0(f"qb{i}", [P, 2 * P]) for i in range(2)]
        sall = sb0("sall", [P, NPG, 4 * NB])
        sprob = sb0("sprob", [4 * NB, 512])
        pds = sb0("pds", [P, 80])
        enew = sb0("enew", [4 * NB, 2 * NB])
        small = sb0("small", [P, 48])
        small2 = sb0("small2", [P, 48])
        ub = sb0("ub", [P, 2, 16 + T])
        pw = sb0("pw", [P, 2, 256])
        spool = sb0("spool", [NB * CTX, 256])
        utok = sb0("utok", [32, 256])
        lam4 = sb0("lam4", [P, 4, 64])
        lam = sb0("lam", [P, 8])
        pages = sb0("pages", [1, NB * NPG], I32)
        prob = probw[:, 0:2 * TP].rearrange("p (m t) -> p m t", m=2)
        win = [probw[:, 0:16 + TP], probw[:, 16 + TP:2 * (16 + TP)]]
        stage.close()
        stage = ExitStack()
        sb1 = lambda name, shape, dt=F32: sb(name, shape, dt, stage)
        hbuf = sb1("hbuf", [P, 2, T])
        acc = sb1("acc", [P, T])
        stage.close()
        stage = ExitStack()
        lower = sb1("lower", [P, n_second])
        lrT = sb1("lrT", [RANK, T])
        wa2 = sb1("wa2", [RANK, GK])
        gq = sb1("gq", [P, 2, T])
        gk = sb1("gk", [P, 2, T])
        gb = sb1("gb", [P, 2, T])
        gv = sb1("gv", [P, TT + 1, GV])
        eq = sb1("eq", [P, 2, P])
        ek = sb1("ek", [P, 2, KLEN])
        ed = sb1("ed", [P, 2, P])
        el = sb1("el", [P, 2, P])
        kd = [sb1(f"kd{i}", [P, GK]) for i in range(2)]
        st = [sb1(f"st{i}", [P, P]) for i in range(2)]
        state = sb1("state", [P, 2, GV])
        og = sb1("og", [P, 4, T])
        refs = sb1("refs", [P, 2, 17])
        lastr = sb1("lastr", [P, 2, 5])
        elast = sb1("elast", [P, 2, 5])
        eg = sb1("eg", [P, 2, NB])
        sst = [sb1(f"sst{i}", [P, 2, GV]) for i in range(2)]
        vb = [sb1(f"vb{i}", [P, GV]) for i in range(2)]
        stage.close()

        w_in0, w_out0, w_in1, w_out1 = A["w_in_0"], A["w_out_0"], A["w_in_1"], A["w_out_1"]
        eps, one = stat[:, 0:1], stat[:, 1:2]
        score2 = score[:].rearrange("p (b n) -> p b n", b=2)
        acc_of = [acc0, acc, acc, acc]
        sq_of = [tzf, tef]

        def tile_at(buf, i, a=0, b=T):
            return buf[:, bass.ds(i, 1), a:b].rearrange("p o t -> p (o t)")

        def wchunk(w, col, kc, width=P):
            return w[kc * HC * P:(kc + 1) * HC * P, bass.ds(col, width)].rearrange("(k p) n -> p k n", p=P)

        def pair_col(i, g):
            base = {"q": C_Q, "k": C_K, "v": C_V, "g": C_AG, "u": C_U, "p": C_PG}[PAIR_TILES[i][0]]
            return (g + 1) * 256 + (base + P * (PAIR_TILES[i][1] in "B1") - 256)

        def head_col(i, s):
            kind, j = HEAD_TILES[i][0], int(HEAD_TILES[i][1])
            base, step = {"q": (G_Q, GK), "k": (G_K, GK), "v": (G_V, GV), "g": (G_G, GV)}[kind]
            return (s + 1) * step + (base + P * j - step)

        def y_buffer(i):
            return wraw[:, (i % 4) // 2, 4 * (i % 2):4 * (i % 2) + 4, :]

        def y_stores(i):
            return sum(16 * (1 + (q % 5 == TT)) for q in range(i % 4, i, 4))

        block = ctx.enter_context(nc.Block())

        @block.sync
        def _(sp):
            def load(n, kc, w, col, width=P):
                src = wchunk(w, col, kc, width)
                sp.wait_ge(s_lo, 2 * n + kc + 1)
                sp.dma_start(wraw[:, kc, :, 0:width], src).then_inc(s_raw[kc], 16)

            xp, xs, mt = A["x_prompt"][0], A["x_sample"].rearrange("b s d -> (b s) d"), A["meta_tokens"]
            sp.dma_start(xin[0][0:META, :], mt).then_inc(s_xin[0], 16)
            sp.dma_start(xin[0][META:P, :], xp[0:P - META, :]).then_inc(s_xin[0], 16)
            sp.dma_start(both[:], A["both"]).then_inc(s_const, 16)
            for tt in range(1, TT):
                sp.dma_start(xin[tt][:], xp[tt * P - META:(tt + 1) * P - META, :]).then_inc(s_xin[tt], 16)
            sp.dma_start(xin[4][0:TAIL, :], xp[SEQ - TAIL:SEQ, :]).then_inc(s_xin[4], 16)
            sp.dma_start(xin[4][TAIL:TB, :], xs).then_inc(s_xin[4], 16)
            for name, r, n in (("pre_norm_0", PRE0, 16), ("post_norm_0", POST0, 16), ("pre_norm_1", PRE1, 16),
                               ("post_norm_1", POST1, 16), ("pool_scale_0", PSC, 8), ("gla_ba_1", BA, 8),
                               ("gla_norm_1", GN, 4), ("subln_0", SUBG, 1)):
                sp.dma_start(rows[r:r + n, :], A[name].rearrange("(k p) -> k p", p=P)).then_inc(s_const, 16)
            load(0, 0, w_in0, pair_col(0, 0))
            load(0, 1, w_in0, pair_col(0, 0))
            sp.dma_start(pool_sample[:, 0:CTX - 1, :], A["state_pool"][:, 1:CTX, :]).then_inc(s_store, 16)
            sp.wait_ge(s_xd, 10)
            sp.wait_ge(s_xa, 10)
            sp.dma_start(h_dram[0].rearrange("k p t -> p k t"), mix[:]).then_inc(s_hst, 16)
            sp.wait_ge(s_rstd, 1)
            sp.wait_ge(s_cols, 1)
            sp.dma_start(first[:], A["first"]).then_inc(s_c0, 16)
            sp.dma_start(pages[:], A["page_table"].rearrange("b (o n) -> o (b n)", o=1)).then_inc(s_c0, 16)
            for i, name in enumerate(("lambda_q1_0", "lambda_k1_0", "lambda_q2_0", "lambda_k2_0")):
                sp.dma_start(lam4[:, i, :], A[name].rearrange("(o n) -> o n", o=1).to_broadcast([P, 64])).then_inc(s_c0, 16)

            def pair(g, skip=0):
                for c in range(skip, 24):
                    load(12 * g + c // 2, c % 2, w_in0, pair_col(c // 2, g))
                    if c == 20:
                        dst = sn_dram[bass.ds(g, 1)].rearrange("o b c -> (o b) c")
                        sp.wait_ge(s_snr, g + 1)
                        sp.dma_start(dst, small2[TAIL:TB, 0:4]).then_inc(s_sns, 16)
                    if c == 21:
                        src = sn_dram[bass.ds(g, 1)].rearrange("o b (c e) -> (o b c) e", e=1)
                        sp.wait_ge(s_sns, g * 16 + 16)
                        sp.dma_start(small2[0:4 * NB, 40:41], src).then_inc(s_sn, 16)

            pair(0, skip=2)
            with sp.Fori(1, PAIRS) as g:
                pair(g)

            def out_proj(n0, w, i):
                for par in range(2):
                    for kc in range(2):
                        load(n0 + par + 2 * i, kc, w, 256 * (i + 1) + (P * par - 256))

            with sp.Fori(0, KT // 2) as i:
                out_proj(N_OUT0, w_out0, i)
            for kc in range(2):
                load(N_LR, kc, w_in1, G_LR, RANK)
            sp.wait_ge(s_hn, KT)
            sp.dma_start(lower[:], A["lower"]).then_inc(s_c1, 16)

            def head(s):
                for c in range(24):
                    load(N_HEAD + c // 2 + 12 * s, c % 2, w_in1, head_col(c // 2, s))
                    if c == 0:
                        src = A["gla_wa2_1"][:, bass.ds((s + 1) * GK - GK, GK)]
                        sp.wait_ge(*freed_back("head", "G11", s))
                        sp.dma_start(wa2[:], src).then_inc(s_wa2, 16)

            with sp.Fori(0, GH) as s:
                head(s)
            with sp.Fori(0, KT // 2) as i:
                out_proj(N_OUT1, w_out1, i)
            yp, ys = y_prompt[0], y_sample.rearrange("b s d -> (b s) d")
            for i in range(20):
                kq, tt, buf = i // 5, i % 5, y_buffer(i)
                f = slice(kq * 512, (kq + 1) * 512)
                sp.wait_ge((s_fd2, s_fa2)[i % 2], i // 2 + 1)
                cut = lambda a, b: buf[a:b].rearrange("p k e -> p (k e)")
                if tt == 0:
                    sp.dma_start(yp[0:P - META, f], cut(META, P)).then_inc(s_yout[i % 4], 16)
                elif tt < TT:
                    sp.dma_start(yp[tt * P - META:(tt + 1) * P - META, f], cut(0, P)).then_inc(s_yout[i % 4], 16)
                else:
                    sp.dma_start(yp[SEQ - TAIL:SEQ, f], cut(0, TAIL)).then_inc(s_yout[i % 4], 16)
                    sp.dma_start(ys[:, f], cut(TAIL, TB)).then_inc(s_yout[i % 4], 16)
            for i in range(20, 24):
                sp.wait_ge(s_yout[i % 4], y_stores(i))
            sp.wait_ge(s_store, 16)
            sp.wait_ge(s_hst, 16 + 16 * KT)

        @block.gpsimd
        def _(pool):
            def lo(c, slot, width=P):
                kc = slot % 2
                pool.wait_ge(s_hi, c + 1)
                pool.tensor_tensor(wlo[:, slot, :, 0:width], wraw[:, kc, :, 0:width],
                                   whi[:, slot, :, 0:width].bitcast(F32), ALU.subtract).then_inc(s_lo, 1)

            def accumulate(r, j, k):
                pool.wait_ge(s_sq, r * KT + k + 1)
                if isinstance(k, int) and k == 0:
                    pool.tensor_copy(acc_of[r][:], sq_of[j]).then_inc(s_acc, 1)
                else:
                    pool.wait_ge(s_acc, r * KT + k)
                    pool.tensor_tensor(acc_of[r][:], acc_of[r][:], sq_of[j], ALU.add).then_inc(s_acc, 1)

            pool.sem_inc(s_lo, 2)
            for k in range(KT):
                accumulate(0, k % 2, k)
            lo(0, 0)
            lo(1, 1)

            def pair(g):
                for s in range(24):
                    lo(24 * g + s + 2, (s + 2) % 4)
                    if 14 <= s < 22:
                        b = s - 14
                        pool.wait_ge(s_kv[b % 2], 512 * g + 64 * (b // 2 + 1))
                        pool.wait_ge(s_qb[b % 2], 64 * g + 16 * (b // 2 + 1))
                        pool.tensor_tensor(kv[b % 2][:], kv[b % 2][:], qb[b % 2][:, None, :].to_broadcast([P, NPG, 2 * P]),
                                           ALU.mult).then_inc(s_prod, 1)

            with pool.Fori(0, PAIRS) as g:
                pair(g)

            def out_proj(r, n0, i, par, last=False, narrow=False):
                n, slot = n0 + 2 * i + par, (2 * (n0 + par) + 2) % 4
                if not last:
                    for kc in range(2):
                        lo(2 * n + 2 + kc, slot + kc, RANK if narrow else P)
                accumulate(r, par, 2 * i + par)

            for par in range(2):
                out_proj(1, N_OUT0, 0, par)
            with pool.Fori(1, KT // 2 - 1) as i:
                for par in range(2):
                    out_proj(1, N_OUT0, i, par)
            out_proj(1, N_OUT0, KT // 2 - 1, 0)
            out_proj(1, N_OUT0, KT // 2 - 1, 1, narrow=True)
            for k in range(KT):
                pool.wait_ge(s_yt, k + 1)
                pool.wait_ge(s_hld[k % 2], 16 * (k // 2 + 1))
                pool.tensor_tensor(mix[:, k, :], mix[:, k, :], hbuf[:, k % 2, :], ALU.add).then_inc(s_hn, 1)
            lo(2 * N_HEAD, (2 * N_HEAD) % 4)
            lo(2 * N_HEAD + 1, (2 * N_HEAD + 1) % 4)
            with pool.Fori(0, GH) as s:
                for c in range(24):
                    lo(24 * s + 2 * N_HEAD + c + 2, (2 * N_HEAD + c + 2) % 4)
            for par in range(2):
                out_proj(3, N_OUT1, 0, par)
            with pool.Fori(1, KT // 2 - 1) as i:
                for par in range(2):
                    out_proj(3, N_OUT1, i, par)
            out_proj(3, N_OUT1, KT // 2 - 1, 0)
            out_proj(3, N_OUT1, KT // 2 - 1, 1, last=True)
            for k in range(KT):
                pool.wait_ge(s_yt, KT + k + 1)
                pool.wait_ge(s_hld[k % 2], 16 * (KT // 2 + k // 2 + 1))
                pool.tensor_tensor(mix[:, k, :], mix[:, k, :], hbuf[:, k % 2, :], ALU.add).then_inc(s_hn, 1)

        @block.scalar
        def _(act):
            chain = Chain(s_a, act)

            def split(n, kc, par, width=P):
                act.wait_ge(s_raw[kc], n * 16 + 16)
                act.wait_ge(s_tile, n + 1)
                act.activation(whi[:, 2 * par + kc, :, 0:width], wraw[:, kc, :, 0:width], ACT.Copy).then_inc(s_hi, 1)

            def square(r, j, k, src, ready=None):
                act.wait_ge(s_acc, r * KT + k - 1) if not (isinstance(k, int) and r * KT + k < 2) else None
                act.activation(sq_of[j] if src.shape[1] == T else (tz, te)[j][:], src, ACT.Square).then_inc(s_sq, 1)

            def finish_rms(r):
                act.wait_ge(s_ss, r + 1)
                chain.link(act.activation(rstd[:], score2[:, :, 0:TH], ACT.Ln, scale=1.0 / D, bias=eps))
                act.activation(rstd[:], rstd[:], ACT.Exp, scale=-0.5).then_inc(s_rstd, 1)

            act.wait_ge(s_init, 1)
            act.sem_inc(s_tile, 2)
            act.sem_inc(s_fa, 2)
            for i in range(1, 20, 2):
                tt, kq = i // 4, i % 4
                w = P if tt < TT else TB
                act.wait_ge(s_xt, i + 1)
                act.copy(mix[:, 4 * kq:4 * kq + 4, tt * P:tt * P + w],
                         banks[i % 8].rearrange("p (k t) -> p k t", k=4)[:, :, 0:w]).then_inc(s_xa, 1)
            act.wait_ge(s_xd, 10)
            act.wait_ge(s_xa, 10)
            act.wait_ge(s_cols, 1)
            for k in range(KT):
                act.activation(xhi[:, k, :], mix[:, k, :], ACT.Copy, scale=cols[:, PRE0 + k:PRE0 + k + 1]).then_inc(s_xhi, 1)
                square(0, k % 2, k, mix[:, k, :])
            finish_rms(0)
            split(0, 0, 0)
            split(0, 1, 0)
            act.wait_ge(s_lam, 1)
            act.activation(lam[:, 6:8], lam[:, 4:6], ACT.Exp).then_inc(s_lam, 1)

            def gate_exp(phase, name, n, i):
                act.wait_ge(s_evac, n + 3)
                act.activation(te[:], tz[:], ACT.Exp, scale=-1.0).then_inc(gexp_ready.sem, 1)

            def pair(g):
                n0 = 12 * g

                def k_rows(hb):
                    h, x = 2 * g + hb, "AB"[hb]
                    act.wait_ge(*full.at("pair", "KT0" + x, g))
                    act.wait_ge(s_kout, 32 * g + 16 * hb)
                    act.copy(ktok[:], bank_of("pair", "KT0" + x)[:].rearrange("p (t e) -> p t e", t=TT)).then_inc(s_fa, 1)
                    act.wait_ge(*full.at("pair", "KT1" + x, g))
                    act.wait_ge(s_qk, 96 * g + 48 * hb)
                    act.wait_ge(s_snr, g)
                    act.copy(qk_tok[0:TB, :, hb, :], bank_of("pair", "KT1" + x)[0:TB, 0:2 * P].rearrange("p (a e) -> p a e", a=2)).then_inc(s_fa, 1)
                    act.wait_ge(*free_a.at("pair", "KT1" + x, g))
                    act.dma_start(k_prompt[0, 0:TT * P, bass.ds(h, 1), :].rearrange("(t p) o e -> p (t o) e", p=P), ktok[:]).then_inc(s_kout, 16)
                    act.dma_start(k_prompt[0, TT * P:TP, bass.ds(h, 1), :].rearrange("t o e -> t (o e)"), qk_tok[0:TAIL, 1, hb, :]).then_inc(s_qk, 16)
                    act.dma_start(k_sample[:, 0, bass.ds(h, 1), :].rearrange("b o e -> b (o e)"), qk_tok[TAIL:TB, 1, hb, :]).then_inc(s_qk, 16)
                    act.dma_start(q_dram[bass.ds(g, 1), :, hb * P:(hb + 1) * P].rearrange("o b e -> (o b) e"), qk_tok[TAIL:TB, 0, hb, :]).then_inc(s_qk, 16)

                def v_rows(hb):
                    h, x = 2 * g + hb, "AB"[hb]
                    act.wait_ge(s_vout[hb], 48 * g)
                    act.wait_ge(*full.at("pair", "VT0" + x, g))
                    act.copy(vtok[hb][:, 0:TT, :], bank_of("pair", "VT0" + x)[:].rearrange("p (t e) -> p t e", t=TT)).then_inc(s_fa, 1)
                    act.wait_ge(*full.at("pair", "VT1" + x, g))
                    act.copy(vtok[hb][0:TB, TT, :], bank_of("pair", "VT1" + x)[0:TB, 0:P]).then_inc(s_fa, 1)
                    act.wait_ge(*free_a.at("pair", "VT1" + x, g))
                    act.dma_start(v_prompt[0, 0:TT * P, bass.ds(h, 1), :].rearrange("(t p) o e -> p (t o) e", p=P), vtok[hb][:, 0:TT, :]).then_inc(s_vout[hb], 16)
                    act.dma_start(v_prompt[0, TT * P:TP, bass.ds(h, 1), :].rearrange("t o e -> t (o e)"), vtok[hb][0:TAIL, TT, :]).then_inc(s_vout[hb], 16)
                    act.dma_start(v_sample[:, 0, bass.ds(h, 1), :].rearrange("b o e -> b (o e)"), vtok[hb][TAIL:TB, TT, :]).then_inc(s_vout[hb], 16)

                def exps(t, hb):
                    act.wait_ge(*max_ready.at("pair", f"{t}{'AB'[hb]}", g))
                    if t < TT:
                        n = (t + 1) * P
                        for m in range(2):
                            last = act.activation(prob[:, m, 0:n], score2[:, m, 0:n], ACT.Exp, bias=small[:, 2 + m:3 + m],
                                                  scale=SCALE, accum_out=small[:, 4 + m:5 + m])
                    else:
                        last = act.activation(probw[0:2 * TAIL, 0:TP], score[0:2 * TAIL, 0:TP], ACT.Exp,
                                              bias=small[0:2 * TAIL, 2:3], scale=SCALE, accum_out=small[0:2 * TAIL, 4:5])
                    last.then_inc(exp_done.sem, 1)

                def o_square(hb):
                    act.wait_ge(*free_d.at("pair", f"O{TT}{'AB'[hb]}", g))
                    act.activation(pd[:, 0:TP], oT[:, 0:TP], ACT.Square).then_inc(osq_ready.sem, 1)

                def o_rstd(hb):
                    x, half = "AB"[hb], TP // 2
                    for a in range(2):
                        act.wait_ge(*full.at("pair", f"SS{a}{x}", g))
                        act.activation(pd[:, a * half:(a + 1) * half], bank_of("pair", f"SS{a}{x}")[:, 0:half], ACT.Ln,
                                       scale=1.0 / P, bias=eps).then_inc(s_fa, 1)
                    act.wait_ge(*free_a.at("pair", f"SS1{x}", g))
                    act.activation(pd[:, 0:TP], pd[:, 0:TP], ACT.Exp, scale=-0.5).then_inc(ro_ready.sem, 1)

                def fetch(cache, b, ready):
                    page = [act.value_load(pages[0:1, b * NPG + pg:b * NPG + pg + 1], min_val=0, max_val=PHYS - 1) for pg in range(NPG)]
                    src = [cache[bass.ds(p, 1), :, bass.ds(g * 256, 256)].rearrange("o p d -> p (o d)") for p in page]
                    act.wait_ge(*ready)
                    for pg in range(NPG):
                        act.dma_start(kv[b % 2][:, pg, :], src[pg]).then_inc(s_kv[b % 2], 16)

                def fetch_q(b):
                    act.dma_start(qb[b % 2][:], q_dram[bass.ds(g, 1), b, :].to_broadcast([P, 2 * P])).then_inc(s_qb[b % 2], 16)

                ck = A["cache_k"].rearrange("n p h e -> n p (h e)")
                cv = A["cache_v"].rearrange("n p h e -> n p (h e)")
                for s in range(24):
                    tile = (s + 2) // 2
                    split(n0 + tile, s % 2, tile % 2)
                    if s == 3:
                        act.wait_ge(*free_d.before("pair", BY_DVE["pair"][0], g))
                        act.dma_start(spool[:], A["state_pool"][:, :, bass.ds(g * 256, 256)].rearrange("b r c -> (b r) c")).then_inc(s_sg, 16)
                        act.dma_start(pw[:], A["pool_w_0"][bass.ds(g, 1)].rearrange("o (c p) d -> p (o c) d", p=P)).then_inc(s_pw, 16)
                    if s == 5: k_rows(0)
                    if s == 6: v_rows(0)
                    if s == 8:
                        gate_exp("pair", "gA", n0 + 3, g)
                        used = free_d.before("pair", BY_DVE["pair"][0], g)
                        fetch(ck, 0, used)
                        fetch(ck, 1, used)
                    if 8 <= s < 13: exps(s - 8, 0)
                    if s == 13: k_rows(1)
                    if s == 14:
                        act.wait_ge(s_qk, 96 * g + 96)
                        fetch_q(0)
                        fetch_q(1)
                        v_rows(1)
                        o_square(0)
                    if s == 15: o_rstd(0)
                    if 16 <= s < 22:
                        b = s - 14
                        act.wait_ge(s_prod, 8 * g + b - 1)
                        fetch_q(b)
                        fetch(ck, b, (s_kred, 8 * g + b - 1))
                    if s == 16: gate_exp("pair", "gB", n0 + 7, g)
                    if 16 <= s < 21: exps(s - 16, 1)
                    if s == 21:
                        act.wait_ge(*full.at("pair", "UT", g))
                        act.wait_ge(s_uout, 32 * g)
                        act.copy(utok[0:TB, :], bank_of("pair", "UT")[0:TB, 0:256]).then_inc(s_fa, 1)
                        act.wait_ge(*free_a.at("pair", "UT", g))
                        act.dma_start(pool_prompt[0, :, bass.ds(g * 256, 256)], utok[1:TAIL, :]).then_inc(s_uout, 16)
                        act.dma_start(pool_sample[:, CTX - 1, bass.ds(g * 256, 256)], utok[TAIL:TB, :]).then_inc(s_uout, 16)
                    if s == 22:
                        gate_exp("pair", "p0", n0 + 10, g)
                        fetch(cv, 0, (s_kred, 8 * g + 7))
                        o_square(1)
                        fetch(cv, 1, (s_kred, 8 * g + 8))
                        act.wait_ge(*max_ready.at("pair", "s", g))
                        act.activation(sprob[:], sprob[:], ACT.Exp, bias=small2[0:32, 34:35], scale=SCALE, accum_out=small2[0:32, 35:36])
                        act.activation(small2[0:32, 36:37], small2[0:32, 40:41], ACT.Exp, bias=small2[0:32, 34:35], scale=SCALE).then_inc(exp_done.sem, 1)
                    if s == 23: o_rstd(1)
                gate_exp("pair", "p1", n0 + 11, g)
                for b in range(2, NB):
                    fetch(cv, b, (s_pv, 7 * g + b - 1))
                act.wait_ge(*free_d.at("pair", "OS", g))
                act.activation(small2[:, 0:16], small[:, 32:48], ACT.Square).then_inc(osq_ready.sem, 1)
                act.wait_ge(*full.at("pair", "SN", g))
                act.activation(small2[:, 16:32], bank_of("pair", "SN")[:, 0:16], ACT.Ln, scale=1.0 / P, bias=eps).then_inc(s_fa, 1)
                act.wait_ge(*free_a.at("pair", "SN", g))
                act.activation(small2[:, 16:32], small2[:, 16:32], ACT.Exp, scale=-0.5).then_inc(ro_ready.sem, 1)

            with act.Fori(0, PAIRS) as g:
                pair(g)
            for s_out, n in ((s_kout, 32), (s_qk, 96), (s_vout[0], 48), (s_vout[1], 48), (s_uout, 32)):
                act.wait_ge(s_out, n * PAIRS)

            def mix_hi(phase):
                act.wait_ge(s_mix, phase + 1)
                act.wait_ge(s_tile, (N_OUT0 if phase == 0 else N_OUT1) + 2)
                for k in range(KT):
                    act.activation(xhi[:, k, :], mix[:, k, :], ACT.Copy).then_inc(s_xhi, 1)

            def out_proj(r, n0, i, par, last=False, narrow=False):
                n = n0 + 2 * i + par
                if not last:
                    for kc in range(2):
                        split(n + 1, kc, (n0 + par + 1) % 2, RANK if narrow else P)
                act.wait_ge(s_tile, n + 3)
                square(r, par, 2 * i + par, proj[(n0 + par) % 2][:, :, 0:TH])

            def out_stage(r, n0, narrow):
                for par in range(2):
                    out_proj(r, n0, 0, par)
                with act.Fori(1, KT // 2 - 1) as i:
                    for par in range(2):
                        out_proj(r, n0, i, par)
                out_proj(r, n0, KT // 2 - 1, 0)
                out_proj(r, n0, KT // 2 - 1, 1, last=not narrow, narrow=narrow)

            def fetch_h(layer, k):
                act.dma_start(hbuf[:, k % 2, :], h_dram[layer, k]).then_inc(s_hld[k % 2], 16)

            mix_hi(0)
            out_stage(1, N_OUT0, True)
            fetch_h(0, 0)
            fetch_h(0, 1)
            finish_rms(1)
            for k in range(KT):
                act.wait_ge(s_hn, k + 1)
                act.dma_start(h_dram[1, k], mix[:, k, :]).then_inc(s_hst, 16)
                if k + 2 < KT:
                    fetch_h(0, k + 2)
                act.activation(xhi[:, k, :], mix[:, k, :], ACT.Copy, scale=cols[:, PRE1 + k:PRE1 + k + 1]).then_inc(s_xhi, 1)
                square(2, k % 2, k, mix[:, k, :])
            finish_rms(2)
            act.wait_ge(s_hst, 16 + 16 * KT)
            split(N_HEAD, 0, 1)
            split(N_HEAD, 1, 1)

            def head(s):
                n0 = N_HEAD + 12 * s

                def decay_logs(j):
                    act.wait_ge(s_zg, 2 * s + j + 1)
                    if j:
                        act.wait_ge(s_g, 2 * s + 1)
                    chain.link(act.activation(tef, gb[:, j, :], ACT.Abs))
                    chain.link(act.activation(tef, tef, ACT.Exp, scale=-1.0))
                    act.activation(tef, tef, ACT.Ln, bias=one).then_inc(s_ga, 1)

                def decays(c):
                    c0, w = c * P, P if c < TT else TAIL
                    act.wait_ge(*dq_ready.at("head", str(c), s))
                    act.activation(eq[:, :, 0:w], eq[:, :, 0:w], ACT.Exp, scale=1.0 / TAU)
                    for j in range(2):
                        for i in range(4 if c < TT else 1):
                            m, ref = (SUB * (i + 1), 4 * c + i) if c < TT else (TAIL, 16)
                            act.activation(ek[:, j, KOFF[i]:KOFF[i] + m], gb[:, j, c0:c0 + m], ACT.Exp,
                                           scale=-1.0 / TAU, bias=refs[:, j, ref:ref + 1])
                        last = act.activation(el[:, j, 0:w], gb[:, j, c0:c0 + w], ACT.Exp, scale=-1.0 / TAU, bias=lastr[:, j, c:c + 1])
                    last.then_inc(dec_ready.sem, 1)

                def decay_start(c):
                    c0, w = c * P, P if c < TT else TAIL
                    act.activation(ed[:, :, 0:w], gb[:, :, c0:c0 + w], ACT.Exp, scale=1.0 / TAU).then_inc(ed_exp.sem, 1)

                def o_rows(c):
                    c0, w = c * P, P if c < TT else TAIL
                    act.wait_ge(*full.at("head", f"OC{c}", s))
                    act.copy(og[:, :, c0:c0 + w], bank_of("head", f"OC{c}")[:, 0:4 * w].rearrange("p (v t) -> p v t", v=4)).then_inc(s_fa, 1)

                def v_rows(j):
                    act.wait_ge(*full.at("head", f"VT0{j}", s))
                    act.copy(gv[:, 0:TT, j * P:(j + 1) * P], bank_of("head", f"VT0{j}")[:].rearrange("p (t e) -> p t e", t=TT)).then_inc(s_fa, 1)
                    act.wait_ge(*full.at("head", f"VT1{j}", s))
                    act.copy(gv[0:TB, TT, j * P:(j + 1) * P], bank_of("head", f"VT1{j}")[0:TB, 0:P]).then_inc(s_fa, 1)

                def fetch_s(b):
                    i = b % 2
                    act.wait_ge(s_so, 8 * s + b - 1) if b >= 2 else None
                    act.wait_ge(s_sout[i], 64 * s + 16 * (b // 2))
                    act.dma_start(sst[i][:], A["state_gla"][b, bass.ds(s, 1)].rearrange("o (j p) v -> p (o j) v", p=P)).then_inc(s_st[i], 16)
                    act.dma_start(vb[i][:], vs_dram[bass.ds(s, 1), b, :].to_broadcast([P, GV])).then_inc(s_vb[i], 16)

                def decay_s(b):
                    i = b % 2
                    act.wait_ge(s_st[i], 64 * s + 16 * (b // 2 + 1))
                    for j in range(2):
                        last = act.activation(sst[i][:, j, :], sst[i][:, j, :], ACT.Copy, scale=eg[:, j, b:b + 1])
                    last.then_inc(s_sdec, 1)

                def store_s(b):
                    i = b % 2
                    act.wait_ge(s_snew, 8 * s + b + 1)
                    act.dma_start(gla_sample[b, bass.ds(s, 1)].rearrange("o (j p) v -> p (o j) v", p=P), sst[i][:]).then_inc(s_sout[i], 16)

                for c in range(24):
                    tile = (c + 2) // 2
                    split(n0 + tile, c % 2, (tile + 1) % 2)
                    if c == 1: decay_logs(0)
                    if c == 2: decay_logs(1)
                    if c == 3:
                        act.wait_ge(s_refs, s + 1)
                        act.activation(elast[:], lastr[:], ACT.Exp)
                        act.activation(eg[:], gb[:, :, TP:T], ACT.Exp, scale=1.0 / TAU).then_inc(s_last, 1)
                    if c == 9:
                        decays(0)
                    if c in (10, 12, 14, 16): v_rows((c - 10) // 2)
                    if c == 16:
                        decays(1)
                        act.wait_ge(*free_a.at("head", "VT13", s))
                        act.dma_start(vs_dram[bass.ds(s, 1)].rearrange("o b v -> (o b) v"), gv[TAIL:TB, TT, :]).then_inc(s_vs, 16)
                    if c in (18, 20, 22): gate_exp("head", f"g{(c - 18) // 2}", n0 + 8 + (c - 18) // 2, s)
                    if 17 <= c < 22:
                        o_rows(c - 17)
                        if c < 21:
                            decay_start(c - 16)
                        if c < 20:
                            decays(c - 15)
                    if c == 17:
                        act.wait_ge(s_vs, 16 * s + 16)
                        fetch_s(0)
                        fetch_s(1)
                    if 19 <= c < 23:
                        for b in (2 * (c - 19), 2 * (c - 19) + 1):
                            decay_s(b)
                        for b in (2 * (c - 19), 2 * (c - 19) + 1):
                            store_s(b)
                            if b + 2 < NB:
                                fetch_s(b + 2)
                    if c == 22:
                        act.wait_ge(*free_d.at("head", "SU41", s))
                        act.dma_start(gla_prompt[0, bass.ds(s, 1)].rearrange("o (j p) v -> p (o j) v", p=P), state[:]).then_inc(s_gout, 16)
                gate_exp("head", "g3", n0 + 11, s)
                act.wait_ge(s_osg, s + 1)
                for v in range(4):
                    buf = (gq, gk)[v // 2]
                    last = act.activation(buf[:, v % 2, :], og[:, v, :], ACT.Square)
                last.then_inc(s_gsq, 1)
                r = ek[:].rearrange("p j t -> p (j t)")[:, 0:T]
                for a in range(2):
                    act.wait_ge(*full.at("head", f"SS{a}", s))
                    act.activation(r[:, a * TH:(a + 1) * TH], bank_of("head", f"SS{a}")[:, 0:TH], ACT.Ln, scale=1.0 / GV, bias=eps).then_inc(s_fa, 1)
                act.wait_ge(*free_a.at("head", "SS1", s))
                act.activation(r, r, ACT.Exp, scale=-0.5).then_inc(ro_ready.sem, 1)

            with act.Fori(0, GH) as s:
                chain.enter(s, HEAD_LINKS_ACT)
                head(s)
                chain.leave(GH)
            act.wait_ge(s_gout, 16 * GH)
            act.wait_ge(s_sout[0], 64 * GH)
            act.wait_ge(s_sout[1], 64 * GH)
            mix_hi(1)
            out_stage(3, N_OUT1, False)
            fetch_h(1, 0)
            fetch_h(1, 1)
            finish_rms(3)
            for k in range(KT):
                act.wait_ge(s_hn, KT + k + 1)
                if k + 2 < KT:
                    fetch_h(1, k + 2)
            for i in range(1, 20, 2):
                w = P if i % 5 < TT else TB
                act.wait_ge(s_fT, i + 1)
                if i >= 4:
                    act.wait_ge(s_yout[i % 4], y_stores(i))
                act.copy(y_buffer(i)[0:w], banks[i % 8].rearrange("p (k e) -> p k e", k=4)[0:w]).then_inc(s_fa2, 1)

        @block.tensor
        def _(pe):
            def matmul(out, lhsT, rhs, start=True, stop=True):
                return pe.matmul(out, lhsT, rhs, start=start, stop=stop, skip_group_check=True)

            def transpose(out, x):
                return pe.transpose(out, x, ident[0:x.shape[0], 0:x.shape[0]])

            def chunk(n, par, kc, x_level):
                if kc == 0:
                    pe.wait_ge(s_evac, n + 1)
                pe.wait_ge(s_lo, 2 * n + kc + 3)
                pe.wait_ge(s_x, x_level + HC * (kc + 1))
                slot = 2 * par + kc
                for a in range(2):
                    for k in range(HC):
                        x = slice(a * TH, (a + 1) * TH)
                        kt = kc * HC + k
                        out = proj[par][:, a, 0:TH]
                        matmul(out, wlo[:, slot, k, :], xhi[:, kt, x], start=kt == 0, stop=False)
                        matmul(out, whi[:, slot, k, :], xlo[:, kt, x], start=False, stop=False)
                        last = matmul(out, whi[:, slot, k, :], xhi[:, kt, x], start=False, stop=kt == KT - 1)
                if kc == 1:
                    last.then_inc(s_tile, 1)

            def sum_squares(r):
                pe.wait_ge(s_acc, KT * (r + 1))
                for a in range(2):
                    last = matmul(score2[:, a, 0:TH], ones, acc_of[r][:, a * TH:(a + 1) * TH])
                last.then_inc(s_ss, 1)

            pe.wait_ge(s_const, 16 * 9)
            for i in range(20):
                tt, kq = i // 4, i % 4
                w = P if tt < TT else TB
                if kq == 0:
                    pe.wait_ge(s_xin[tt], 32 if tt in (0, 4) else 16)
                if i >= 8:
                    pe.wait_ge((s_xd, s_xa)[i % 2], (i - 8) // 2 + 1)
                for k in range(4):
                    last = transpose(banks[i % 8][:, k * P:k * P + w], xin[tt][0:w, (4 * kq + k) * P:(4 * kq + k + 1) * P])
                last.then_inc(s_xt, 1)
            pe.wait_ge(s_xd, 9)
            transpose(banks[0][:, 0:85], rows[:, :]).then_inc(s_v, 1)
            sum_squares(0)

            def pair(g):
                n0 = 12 * g

                def job(name):
                    k = PAIR_JOBS.index(name)
                    prev = PAIR_JOBS[k - 2]
                    if k < 2:
                        pe.wait_ge(*freed_back("pair", prev, g))
                    else:
                        pe.wait_ge(*freed("pair", prev, g))
                    return scratch[k % 2]

                def done(last):
                    last.then_inc(s_full, 1)

                def run(op):
                    kind, x = op[:2], op[-1]
                    hb = "AB".find(x)
                    if op[0] == "S" and op[1] in "01234":
                        t = int(op[1])
                        pe.wait_ge(*exp_done.before("pair", f"{t}{x}", g))
                        pe.wait_ge(*rope_ready.at("pair", "k" + x, g))
                        if t < TT:
                            n = (t + 1) * P
                            for m in range(2):
                                d = slice(64 * m, 64 * m + 64)
                                matmul(score2[:, m, 0:n], qT[hb][d, t * P:(t + 1) * P], kT[hb][d, 0:n], stop=False)
                                last = matmul(score2[:, m, n - P:n], ident, causal, start=False)
                        else:
                            pe.wait_ge(s_qblk, 2 * g + hb + 1)
                            r = 2 * TAIL
                            matmul(score[0:r, 0:TT * P], qblk[:], kT[hb][:, 0:TT * P])
                            matmul(score[0:r, TT * P:TP], qblk[:], kT[hb][:, TT * P:TP], stop=False)
                            last = matmul(score[0:r, TT * P:TP], ident[0:r, 0:r], tmask[0:r, :], start=False)
                        last.then_inc(score_ready.sem, 1)
                        return
                    out = job(op)
                    if kind in ("RQ", "RK"):
                        a = int(op[2])
                        pe.wait_ge(s_evac, n0 + 4 * hb + (kind == "RK") + 3)
                        done(matmul(out[:, 0:TH], rot, tz[:, a, :]))
                    elif kind == "KT":
                        if op[2] == "0":
                            pe.wait_ge(*rope_ready.at("pair", "k" + x, g))
                            for t in range(TT):
                                last = transpose(out[:, t * P:(t + 1) * P], kT[hb][:, t * P:(t + 1) * P])
                        else:
                            transpose(out[0:TB, 0:P], qT[hb][:, TT * P:T])
                            last = transpose(out[0:TB, P:2 * P], kT[hb][:, TT * P:T])
                        done(last)
                    elif kind == "VT":
                        pe.wait_ge(s_evac, n0 + 4 * hb + 2 + 3)
                        if op[2] == "0":
                            for t in range(TT):
                                last = transpose(out[:, t * P:(t + 1) * P], tzf[:, t * P:(t + 1) * P])
                        else:
                            last = transpose(out[0:TB, 0:P], tzf[:, TT * P:T])
                        done(last)
                    elif kind == "PT":
                        t = int(op[2])
                        pe.wait_ge(*pd_ready.at("pair", f"{t}{x}", g))
                        if t < TT:
                            for k in range(t + 1):
                                last = transpose(out[:, k * P:(k + 1) * P], pd[:, k * P:(k + 1) * P])
                        else:
                            for k in range(TT + 1):
                                m = P if k < TT else TAIL
                                last = matmul(out[0:m, k * TAIL:(k + 1) * TAIL], probw[0:2 * TAIL, k * P:k * P + m], tsel[0:2 * TAIL, :])
                        done(last)
                    elif op[0] == "O" and op[1] != "S":
                        t = int(op[1])
                        w = P if t < TT else TAIL
                        pe.wait_ge(*free_d.at("pair", f"PT{t}{x}", g))
                        pe.wait_ge(*free_a.at("pair", f"VT1{x}", g))
                        for k in range(t + 1):
                            m = P if k < TT else TAIL
                            last = matmul(out[:, 0:w], vtok[hb][0:m, k, :], pdT[(5 * hb + t) % 2][0:m, k * w:(k + 1) * w],
                                          start=k == 0, stop=k == t)
                        done(last)
                    elif kind == "SS":
                        a, half = int(op[2]), TP // 2
                        pe.wait_ge(*osq_ready.at("pair", x, g))
                        done(matmul(out[:, 0:half], ones, pd[:, a * half:(a + 1) * half]))
                    elif op == "SG":
                        pe.wait_ge(s_sg, g * 16 + 16)
                        r = NB * CTX
                        for j in range(2):
                            last = transpose(out[:, j * r:(j + 1) * r], spool[:, j * P:(j + 1) * P])
                        done(last)
                    elif op == "UT":
                        pe.wait_ge(s_evac, n0 + 9 + 3)
                        for j in range(2):
                            last = transpose(out[0:TB, j * P:(j + 1) * P], ub[:, j, META + TT * P:META + T])
                        done(last)
                    elif op == "ST":
                        pe.wait_ge(s_kred, 8 * g + 8)
                        for k in range(NPG):
                            last = transpose(out[0:4 * NB, k * P:(k + 1) * P], sall[:, k, :])
                        done(last)
                    elif op == "SD":
                        pe.wait_ge(*pd_ready.at("pair", "s", g))
                        for k in range(NPG):
                            matmul(out[:, 16 * k:16 * k + 16], sprob[:, k * P:(k + 1) * P], ssel[0:4 * NB, :])
                        done(matmul(out[:, 64:80], ones[0:4 * NB, :], enew[:]))
                    elif kind == "PO":
                        j, a = int(op[2]), int(op[3])
                        pe.wait_ge(s_d, g + 1)
                        pe.wait_ge(s_pw, g * 16 + 16)
                        for k in range(2):
                            last = matmul(out[:, 0:TH], pw[:, k, j * P:(j + 1) * P], ub[:, k, META + a * TH:META + (a + 1) * TH],
                                          start=k == 0, stop=k == 1)
                        done(last)
                    elif op == "OS":
                        pe.wait_ge(*free_d.at("pair", "SD", g))
                        for b in range(NB):
                            pe.wait_ge(s_kv[b % 2], 512 * g + 256 + 64 * (b // 2 + 1))
                            for j in range(2):
                                for k in range(NPG):
                                    c = 2 * b + j
                                    last = matmul(out[:, c:c + 1], kv[b % 2][:, k, j * P:(j + 1) * P], pds[:, 16 * k + c:16 * k + c + 1],
                                                  start=k == 0, stop=k == NPG - 1)
                            if b < NB - 1:
                                last.then_inc(s_pv, 1)
                        done(last)
                    elif op == "SN":
                        pe.wait_ge(*osq_ready.at("pair", "s", g))
                        done(matmul(out[:, 0:16], ones, small2[:, 0:16]))
                    else:
                        raise ValueError(op)

                for s in range(24):
                    chunk(n0 + s // 2, (s // 2) % 2, s % 2, X_IN0)
                    for op in PAIR_PLAN.get(s, "").split():
                        run(op)

            pe.wait_ge(s_c0, 96)
            with pe.Fori(0, PAIRS) as g:
                pair(g)

            def out_proj(n0, x_level):
                with pe.Fori(0, KT // 2) as i:
                    for par in range(2):
                        for kc in range(2):
                            chunk(2 * i + (n0 + par), (n0 + par) % 2, kc, x_level)

            out_proj(N_OUT0, X_OUT0)
            sum_squares(1)
            for kc in range(2):
                chunk(N_LR, 0, kc, X_IN1)
            sum_squares(2)

            def head(s):
                n0 = N_HEAD + 12 * s

                def job(name):
                    k = HEAD_JOBS.index(name)
                    prev = HEAD_JOBS[k - 2]
                    if k < 2:
                        pe.wait_ge(*freed_back("head", prev, s))
                    else:
                        pe.wait_ge(*freed("head", prev, s))
                    return scratch[k % 2]

                def done(last):
                    last.then_inc(s_full, 1)

                def run(op):
                    kind = op[:2]
                    if op[0] == "B":
                        b = int(op[1])
                        pe.wait_ge(s_snew, 8 * s + b + 1)
                        for v in range(4):
                            for j in range(2):
                                last = matmul(score[:, v * NB + b:v * NB + b + 1], sst[b % 2][:, j, v * P:(v + 1) * P],
                                              gq[:, j, TP + b:TP + b + 1], start=j == 0, stop=j == 1)
                        last.then_inc(s_so, 1)
                        return
                    out = job(op)
                    if op[0] == "G":
                        j, a = int(op[1]), int(op[2])
                        pe.wait_ge(s_lr, 1)
                        pe.wait_ge(s_wa2, s * 16 + 16)
                        done(matmul(out[:, 0:TH], wa2[:, j * P:(j + 1) * P], lrT[:, a * TH:(a + 1) * TH]))
                    elif kind == "VT":
                        j = int(op[3])
                        pe.wait_ge(s_evac, n0 + 4 + j + 3)
                        if op[2] == "0":
                            for t in range(TT):
                                last = transpose(out[:, t * P:(t + 1) * P], tzf[:, t * P:(t + 1) * P])
                        else:
                            last = transpose(out[0:TB, 0:P], tzf[:, TT * P:T])
                        done(last)
                    elif kind == "SK":
                        c = int(op[2])
                        pe.wait_ge(*fac_ready.at("head", str(c), s))
                        for i in range(4 if c < TT else 1):
                            m, w = (SUB * (i + 1), SUB) if c < TT else (TAIL, TAIL)
                            for j in range(2):
                                matmul(out[0:m, SUB * i:SUB * i + w], ek[:, j, KOFF[i]:KOFF[i] + m], eq[:, j, SUB * i:SUB * i + w],
                                       start=j == 0, stop=j == 1)
                        w = P if c < TT else TAIL
                        for j in range(2):
                            last = transpose(out[0:w, P * (j + 1):P * (j + 2)], el[:, j, 0:w])
                        done(last)
                    elif kind == "OC":
                        c = int(op[2])
                        w = P if c < TT else TAIL
                        pe.wait_ge(*free_d.at("head", f"SK{c}", s))
                        pe.wait_ge(*free_a.at("head", "VT13", s))
                        if c:
                            pe.wait_ge(*ed_ready.at("head", str(c), s))
                            pe.wait_ge(*free_d.at("head", f"SU{c - 1}1", s))
                        for v in range(4):
                            o, vc = out[:, v * w:(v + 1) * w], slice(v * P, (v + 1) * P)
                            if c:
                                for j in range(2):
                                    matmul(o, state[:, j, vc], ed[:, j, 0:w], start=j == 0, stop=False)
                            last = matmul(o, gv[0:w, c, vc], st[c % 2][0:w, 0:w], start=c == 0, stop=True)
                        done(last)
                    elif kind == "SU":
                        c, j = int(op[2]), int(op[3])
                        w = P if c < TT else TAIL
                        done(matmul(out[:, 0:GV], kd[c % 2][0:w, j * P:(j + 1) * P], gv[0:w, c, :]))
                    elif kind == "SS":
                        a = int(op[2])
                        pe.wait_ge(s_gsq, s + 1)
                        for v in range(4):
                            last = matmul(out[:, 0:TH], ones, (gq, gk)[v // 2][:, v % 2, a * TH:(a + 1) * TH], start=v == 0, stop=v == 3)
                        done(last)
                    else:
                        raise ValueError(op)

                for c in range(24):
                    chunk(n0 + c // 2, (1 + c // 2) % 2, c % 2, X_IN1)
                    for op in HEAD_PLAN.get(c, "").split():
                        run(op)

            with pe.Fori(0, GH) as s:
                head(s)
            out_proj(N_OUT1, X_OUT1)
            sum_squares(3)
            for i in range(20):
                kq, tt = i // 5, i % 5
                w = P if tt < TT else TB
                if tt == 0:
                    pe.wait_ge(s_hn, KT + 4 * kq + 4)
                if i == 0:
                    pe.wait_ge(s_rstd, 4)
                if i >= 8:
                    pe.wait_ge((s_fd2, s_fa2)[i % 2], (i - 8) // 2 + 1)
                for k in range(4):
                    last = transpose(banks[i % 8][0:w, k * P:(k + 1) * P], mix[:, 4 * kq + k, tt * P:tt * P + w])
                last.then_inc(s_fT, 1)

        @block.vector
        def _(dve):
            chain = Chain(s_vc, dve)
            link = chain.link

            def evac(n, par, dst, scale=None):
                dve.wait_ge(s_tile, n + 3)
                src = proj[par][:, :, 0:TH]
                if scale is None:
                    dve.tensor_tensor(dst, src, rstd[:], ALU.mult).then_inc(s_evac, 1)
                else:
                    dve.scalar_tensor_tensor(out=dst, in0=src, scalar=scale, in1=rstd[:], op0=ALU.mult, op1=ALU.mult).then_inc(s_evac, 1)
                dve.wait_ge(s_evac, n + 3)

            def lows(level, scale_col=None):
                for k in range(KT):
                    dve.wait_ge(s_xhi, level + k + 1)
                    if scale_col is None:
                        dve.tensor_tensor(xlo[:, k, :], mix[:, k, :], xhi[:, k, :].bitcast(F32), ALU.subtract).then_inc(s_x, 1)
                    else:
                        dve.scalar_tensor_tensor(out=xlo[:, k, :], in0=mix[:, k, :], scalar=cols[:, scale_col + k:scale_col + k + 1],
                                                 in1=xhi[:, k, :].bitcast(F32), op0=ALU.mult, op1=ALU.subtract).then_inc(s_x, 1)

            dve.sem_inc(s_evac, 2)
            dve.sem_inc(s_fd, 2)
            dve.memset(stat[:, 0:1], EPS)
            link(dve.memset(stat[:, 1:2], 1.0))
            dve.sem_inc(s_init, 1)
            for i in range(0, 20, 2):
                tt, kq = i // 4, i % 4
                w = P if tt < TT else TB
                dve.wait_ge(s_xt, i + 1)
                dve.tensor_copy(mix[:, 4 * kq:4 * kq + 4, tt * P:tt * P + w],
                                banks[i % 8].rearrange("p (k t) -> p k t", k=4)[:, :, 0:w]).then_inc(s_xd, 1)
            dve.wait_ge(s_v, 1)
            link(dve.tensor_copy(cols[:, 0:85], banks[0][:, 0:85]))
            dve.tensor_scalar(cols[:, SUBG8:SUBG8 + 1], cols[:, SUBG:SUBG + 1], 1.0 - LAM_INIT, None, ALU.mult).then_inc(s_cols, 1)
            dve.wait_ge(s_cols, 1)
            lows(X_IN0, PRE0)
            dve.wait_ge(s_c0, 96)
            link(dve.tensor_tensor(lam4[:, 0:3:2, :], lam4[:, 0:3:2, :], lam4[:, 1:4:2, :], ALU.mult))
            dve.tensor_reduce(lam[:, 4:6], lam4[:, 0:3:2, :], AX.X, ALU.add).then_inc(s_lam, 1)
            dve.memset(qblk[:], 0.0)
            dve.memset(ub[:, :, 0:META], 0.0)
            dve.wait_ge(s_lam, 2)
            link(dve.tensor_tensor(lam[:, 0:1], lam[:, 6:7], lam[:, 7:8], ALU.subtract))
            link(dve.tensor_scalar(lam[:, 1:2], lam[:, 0:1], LAM_INIT, -1.0, ALU.add, ALU.mult))
            dve.scalar_tensor_tensor(out=lam[:, 2:3], in0=tmap[:, 1:2], scalar=lam[:, 1:2], in1=tmap[:, 0:1], op0=ALU.mult, op1=ALU.add)
            dve.scalar_tensor_tensor(out=lam[:, 3:4], in0=smap[:, 1:2], scalar=lam[:, 1:2], in1=smap[:, 0:1], op0=ALU.mult, op1=ALU.add)
            link(dve.memset(lam[:, 0:1], 1.0))
            dve.wait_ge(s_rstd, 1)
            dve.wait_ge(s_hst, 16)

            def pair(g):
                n0 = 12 * g

                def gate(name, dst):
                    dve.wait_ge(*gexp_ready.at("pair", name, g))
                    link(dve.tensor_scalar(te[:], te[:], 1.0, None, ALU.add))
                    link(dve.reciprocal(te[:], te[:]))
                    link(dve.tensor_tensor(dst, tzf, tef, ALU.mult))

                def rope_start(n, dst):
                    evac(n, n % 2, tz[:])
                    link(dve.tensor_tensor(dst[:], tzf, cos, ALU.mult))

                def rope_end(op, x, dst):
                    for a in range(2):
                        c = slice(a * TH, (a + 1) * TH)
                        dve.wait_ge(*full.at("pair", f"{op}{a}{x}", g))
                        dve.tensor_tensor(te[:, a, :], bank_of("pair", f"{op}{a}{x}")[:, 0:TH], sin[:, c], ALU.mult).then_inc(s_fd, 1)
                        dve.wait_ge(*free_d.at("pair", f"{op}{a}{x}", g))
                        last = dve.tensor_tensor(dst[:, c], dst[:, c], te[:, a, :], ALU.add)
                    last.then_inc(rope_ready.sem, 1)

                def tail_queries(hb):
                    dve.wait_ge(*rope_ready.at("pair", "q" + "AB"[hb], g))
                    dve.tensor_copy(qblk[0:64, 0:TAIL], qT[hb][0:64, TT * P:TP])
                    dve.tensor_copy(qblk[64:P, TAIL:2 * TAIL], qT[hb][64:P, TT * P:TP]).then_inc(s_qblk, 1)

                def maxima(t, hb):
                    dve.wait_ge(*score_ready.at("pair", f"{t}{'AB'[hb]}", g))
                    if t < TT:
                        link(dve.tensor_reduce(small[:, 0:2], score2[:, :, 0:(t + 1) * P], AX.X, ALU.max))
                        dve.tensor_scalar(small[:, 2:4], small[:, 0:2], -SCALE, None, ALU.mult).then_inc(max_ready.sem, 1)
                    else:
                        r = 2 * TAIL
                        link(dve.tensor_reduce(small[0:r, 0:1], score[0:r, 0:TP], AX.X, ALU.max))
                        dve.tensor_scalar(small[0:r, 2:3], small[0:r, 0:1], -SCALE, None, ALU.mult).then_inc(max_ready.sem, 1)

                def combine(t, hb):
                    dve.wait_ge(*exp_done.at("pair", f"{t}{'AB'[hb]}", g))
                    if t < TT:
                        n = (t + 1) * P
                        link(dve.reciprocal(small[:, 6:8], small[:, 4:6]))
                        link(dve.tensor_tensor(small[:, 8:10], small[:, 6:8], lam[:, 0:2], ALU.mult))
                        link(dve.tensor_scalar(prob[:, 0, 0:n], prob[:, 0, 0:n], small[:, 8:9], None, ALU.mult))
                        dve.scalar_tensor_tensor(out=pd[:, 0:n], in0=prob[:, 1, 0:n], scalar=small[:, 9:10], in1=prob[:, 0, 0:n],
                                                 op0=ALU.mult, op1=ALU.add).then_inc(pd_ready.sem, 1)
                    else:
                        r = 2 * TAIL
                        link(dve.reciprocal(small[0:r, 6:7], small[0:r, 4:5]))
                        link(dve.tensor_tensor(small[0:r, 8:9], small[0:r, 6:7], lam[0:r, 2:3], ALU.mult))
                        dve.tensor_scalar(probw[0:r, 0:TP], probw[0:r, 0:TP], small[0:r, 8:9], None, ALU.mult).then_inc(pd_ready.sem, 1)

                def probs_out(t, hb):
                    x, buf = "AB"[hb], pdT[(5 * hb + t) % 2]
                    dve.wait_ge(*full.at("pair", f"PT{t}{x}", g))
                    src = bank_of("pair", f"PT{t}{x}")
                    if t < TT:
                        dve.tensor_copy(buf[:, 0:(t + 1) * P], src[:, 0:(t + 1) * P]).then_inc(s_fd, 1)
                    else:
                        dve.tensor_copy(buf[:, 0:TT * TAIL], src[:, 0:TT * TAIL])
                        dve.tensor_copy(buf[0:TAIL, TT * TAIL:(TT + 1) * TAIL], src[0:TAIL, TT * TAIL:(TT + 1) * TAIL]).then_inc(s_fd, 1)

                def output(t, hb):
                    x, w = "AB"[hb], P if t < TT else TAIL
                    dve.wait_ge(*full.at("pair", f"O{t}{x}", g))
                    dve.tensor_copy(oT[:, t * P:t * P + w], bank_of("pair", f"O{t}{x}")[:, 0:w]).then_inc(s_fd, 1)

                def mix_head(hb):
                    dve.wait_ge(*ro_ready.at("pair", "AB"[hb], g))
                    dve.wait_ge(*free_d.at("pair", f"O{TT}{'AB'[hb]}", g))
                    link(dve.scalar_tensor_tensor(out=oT[:, 0:TP], in0=oT[:, 0:TP], scalar=cols[:, SUBG8:SUBG8 + 1], in1=pd[:, 0:TP],
                                                  op0=ALU.mult, op1=ALU.mult))
                    m = mix[:, HC + 2 * g + hb, 0:TP]
                    link(dve.tensor_tensor(m, m, oT[:, 0:TP], ALU.mult))

                def key_sums(b):
                    dve.wait_ge(s_prod, 8 * g + b + 1)
                    dve.tensor_reduce(sall[:, :, 4 * b:4 * b + 4], kv[b % 2][:].rearrange("p k (m d) -> p k m d", d=64),
                                      AX.X, ALU.add).then_inc(s_kred, 1)

                def own_key_scores():
                    dve.wait_ge(*free_a.at("pair", "KT1B", g))
                    link(dve.tensor_tensor(tef[0:TB, 0:2 * P], qk_tok[0:TB, 0].rearrange("p h e -> p (h e)"),
                                           qk_tok[0:TB, 1].rearrange("p h e -> p (h e)"), ALU.mult))
                    dve.tensor_reduce(small2[0:TB, 0:4], tef[0:TB, 0:2 * P].rearrange("p (m d) -> p m d", d=64), AX.X, ALU.add).then_inc(s_snr, 1)

                def pooled_rows():
                    w = 2 << g
                    dve.wait_ge(*full.at("pair", "SG", g))
                    src = bank_of("pair", "SG")[:, 0:2 * NB * CTX].rearrange("p (b r) -> p b r", r=CTX)
                    dve.tensor_reduce(small[:, 16:32], src[:, :, CTX - (w - 1):CTX], AX.X, ALU.add).then_inc(s_fd, 1)

                def window_means():
                    w = 2 << g
                    dve.wait_ge(*full.at("pair", "UT", g))
                    for j in range(2):
                        u = ub[:, j, 0:META + TP]
                        src, x = u, 1
                        for step in range(g + 1):
                            dst = win[step % 2]
                            link(dve.tensor_tensor(dst[:, 16:], src[:, 16:], src[:, 16 - x:META + TP - x], ALU.add))
                            if step < g:
                                link(dve.memset(dst[:, 0:16], 0.0))
                            src, x = dst, 2 * x
                        link(dve.tensor_tensor(small2[:, 16:32], src[:, 16:32], counts[:, g, :], ALU.mult))
                        link(dve.tensor_tensor(small2[:, 16:32], small2[:, 16:32], u[:, 16:32], ALU.subtract))
                        link(dve.scalar_tensor_tensor(out=u[:, 32:], in0=src[:, 32:], scalar=1.0 / w, in1=u[:, 32:], op0=ALU.mult, op1=ALU.subtract))
                        dve.tensor_copy(u[:, 16:32], small2[:, 16:32])
                        us, t8 = ub[:, j, META + TP:META + T], small[:, 16 + 8 * j:24 + 8 * j]
                        link(dve.tensor_tensor(t8, t8, us, ALU.add))
                        last = dve.scalar_tensor_tensor(out=us, in0=t8, scalar=1.0 / w, in1=us, op0=ALU.mult, op1=ALU.subtract)
                        if j == 0:
                            link(last)
                    last.then_inc(s_d, 1)

                def sample_softmax():
                    dve.wait_ge(*full.at("pair", "ST", g))
                    dve.tensor_copy(sprob[:], bank_of("pair", "ST")[0:4 * NB, :]).then_inc(s_fd, 1)
                    dve.wait_ge(*free_d.at("pair", "ST", g))
                    link(dve.tensor_reduce(small2[0:32, 32:33], sprob[:], AX.X, ALU.max))
                    dve.wait_ge(s_sn, g * 16 + 16)
                    link(dve.tensor_tensor(small2[0:32, 33:34], small2[0:32, 32:33], small2[0:32, 40:41], ALU.max))
                    dve.tensor_scalar(small2[0:32, 34:35], small2[0:32, 33:34], -SCALE, None, ALU.mult).then_inc(max_ready.sem, 1)
                    dve.wait_ge(*exp_done.at("pair", "s", g))
                    link(dve.tensor_tensor(small2[0:32, 37:38], small2[0:32, 35:36], small2[0:32, 36:37], ALU.add))
                    link(dve.reciprocal(small2[0:32, 37:38], small2[0:32, 37:38]))
                    link(dve.tensor_tensor(small2[0:32, 38:39], small2[0:32, 37:38], lam[0:32, 3:4], ALU.mult))
                    link(dve.tensor_tensor(small2[0:32, 39:40], small2[0:32, 38:39], small2[0:32, 36:37], ALU.mult))
                    dve.tensor_scalar(sprob[:], sprob[:], small2[0:32, 38:39], None, ALU.mult)
                    dve.tensor_scalar(enew[:], ssel[0:32, :], small2[0:32, 39:40], None, ALU.mult).then_inc(pd_ready.sem, 1)

                def sample_probs():
                    dve.wait_ge(*full.at("pair", "SD", g))
                    dve.tensor_copy(pds[:], bank_of("pair", "SD")[:, 0:80]).then_inc(s_fd, 1)
                    dve.wait_ge(*free_d.at("pair", "SD", g))

                def pooled_out(j):
                    k = 2 * g + j
                    for a in range(2):
                        dve.wait_ge(*full.at("pair", f"PO{j}{a}", g))
                        m = mix[:, k, a * TH:(a + 1) * TH]
                        dve.scalar_tensor_tensor(out=m, in0=bank_of("pair", f"PO{j}{a}")[:, 0:TH], scalar=cols[:, PSC + k:PSC + k + 1],
                                                 in1=m, op0=ALU.mult, op1=ALU.mult).then_inc(s_fd, 1)

                def sample_mix():
                    os = small[:, 32:48]
                    v = vs[:].rearrange("p h b -> p b h")
                    link(dve.tensor_tensor(os.rearrange("p (b h) -> p b h", h=2), pds[:, 64:80].rearrange("p (b h) -> p b h", h=2), v, ALU.mult))
                    dve.wait_ge(*full.at("pair", "OS", g))
                    dve.tensor_tensor(os, os, bank_of("pair", "OS")[:, 0:16], ALU.add).then_inc(s_fd, 1)
                    dve.wait_ge(*ro_ready.at("pair", "s", g))
                    link(dve.scalar_tensor_tensor(out=os, in0=os, scalar=cols[:, SUBG8:SUBG8 + 1], in1=small2[:, 16:32], op0=ALU.mult, op1=ALU.mult))
                    m = mix[:, HC + 2 * g:HC + 2 * g + 2, TP:T]
                    link(dve.tensor_tensor(m, m, os.rearrange("p (b h) -> p h b", h=2), ALU.mult))

                for s in range(24):
                    if s == 1: rope_start(n0, qT[0])
                    if s == 2: rope_end("RQ", "A", qT[0])
                    if s == 3: rope_start(n0 + 1, kT[0])
                    if s == 4: rope_end("RK", "A", kT[0])
                    if s == 5:
                        evac(n0 + 2, 0, tz[:])
                        link(dve.tensor_copy(vs[:, 0, :], tzf[:, TP:T]))
                    if s == 7:
                        dve.wait_ge(*full.at("pair", "VT1A", g))
                        evac(n0 + 3, 1, tz[:])
                    if s == 8: gate("gA", mix[:, HC + 2 * g, :])
                    if s == 9: rope_start(n0 + 4, qT[1])
                    if s == 11: rope_start(n0 + 5, kT[1])
                    if s == 13:
                        evac(n0 + 6, 0, tz[:])
                        link(dve.tensor_copy(vs[:, 1, :], tzf[:, TP:T]))
                    if s == 15:
                        own_key_scores()
                        dve.wait_ge(*full.at("pair", "VT1B", g))
                        evac(n0 + 7, 1, tz[:])
                        mix_head(0)
                    if s == 16:
                        gate("gB", mix[:, HC + 2 * g + 1, :])
                    if s in (17, 19):
                        evac(n0 + 8 + (s - 17) // 2, (s - 17) // 2, ub[:, (s - 17) // 2, META:].rearrange("p (a t) -> p a t", a=2))
                    if s in (21, 23):
                        evac(n0 + 10 + (s - 21) // 2, (s - 21) // 2, tz[:])
                    for hb, s0 in ((0, 8), (1, 16)):
                        t = s - s0
                        if 1 <= t <= 5: probs_out(t - 1, hb)
                        if 2 <= t <= 6: output(t - 2, hb)
                        if t == 3: tail_queries(hb)
                        if 0 <= t <= 4:
                            maxima(t, hb)
                            combine(t, hb)
                    if s == 10: rope_end("RQ", "B", qT[1])
                    if s == 12: rope_end("RK", "B", kT[1])
                    if s == 16: pooled_rows()
                    if 15 <= s < 23: key_sums(s - 15)
                    if s == 22:
                        gate("p0", mix[:, 2 * g, :])
                        sample_softmax()
                        window_means()
                    if s == 23:
                        mix_head(1)
                        sample_probs()
                        gate("p1", mix[:, 2 * g + 1, :])
                        pooled_out(0)
                        pooled_out(1)
                        sample_mix()

            for g in range(PAIRS):
                pair(g)
            dve.sem_inc(s_mix, 1)
            lows(X_OUT0)

            def out_stage(r, n0, post):
                with dve.Fori(0, KT // 2) as i:
                    for par in range(2):
                        k = 2 * i + par
                        dst = tile_at(mix, k).rearrange("p (a t) -> p a t", a=2)
                        gain = cols[:, bass.ds(2 * i + (post + par), 1)]
                        dve.wait_ge(s_sq, 2 * i + (r * KT + par + 1))
                        dve.tensor_scalar(dst, proj[(n0 + par) % 2][:, :, 0:TH], gain, None, ALU.mult).then_inc(s_evac, 1)
                dve.wait_ge(s_evac, n0 + KT + 2)

            def add_residual(k):
                dve.tensor_tensor(mix[:, k, :], mix[:, k, :], rstdf, ALU.mult).then_inc(s_yt, 1)

            out_stage(1, N_OUT0, POST0)
            dve.wait_ge(s_rstd, 2)

            def lows_and_sum(k):
                dve.wait_ge(s_xhi, X_IN1 + k + 1)
                dve.scalar_tensor_tensor(out=xlo[:, k, :], in0=mix[:, k, :], scalar=cols[:, PRE1 + k:PRE1 + k + 1],
                                         in1=xhi[:, k, :].bitcast(F32), op0=ALU.mult, op1=ALU.subtract).then_inc(s_x, 1)
                dve.wait_ge(s_sq, 2 * KT + k + 1)
                dve.wait_ge(s_acc, 2 * KT + k)
                if k == 0:
                    dve.tensor_copy(acc[:], sq_of[0]).then_inc(s_acc, 1)
                else:
                    dve.tensor_tensor(acc[:], acc[:], sq_of[k % 2], ALU.add).then_inc(s_acc, 1)

            for k in range(KT):
                add_residual(k)
                if k >= 2:
                    lows_and_sum(k - 2)
            lows_and_sum(KT - 2)
            lows_and_sum(KT - 1)
            dve.wait_ge(s_rstd, 3)
            dve.memset(st[0][:], 0.0)
            link(dve.memset(st[1][:], 0.0))
            dve.wait_ge(s_tile, N_LR + 3)
            dve.tensor_tensor(lrT[:].rearrange("p (a t) -> p a t", a=2), proj[0][0:RANK, :, 0:TH], rstd[0:RANK], ALU.mult).then_inc(s_evac, 1)
            dve.wait_ge(s_evac, N_LR + 3)
            dve.sem_inc(s_lr, 1)
            dve.wait_ge(s_c1, 16)
            dve.wait_ge(s_hst, 16 + 16 * KT)

            def head(s):
                n0 = N_HEAD + 12 * s

                def two(buf, j):
                    return buf[:, j, :].rearrange("p (a t) -> p a t", a=2)

                def gate(v):
                    dve.wait_ge(*gexp_ready.at("head", f"g{v}", s))
                    link(dve.tensor_scalar(te[:], te[:], 1.0, None, ALU.add))
                    link(dve.reciprocal(te[:], te[:]))
                    link(dve.tensor_tensor(tile_at(mix, 4 * s + v), tzf, tef, ALU.mult))

                def decay_logits(j):
                    for a in range(2):
                        dve.wait_ge(*full.at("head", f"G{j}{a}", s))
                        dve.tensor_scalar(gb[:, j, a * TH:(a + 1) * TH], bank_of("head", f"G{j}{a}")[:, 0:TH],
                                          ba_col(s, j), None, ALU.add).then_inc(s_fd, 1)
                    dve.wait_ge(*free_d.at("head", f"G{j}1", s))
                    dve.sem_inc(s_zg, 1)

                def ba_col(s, j):
                    return cols[:, bass.ds(2 * s + (BA + j), 1)]

                def running_sums(j):
                    dve.wait_ge(s_ga, 2 * s + j + 1)
                    dve.scalar_tensor_tensor(out=gb[:, j, :], in0=gb[:, j, :], scalar=0.0, in1=tef, op0=ALU.min, op1=ALU.subtract).then_inc(s_g, 1)
                    dve.wait_ge(s_g, 2 * s + j + 1)
                    for c in range(TT + 1):
                        w = P if c < TT else TAIL
                        x = gb[:, j, c * P:c * P + w]
                        last = dve.tensor_tensor_scan(x, ones[:, 0:w], x, 0.0, ALU.mult, ALU.add)
                    link(last)

                def references():
                    k = 1.0 / TAU
                    dve.tensor_scalar(refs[:, :, 0:16], gb[:, :, 15:TT * P:SUB], k, None, ALU.mult)
                    dve.tensor_scalar(refs[:, :, 16:17], gb[:, :, TT * P + 7:TT * P + 8], k, None, ALU.mult)
                    dve.tensor_scalar(lastr[:, :, 0:4], gb[:, :, P - 1:TT * P:P], k, None, ALU.mult)
                    dve.tensor_scalar(lastr[:, :, 4:5], gb[:, :, TP - 1:TP], k, None, ALU.mult).then_inc(s_refs, 1)
                    dve.wait_ge(s_refs, s + 1)

                def distances(c):
                    if c < TT:
                        x = gb[:, :, c * P:(c + 1) * P].rearrange("p j (i t) -> p j i t", t=SUB)
                        dve.tensor_tensor(eq[:].rearrange("p j (i t) -> p j i t", t=SUB), x, x[:, :, :, 15:16].to_broadcast([P, 2, 4, SUB]),
                                          ALU.subtract).then_inc(dq_ready.sem, 1)
                    else:
                        x = gb[:, :, TT * P:TP]
                        dve.tensor_tensor(eq[:, :, 0:TAIL], x, x[:, :, 7:8].to_broadcast([P, 2, TAIL]), ALU.subtract).then_inc(dq_ready.sem, 1)

                def factors(c):
                    c0, w = c * P, P if c < TT else TAIL
                    dve.wait_ge(*dec_ready.at("head", str(c), s))
                    dve.tensor_tensor(eq[:, :, 0:w], eq[:, :, 0:w], gq[:, :, c0:c0 + w], ALU.mult)
                    dve.tensor_tensor(el[:, :, 0:w], el[:, :, 0:w], gk[:, :, c0:c0 + w], ALU.mult)
                    for i in range(4 if c < TT else 1):
                        m = SUB * (i + 1) if c < TT else TAIL
                        x = ek[:, :, KOFF[i]:KOFF[i] + m]
                        last = dve.tensor_tensor(x, x, gk[:, :, c0:c0 + m], ALU.mult)
                    last.then_inc(fac_ready.sem, 1)

                def query_decay(c):
                    c0, w = c * P, P if c < TT else TAIL
                    dve.wait_ge(*ed_exp.at("head", str(c), s))
                    dve.tensor_tensor(ed[:, :, 0:w], ed[:, :, 0:w], gq[:, :, c0:c0 + w], ALU.mult).then_inc(ed_ready.sem, 1)

                def masked(c):
                    w = P if c < TT else TAIL
                    src = bank_of("head", f"SK{c}")
                    dve.wait_ge(*full.at("head", f"SK{c}", s))
                    for i in range(4 if c < TT else 1):
                        m, n = (SUB * (i + 1), SUB) if c < TT else (TAIL, TAIL)
                        x = slice(SUB * i, SUB * i + n)
                        dve.tensor_tensor(st[c % 2][0:m, x], src[0:m, x], lower[0:m, x], ALU.mult)
                    dve.tensor_copy(kd[c % 2][0:w, :], src[0:w, P:3 * P]).then_inc(s_fd, 1)

                def update(c):
                    for j in range(2):
                        dve.wait_ge(*full.at("head", f"SU{c}{j}", s))
                        src = bank_of("head", f"SU{c}{j}")
                        if c == 0:
                            dve.tensor_copy(state[:, j, :], src[:]).then_inc(s_fd, 1)
                        else:
                            dve.scalar_tensor_tensor(out=state[:, j, :], in0=state[:, j, :], scalar=elast[:, j, c:c + 1], in1=src[:],
                                                     op0=ALU.mult, op1=ALU.add).then_inc(s_fd, 1)

                def new_state(b):
                    i = b % 2
                    dve.wait_ge(s_sdec, 8 * s + b + 1)
                    dve.wait_ge(s_vb[i], 64 * s + 16 * (b // 2 + 1))
                    for j in range(2):
                        last = dve.scalar_tensor_tensor(out=sst[i][:, j, :], in0=vb[i][:], scalar=gk[:, j, TP + b:TP + b + 1], in1=sst[i][:, j, :],
                                                        op0=ALU.mult, op1=ALU.add)
                    last.then_inc(s_snew, 1)

                for c in range(24):
                    tile, done_tile = c // 2, c % 2 == 1
                    kind = HEAD_TILES[tile]
                    if done_tile:
                        par = (1 + tile) % 2
                        if kind[0] == "q": evac(n0 + tile, par, two(gq, int(kind[1])), 1.0 / TAU)
                        elif kind[0] == "k": evac(n0 + tile, par, two(gk, int(kind[1])))
                        else:
                            if kind in ("v1", "v2", "v3"):
                                dve.wait_ge(*full.at("head", f"VT1{int(kind[1]) - 1}", s))
                            if kind == "g0":
                                dve.wait_ge(*full.at("head", "VT13", s))
                            evac(n0 + tile, par, tz[:])
                    if c == 0: decay_logits(0)
                    if c == 1:
                        running_sums(0)
                        decay_logits(1)
                    if c == 2:
                        running_sums(1)
                        references()
                    if c == 8: distances(0)
                    if c == 9: factors(0)
                    if c == 15:
                        masked(0)
                        distances(1)
                    if c == 16: factors(1)
                    if c in (18, 20, 22): gate((c - 18) // 2)
                    if 17 <= c < 22:
                        k = c - 17
                        if k == 0:
                            dve.wait_ge(s_last, s + 1)
                            dve.wait_ge(s_gout, 16 * s)
                        update(k)
                        if k < 4:
                            query_decay(k + 1)
                            masked(k + 1)
                        if k < 3:
                            distances(k + 2)
                            factors(k + 2)
                    if 19 <= c < 23:
                        for b in (2 * (c - 19), 2 * (c - 19) + 1):
                            new_state(b)
                gate(3)
                dve.wait_ge(s_so, 8 * s + 8)
                dve.wait_ge(*free_a.at("head", "OC4", s))
                dve.tensor_copy(og[:, :, TP:T], score[:, 0:4 * NB].rearrange("p (v b) -> p v b", v=4)).then_inc(s_osg, 1)
                dve.wait_ge(*ro_ready.at("head", "o", s))
                r = ek[:].rearrange("p j t -> p (j t)")[:, 0:T]
                for v in range(4):
                    link(dve.scalar_tensor_tensor(out=og[:, v, :], in0=og[:, v, :], scalar=cols[:, GN + v:GN + v + 1], in1=r, op0=ALU.mult, op1=ALU.mult))
                    m = tile_at(mix, 4 * s + v)
                    last = dve.tensor_tensor(m, m, og[:, v, :], ALU.mult)
                    if v < 3:
                        link(last)
                last.then_inc(s_head, 1)
                dve.wait_ge(s_head, s + 1)

            with dve.Fori(0, GH) as s:
                chain.enter(s, HEAD_LINKS)
                head(s)
                chain.leave(GH)
            dve.sem_inc(s_mix, 1)
            lows(X_OUT1)
            out_stage(3, N_OUT1, POST1)
            dve.wait_ge(s_rstd, 4)
            for k in range(KT):
                add_residual(k)
            for i in range(0, 20, 2):
                w = P if i % 5 < TT else TB
                dve.wait_ge(s_fT, i + 1)
                if i >= 4:
                    dve.wait_ge(s_yout[i % 4], y_stores(i))
                dve.tensor_copy(y_buffer(i)[0:w], banks[i % 8].rearrange("p (k e) -> p k e", k=4)[0:w]).then_inc(s_fd2, 1)


_INS = ["x_prompt", "x_sample", "cache_k", "cache_v", "state_pool", "state_gla", "page_table", "meta_tokens",
        "pre_norm_0", "post_norm_0", "w_in_0", "pool_w_0", "pool_scale_0", "lambda_q1_0", "lambda_k1_0",
        "lambda_q2_0", "lambda_k2_0", "subln_0", "w_out_0", "pre_norm_1", "post_norm_1", "w_in_1",
        "gla_wa2_1", "gla_ba_1", "gla_norm_1", "w_out_1"]
_OUTS = [(1, SEQ, D), (NB, 1, D), (1, TP, NH, P), (1, TP, NH, P), (1, CTX, 1024), (1, GH, GK, GV),
         (NB, 1, NH, P), (NB, 1, NH, P), (NB, CTX, 1024), (NB, GH, GK, GV)]


def kernel(**inputs):
    import numpy as _np
    import concourse.bacc as _bacc
    from concourse.bass_utils import run_bass_kernel_spmd as _run

    nc = _bacc.Bacc("TRN2", target_bir_lowering=False, num_devices=1)
    arrays, aps = {}, {}
    tables = constants()
    for name, a in [(n, inputs[n]) for n in _INS] + list(zip(("both", "first", "lower"), tables)):
        a = _np.ascontiguousarray(a)
        arrays[f"in_{name}"] = a
        aps[name] = nc.dram_tensor(f"in_{name}", a.shape, mybir.dt.from_np(a.dtype), kind="ExternalInput").ap()
    outs = [nc.dram_tensor(f"out_{i}", s, F32, kind="ExternalOutput").ap() for i, s in enumerate(_OUTS)]
    build(nc, aps, outs, *[t.shape[1] for t in tables])
    r = _run(nc, [arrays], core_ids=[0])
    return tuple(r.results[0][f"out_{i}"] for i in range(len(_OUTS)))
```

```python
from contextlib import ExitStack

import numpy as np

import concourse.bass as bass
from concourse import mybir

F32 = mybir.dt.float32
F32R = mybir.dt.float32r
I32 = mybir.dt.int32
ALU = mybir.AluOpType
ACT = mybir.ActivationFunctionType
AX = mybir.AxisListType

P = 128
D = 2048
KT = D // P
HC = KT // 2
META, SEQ, NB = 16, 512, 8
TP = META + SEQ
T = TP + NB
TH = T // 2
TT = 4
TAIL = TP - TT * P
TB = T - TT * P
EPS = 1e-6
NH, PAIRS = 8, 4
PAGE, NPG = 128, 4
SCALE = 64 ** -0.5
LAM_INIT = 0.2
CTX = 15
GH, GK, GV, RANK, TAU = 4, 256, 512, 16, 16.0
SUB = 32
PRE0, POST0, PRE1, POST1, PSC, BA, GN, SUBG, SUBG8 = 0, 16, 32, 48, 64, 72, 80, 84, 85
C_U, C_PG, C_Q, C_K, C_V, C_AG = (1024 * i for i in range(6))
G_Q, G_K, G_V, G_G, G_LR = 0, 1024, 2048, 4096, 6144
KOFF = [0, 32, 96, 192]
KLEN = 320
PHYS = 40
RESULT_DVE = [16, 18]
RESULT_ACT = [i for i in range(20) if i not in RESULT_DVE]
TILE_ORDER = [0, 4, 1, 2, 3]
SS_COLS = [(0, TP // 2), (TP // 2, TP), (TP, T)]


class Signal:

    def __init__(self, sem, phases, by=1):
        self.sem, self.by, self.start, self.names, start = sem, by, {}, {}, 0
        for phase, names, times in phases:
            self.start[phase], self.names[phase] = start, list(names)
            start += len(names) * times

    def at(self, phase, name, i=0):
        names = self.names[phase]
        return self.sem, (i * len(names) + (self.start[phase] + names.index(name) + 1)) * self.by

    def before(self, phase, name, i=0):
        names = self.names[phase]
        return self.sem, (i * len(names) + (self.start[phase] + names.index(name))) * self.by


KEY_FETCH = {11: [2], 12: [3], 13: [4], 14: [5], 15: [6], 16: [7]}
KEY_PRODUCT = {10: [0], 11: [1], 12: [2], 13: [3], 14: [4], 15: [5], 16: [6], 17: [7]}
KEY_SUM = {11: [0], 12: [1], 13: [2], 14: [3], 15: [4], 16: [5], 17: [6, 7]}
PAIR_TILES = ["qA", "kA", "qB", "kB", "vA", "gA", "vB", "gB", "u0", "u1", "p0", "p1"]
PAIR_PLAN = {
    2: "RQ0A RQ1A", 4: "RK0A RK1A", 5: "KT0A KT1A", 6: "RQ0B RQ1B",
    8: "RK0B RK1B S0A", 9: "KT0B KT1B PT0A S1A", 10: "VT0A VT1A PT1A O0A S2A", 11: "PT2A O1A S3A",
    12: "PT3A O2A S4A", 13: "PT4A O3A", 14: "O4A VT0B VT1B", 15: "SS0A SS1A",
    16: "S0B SG", 17: "PT0B S1B ST", 18: "PT1B O0B S2B SD", 19: "PT2B O1B S3B V0",
    20: "PT3B O2B S4B V1 UT", 21: "PT4B O3B V2", 22: "O4B V3 PO00 PO01",
    23: "SN SS0B SS1B PO10 PO11",
}
HEAD_LINKS = 14
PAIR_LINKS_ACT, HEAD_LINKS_ACT = 8, 12
HEAD_TILES = ["v0", "v1", "v2", "v3", "q0", "q1", "k0", "k1", "g0", "g1", "g2", "g3"]
HEAD_PLAN = {
    1: "G00 G01", 2: "G10 G11 VT00 VT10", 4: "VT01 VT11", 6: "VT02 VT12", 8: "VT03 VT13",
    16: "SK0 B0 B1", 17: "OC0 SU00 SU01 SK1", 18: "OC1 SU10 SU11 B2 B3 SK2",
    19: "OC2 SU20 SU21 SK3", 20: "OC3 SU30 SU31 B4 B5 SK4", 21: "OC4 SU40 SU41",
    22: "B6 B7", 23: "SO SS0 SS1 SS2",
}
PAIR_OPS = [x for s in range(24) for x in PAIR_PLAN.get(s, "").split()]
HEAD_OPS = [x for s in range(24) for x in HEAD_PLAN.get(s, "").split()]
PAIR_JOBS = [x for x in PAIR_OPS if x not in [f"S{t}{h}" for t in range(5) for h in "AB"]]
HEAD_JOBS = [x for x in HEAD_OPS if x[0] != "B"]
JOBS = {"pair": PAIR_JOBS, "head": HEAD_JOBS}
BY_ACT = {"pair": [j for j in PAIR_JOBS if j[:2] in ("KT", "VT", "SS", "UT", "SN")],
          "head": [j for j in HEAD_JOBS if j[:2] in ("VT", "OC", "SS")]}
BY_DVE = {p: [j for j in JOBS[p] if j not in BY_ACT[p]] for p in JOBS}
ATTN = [f"{t}A" for t in range(5)] + ["0B", "1B", "s"] + [f"{t}B" for t in range(2, 5)]
SCORES = [x for x in ATTN if x != "s"]
N_OUT0 = len(PAIR_TILES) * PAIRS
N_LR = N_OUT0 + KT
N_HEAD = N_LR + 1
N_OUT1 = N_HEAD + len(HEAD_TILES) * GH
X_HI = {"in0": 0, "out0": KT, "in1": 2 * KT, "out1": 3 * KT}
X_LO = {"in0": ((0, HC), (0, 0)), "out0": ((KT, HC // 2), (0, HC // 2)),
        "in1": ((KT + HC, HC), (HC, 0)), "out1": ((2 * KT + HC, HC // 2), (HC, HC // 2))}


def constants():
    ident = np.eye(P)
    causal = np.where(np.arange(P)[None, :] <= np.arange(P)[:, None], 0.0, -1e30)
    rot = np.zeros((P, P))
    rows = np.arange(P) % 64
    for r in range(P):
        if rows[r] < 8:
            rot[r + 8, r] = -1.0
        elif rows[r] < 16:
            rot[r - 8, r] = 1.0
    pos = np.concatenate([np.arange(TP), np.full(NB, 512)]).astype(np.float64)
    inv = 500000.0 ** (-(np.arange(8) * 2.0) / 16)
    ang = pos[None, :] * inv[rows % 8][:, None]
    on = (rows < 16)[:, None]
    cos, sin = np.where(on, np.cos(ang), 1.0), np.where(on, np.sin(ang), 0.0)
    tail = np.zeros((P, 16 + 16 + 2 + 16 + 2))
    for m in range(2):
        for t in range(TAIL):
            r = TAIL * m + t
            tail[r, t] = 1.0
            tail[r, 16:32] = np.where(np.arange(TAIL) <= t, 0.0, -1e30)
            tail[r, 32 + m] = 1.0
    for r in range(4 * NB):
        tail[r, 34 + r // 2] = 1.0
        tail[r, 50 + r % 2] = 1.0
    both = np.concatenate([ident, np.ones((P, P))], 1)
    first = np.concatenate([causal, rot, cos, sin, tail], 1)
    count = np.stack([1.0 / np.minimum(w, np.arange(16) + 1) for w in (2, 4, 8, 16)]).reshape(1, 64)
    first = np.concatenate([first, np.repeat(count, P, 0)], 1)
    lower = (np.arange(P)[:, None] <= np.arange(P)[None, :]).astype(float)
    return [np.ascontiguousarray(a, dtype=np.float32) for a in (both, first, lower)]


def build(nc, A, O, n_both, n_first, n_second):
    y_prompt, y_sample, k_prompt, v_prompt, pool_prompt, gla_prompt, k_sample, v_sample, pool_sample, gla_sample = O
    ctx = ExitStack()
    with ctx:
        def sb(name, shape, dt=F32, where=ctx):
            return where.enter_context(nc.sbuf_tensor(name, shape, dt))

        def sem(name):
            return ctx.enter_context(nc.semaphore(name))

        h_dram = nc.dram_tensor("h_residual", [2, KT, P, T], F32, kind="Internal").ap()
        q_dram = nc.dram_tensor("q_sample_rows", [PAIRS, NB, 2 * P], F32, kind="Internal").ap()
        sn_dram = nc.dram_tensor("new_key_scores", [PAIRS, NB, 4], F32, kind="Internal").ap()
        vs_dram = nc.dram_tensor("v_sample_rows", [GH, NB, GV], F32, kind="Internal").ap()

        xhi = sb("xhi", [P, KT, T], F32R)
        xlo = sb("xlo", [P, KT, T], F32R)
        mix = sb("mix", [P, KT, T])
        wraw = sb("wraw", [P, 2, HC, P])
        whi = sb("whi", [P, 4, HC, P], F32R)
        wlo = sb("wlo", [P, 4, HC, P], F32R)
        both = sb("both", [P, n_both])
        cols = sb("cols", [P, 96])
        rstd = sb("rstd", [P, 2, TH])
        tz = sb("tz", [P, 2, TH])
        te = sb("te", [P, 2, TH])
        stat = sb("stat", [P, 32])
        ident, ones = both[:, 0:P], both[:, P:2 * P]
        tzf = tz[:].rearrange("p a t -> p (a t)")
        tef = te[:].rearrange("p a t -> p (a t)")
        rstdf = rstd[:].rearrange("p a t -> p (a t)")

        proj = [ctx.enter_context(nc.psum_tensor(f"proj{i}", [P, 2, 512], F32)) for i in range(2)]
        score = ctx.enter_context(nc.psum_tensor("score", [P, 1024], F32))
        scratch = [ctx.enter_context(nc.psum_tensor(f"scratch{i}", [P, 512], F32)) for i in range(2)]
        banks = [proj[0][:, 0, :], proj[0][:, 1, :], proj[1][:, 0, :], proj[1][:, 1, :],
                 score[:, 0:512], score[:, 512:1024], scratch[0][:], scratch[1][:]]

        s_const, s_rows = sem("s_const"), sem("s_rows")
        s_tok, s_diag = sem("s_tok"), sem("s_diag")
        s_xin = [sem(f"s_xin{i}") for i in range(5)]
        s_xt = sem("s_xt")
        s_xd, s_xa = sem("s_xd"), sem("s_xa")
        s_raw = [sem("s_raw0"), sem("s_raw1")]
        s_hi, s_lo = sem("s_hi"), sem("s_lo")
        s_tile = sem("s_tile")
        s_evac = sem("s_evac")
        s_xhi, s_x, s_xp = sem("s_xhi"), sem("s_x"), sem("s_xp")
        s_hd = sem("s_hd")
        s_sq, s_acc = sem("s_sq"), sem("s_acc")
        s_ss, s_rstd = sem("s_ss"), sem("s_rstd")
        s_hst, s_hld = sem("s_hst"), sem("s_hld")
        s_yt, s_hn = sem("s_yt"), sem("s_hn")
        s_yout = [sem("s_yout"), sem("s_yout_first")]
        s_fT, s_fd2, s_fa2 = sem("s_fT"), sem("s_fd2"), sem("s_fa2")
        s_lam, s_v = sem("s_lam"), sem("s_v")
        s_a, s_vc = sem("s_a"), sem("s_vc")
        s_full = sem("s_full")
        s_fd, s_fa = sem("s_fd"), sem("s_fa")
        s_store = sem("s_store")

        full = Signal(s_full, [("pair", PAIR_JOBS, PAIRS), ("head", HEAD_JOBS, GH)])
        free_d = Signal(s_fd, [("credit", "ab", 1), ("pair", BY_DVE["pair"], PAIRS), ("head", BY_DVE["head"], GH)])
        free_a = Signal(s_fa, [("credit", "ab", 1), ("pair", BY_ACT["pair"], PAIRS), ("head", BY_ACT["head"], GH)])

        def freed(phase, job, i):
            return (free_a if job in BY_ACT[phase] else free_d).at(phase, job, i)

        def freed_back(phase, job, i):
            sig = free_a if job in BY_ACT[phase] else free_d
            names = sig.names[phase]
            return sig.sem, i * len(names) + (sig.start[phase] + names.index(job) + 1 - len(names))

        def bank_of(phase, job):
            return scratch[JOBS[phase].index(job) % 2]

        class Chain:
            def __init__(self, sem, eng):
                self.sem, self.eng, self.base, self.n, self.i, self.per = sem, eng, 0, 0, None, 0

            def enter(self, i, per):
                self.base += self.n
                self.n, self.i, self.per = 0, i, per

            def leave(self, times):
                assert self.n == self.per, (self.n, self.per)
                self.base += self.per * times
                self.n, self.i = 0, None

            def link(self, ins):
                self.mark(ins)
                self.eng.wait_ge(self.sem, self.value())

            def mark(self, ins):
                ins.then_inc(self.sem, 1)
                self.n += 1

            def value(self):
                return self.base + self.n + (0 if self.i is None else self.i * self.per)


        sig = lambda name, *phases, by=1: Signal(sem(name), phases, by)
        score_ready = sig("scores_ready", ("pair", SCORES, PAIRS))
        max_ready = sig("max_ready", ("pair", ATTN, PAIRS))
        exp_done = sig("exp_done", ("credit", "a", 1), ("pair", ATTN, PAIRS))
        pd_ready = sig("pd_ready", ("pair", ATTN, PAIRS))
        rope_ready = sig("rope_ready", ("pair", ["qA", "kA", "qB", "kB"], PAIRS))
        osq_ready = sig("osq_ready", ("pair", ["A", "s", "B"], PAIRS))
        ro_ready = sig("ro_ready", ("pair", ["A", "s", "B"], PAIRS), ("head", ["o"], GH))
        sigmoid_ready = sig("sigmoid_ready", ("pair", ["gA", "gB", "p0", "p1"], PAIRS), ("head", ["g0", "g1", "g2", "g3"], GH))
        s_qk, s_kout = sem("s_qk"), sem("s_kout")
        s_vout = [sem("s_vout0"), sem("s_vout1")]
        s_sg, s_pw, s_uout = sem("s_sg"), sem("s_pw"), sem("s_uout")
        s_qb = [sem("s_qb0"), sem("s_qb1")]
        s_kv = [sem("s_kv0"), sem("s_kv1")]
        s_prod, s_kred = sem("s_prod"), sem("s_kred")
        s_snr, s_sns, s_sn = sem("s_snr"), sem("s_sns"), sem("s_sn")
        s_d, s_mix = sem("s_d"), sem("s_mix")
        s_init = sem("s_init")
        s_qblk = sem("s_qblk")
        s_c1 = sem("s_c1")
        s_lr = sem("s_lr")
        s_zg, s_ga, s_g = sem("s_zg"), sem("s_ga"), sem("s_g")
        s_refs, s_last = sem("s_refs"), sem("s_last")
        chunks = [str(c) for c in range(5)]
        dq_ready = sig("dq_ready", ("head", chunks, GH))
        dec_ready = sig("decays_ready", ("head", chunks, GH))
        fac_ready = sig("factors_ready", ("head", chunks, GH))
        ed_exp = sig("ed_exp", ("head", chunks[1:], GH))
        ed_ready = sig("ed_ready", ("head", chunks[1:], GH))
        s_c0, s_wa2, s_cols = sem("s_c0"), sem("s_wa2"), sem("s_cols")
        s_vs, s_vb = sem("s_vs"), [sem("s_vb0"), sem("s_vb1")]
        s_st, s_sdec, s_snew = [sem("s_st0"), sem("s_st1")], sem("s_sdec"), sem("s_snew")
        s_so = sem("s_so")
        s_sout = [sem("s_sout0"), sem("s_sout1")]
        s_gout, s_gsq = sem("s_gout"), sem("s_gsq")
        s_srow = sem("s_srow")
        s_head = sem("s_head")

        stage = ExitStack()
        xin = [sb(f"xin{i}", [P, D], where=stage) for i in range(5)]
        rows = sb("rows", [85, P], where=stage)
        stage.close()
        stage = ExitStack()
        sb0 = lambda name, shape, dt=F32: sb(name, shape, dt, stage)
        first = sb0("first", [P, n_first])
        causal, rot = first[:, 0:P], first[:, P:2 * P]
        cos, sin = first[:, 256:256 + T], first[:, 256 + T:256 + 2 * T]
        o = 256 + 2 * T
        tsel, tmask, tmap = first[:, o:o + 16], first[:, o + 16:o + 32], first[:, o + 32:o + 34]
        ssel, smap = first[:, o + 34:o + 50], first[:, o + 50:o + 52]
        counts = first[:, o + 52:o + 116].rearrange("p (g t) -> p g t", g=4)
        qT = [sb0(f"qT{i}", [P, T]) for i in range(2)]
        kT = [sb0(f"kT{i}", [P, T]) for i in range(2)]
        qblk = sb0("qblk", [P, 2 * TAIL])
        ktok = sb0("ktok", [P, TT, P])
        qk_tok = sb0("qk_tok", [32, 2, 2, P])
        vtok = [sb0(f"vtok{i}", [P, TT + 1, P]) for i in range(2)]
        vs = sb0("vs", [P, 2, NB])
        probw = sb0("probw", [P, 2 * (16 + TP)])
        pd = sb0("pd", [P, T])
        pdT = [sb0(f"pdT{i}", [P, 512]) for i in range(2)]
        oT = sb0("oT", [P, T])
        kv = [sb0(f"kv{i}", [P, NPG, 2 * P]) for i in range(2)]
        qb = [sb0(f"qb{i}", [P, 2 * P]) for i in range(2)]
        sall = sb0("sall", [P, NPG, 4 * NB])
        sprob = sb0("sprob", [4 * NB, 512])
        pds = sb0("pds", [P, 80])
        enew = sb0("enew", [4 * NB, 2 * NB])
        small = sb0("small", [P, 48])
        small2 = sb0("small2", [P, 48])
        ub = sb0("ub", [P, 2, 16 + T])
        pw = sb0("pw", [P, 2, 256])
        spool = sb0("spool", [NB * CTX, 256])
        utok = sb0("utok", [32, 256])
        lam4 = sb0("lam4", [P, 4, 64])
        lam = sb0("lam", [P, 8])
        pages = sb0("pages", [1, NB * NPG], I32)
        prob = probw[:, 0:2 * TP].rearrange("p (m t) -> p m t", m=2)
        win = [probw[:, 0:16 + TP], probw[:, 16 + TP:2 * (16 + TP)]]
        stage.close()
        stage = ExitStack()
        sb1 = lambda name, shape, dt=F32: sb(name, shape, dt, stage)
        hbuf = sb1("hbuf", [P, KT, T])
        acc = sb1("acc", [P, T])
        ybuf = sb1("ybuf", [P, 11, 4, P])
        stage.close()
        stage = ExitStack()
        lower = sb1("lower", [P, n_second])
        qd = sb1("qd", [P, 2, NB * NB])
        srow = tef[0:NB, 0:GV]
        lrT = sb1("lrT", [RANK, T])
        wa2 = sb1("wa2", [RANK, GK])
        gq = sb1("gq", [P, 2, T])
        gk = sb1("gk", [P, 2, T])
        gb = sb1("gb", [P, 2, T])
        gv = sb1("gv", [P, TT + 1, GV])
        eq = sb1("eq", [P, 2, P])
        ek = sb1("ek", [P, 2, KLEN])
        ed = sb1("ed", [P, 2, P])
        el = sb1("el", [P, 2, P])
        kd = sb1("kd", [P, GK])
        st = sb1("st", [P, P])
        state = sb1("state", [P, 2, GV])
        og = sb1("og", [P, 4, T])
        refs = sb1("refs", [P, 2, 17])
        lastr = sb1("lastr", [P, 2, 5])
        elast = sb1("elast", [P, 2, 5])
        eg = sb1("eg", [P, 2, NB])
        sst = [sb1(f"sst{i}", [P, 2, GV]) for i in range(2)]
        vb = [sb1(f"vb{i}", [P, GV]) for i in range(2)]
        stage.close()

        w_in0, w_out0, w_in1, w_out1 = A["w_in_0"], A["w_out_0"], A["w_in_1"], A["w_out_1"]
        eps, one = stat[:, 0:1], stat[:, 1:2]
        score2 = score[:].rearrange("p (b n) -> p b n", b=2)
        sq_of = [tzf, tef]

        def tile_at(buf, i, a=0, b=T):
            return buf[:, bass.ds(i, 1), a:b].rearrange("p o t -> p (o t)")

        def wchunk(w, col, kc, width=P):
            return w[kc * HC * P:(kc + 1) * HC * P, bass.ds(col, width)].rearrange("(k p) n -> p k n", p=P)

        def pair_col(i, g):
            base = {"q": C_Q, "k": C_K, "v": C_V, "g": C_AG, "u": C_U, "p": C_PG}[PAIR_TILES[i][0]]
            return (g + 1) * 256 + (base + P * (PAIR_TILES[i][1] in "B1") - 256)

        def head_col(i, s):
            kind, j = HEAD_TILES[i][0], int(HEAD_TILES[i][1])
            base, step = {"q": (G_Q, GK), "k": (G_K, GK), "v": (G_V, GV), "g": (G_G, GV)}[kind]
            return (s + 1) * step + (base + P * j - step)

        def y_buffer(i):
            i %= 15
            return wraw[:, i // 2, 4 * (i % 2):4 * (i % 2) + 4, :] if i < 4 else ybuf[:, i - 4]

        def residual_added(k):
            return (s_hd, k // 3 + 1) if k % 3 == 2 else (s_hn, KT + 2 * (k // 3) + k % 3 + 1)

        def result_read(i):
            return (s_fd2, RESULT_DVE.index(i) + 1) if i in RESULT_DVE else (s_fa2, RESULT_ACT.index(i) + 1)

        block = ctx.enter_context(nc.Block())

        @block.sync
        def _(sp):
            def load(n, kc, w, col, width=P):
                src = wchunk(w, col, kc, width)
                sp.wait_ge(s_lo, 2 * n + kc + 1)
                sp.dma_start(wraw[:, kc, :, 0:width], src).then_inc(s_raw[kc], 16)

            xp, xs, mt = A["x_prompt"][0], A["x_sample"].rearrange("b s d -> (b s) d"), A["meta_tokens"]
            sp.dma_start(both[:], A["both"]).then_inc(s_const, 16)
            sp.dma_start(xin[0][0:META, :], mt).then_inc(s_xin[0], 16)
            sp.dma_start(xin[0][META:P, :], xp[0:P - META, :]).then_inc(s_xin[0], 16)
            sp.dma_start(xin[4][0:TAIL, :], xp[SEQ - TAIL:SEQ, :]).then_inc(s_xin[4], 16)
            sp.dma_start(xin[4][TAIL:TB, :], xs).then_inc(s_xin[4], 16)
            for name, r, n in (("pre_norm_0", PRE0, 16), ("post_norm_0", POST0, 16), ("pre_norm_1", PRE1, 16),
                               ("post_norm_1", POST1, 16), ("pool_scale_0", PSC, 8), ("gla_ba_1", BA, 8),
                               ("gla_norm_1", GN, 4), ("subln_0", SUBG, 1)):
                sp.dma_start(rows[r:r + n, :], A[name].rearrange("(k p) -> k p", p=P)).then_inc(s_rows, 16)
            for tt in range(1, TT):
                sp.dma_start(xin[tt][:], xp[tt * P - META:(tt + 1) * P - META, :]).then_inc(s_xin[tt], 16)
            load(0, 0, w_in0, pair_col(0, 0))
            load(0, 1, w_in0, pair_col(0, 0))
            sp.dma_start(pool_sample[:, 0:CTX - 1, :], A["state_pool"][:, 1:CTX, :]).then_inc(s_store, 16)
            sp.wait_ge(s_xd, 10)
            sp.wait_ge(s_xa, 10)
            sp.wait_ge(s_tok, 6)
            sp.wait_ge(s_cols, 1)
            sp.dma_start(first[:], A["first"]).then_inc(s_c0, 16)
            sp.dma_start(pages[:], A["page_table"].rearrange("b (o n) -> o (b n)", o=1)).then_inc(s_c0, 16)
            for i, name in enumerate(("lambda_q1_0", "lambda_k1_0", "lambda_q2_0", "lambda_k2_0")):
                sp.dma_start(lam4[:, i, :], A[name].rearrange("(o n) -> o n", o=1).to_broadcast([P, 64])).then_inc(s_c0, 16)

            def pair(g, skip=0):
                for c in range(skip, 24):
                    load(12 * g + c // 2, c % 2, w_in0, pair_col(c // 2, g))
                    if skip and c == 5:
                        sp.dma_start(h_dram[0].rearrange("k p t -> p k t"), mix[:]).then_inc(s_hst, 16)
                    if c == 13:
                        dst = sn_dram[bass.ds(g, 1)].rearrange("o b c -> (o b) c")
                        sp.wait_ge(s_snr, g + 2)
                        sp.dma_start(dst, small2[TAIL:TB, 0:4]).then_inc(s_sns, 16)
                    if c == 14:
                        src = sn_dram[bass.ds(g, 1)].rearrange("o b (c e) -> (o b c) e", e=1)
                        sp.wait_ge(s_sns, g * 16 + 16)
                        sp.dma_start(small2[0:4 * NB, 40:41], src).then_inc(s_sn, 16)

            pair(0, skip=2)
            with sp.Fori(1, PAIRS) as g:
                pair(g)

            def out_proj(n0, w, i):
                for par in range(2):
                    for kc in range(2):
                        load(n0 + par + 2 * i, kc, w, 256 * (i + 1) + (P * par - 256))

            with sp.Fori(0, KT // 2) as i:
                out_proj(N_OUT0, w_out0, i)
            for kc in range(2):
                load(N_LR, kc, w_in1, G_LR, RANK)

            def head(s):
                for c in range(24):
                    load(N_HEAD + c // 2 + 12 * s, c % 2, w_in1, head_col(c // 2, s))
                    if c == 2:
                        sp.wait_ge(s_hn, KT)
                        src = A["gla_wa2_1"][:, bass.ds((s + 1) * GK - GK, GK)]
                        sp.wait_ge(*freed_back("head", "G11", s))
                        sp.dma_start(wa2[:], src).then_inc(s_wa2, 16)

            with sp.Fori(0, GH) as s:
                head(s)
            with sp.Fori(0, KT // 2) as i:
                out_proj(N_OUT1, w_out1, i)
            yp, ys = y_prompt[0], y_sample.rearrange("b s d -> (b s) d")
            for i in range(20):
                kq, tt, buf = i // 5, i % 5, y_buffer(i)
                f = slice(kq * 512, (kq + 1) * 512)
                sp.wait_ge(*result_read(i))
                cut = lambda a, b: buf[a:b].rearrange("p k e -> p (k e)")
                if tt == 0:
                    sp.dma_start(yp[0:P - META, f], cut(META, P)).then_inc(s_yout[i < 5], 16)
                elif tt < TT:
                    sp.dma_start(yp[tt * P - META:(tt + 1) * P - META, f], cut(0, P)).then_inc(s_yout[i < 5], 16)
                else:
                    sp.dma_start(yp[SEQ - TAIL:SEQ, f], cut(0, TAIL)).then_inc(s_yout[i < 5], 16)
                    sp.dma_start(ys[:, f], cut(TAIL, TB)).then_inc(s_yout[i < 5], 16)
            sp.wait_ge(s_yout[0], 16 * 18)
            sp.wait_ge(s_yout[1], 16 * 6)
            sp.wait_ge(s_store, 16)
            sp.wait_ge(s_hst, 16 + 16 * KT)

        @block.gpsimd
        def _(pool):
            def lo(c, slot, width=P):
                kc = slot % 2
                pool.wait_ge(s_hi, c + 1)
                pool.tensor_tensor(wlo[:, slot, :, 0:width], wraw[:, kc, :, 0:width],
                                   whi[:, slot, :, 0:width].bitcast(F32), ALU.subtract).then_inc(s_lo, 1)

            def accumulate(r, j, k):
                pool.wait_ge(s_sq, (r - 1) * KT + k + 1)
                if isinstance(k, int) and k == 0:
                    pool.tensor_copy(acc[:], sq_of[j]).then_inc(s_acc, 1)
                else:
                    pool.wait_ge(s_acc, (r - 1) * KT + k)
                    pool.tensor_tensor(acc[:], acc[:], sq_of[j], ALU.add).then_inc(s_acc, 1)

            pool.sem_inc(s_lo, 2)
            lo(0, 0)
            lo(1, 1)

            def pair(g):
                for s in range(24):
                    for b in KEY_PRODUCT.get(s, ()):
                        pool.wait_ge(s_kv[b % 2], 512 * g + 64 * (b // 2 + 1))
                        pool.wait_ge(s_qb[b % 2], 64 * g + 16 * (b // 2 + 1))
                        pool.tensor_tensor(kv[b % 2][:], kv[b % 2][:], qb[b % 2][:, None, :].to_broadcast([P, NPG, 2 * P]),
                                           ALU.mult).then_inc(s_prod, 1)
                    lo(24 * g + s + 2, (s + 2) % 4)

            with pool.Fori(0, PAIRS) as g:
                pair(g)

            def out_proj(r, n0, i, par, last=False, narrow=False):
                n, slot = n0 + 2 * i + par, (2 * (n0 + par) + 2) % 4
                if not last:
                    for kc in range(2):
                        lo(2 * n + 2 + kc, slot + kc, RANK if narrow else P)
                accumulate(r, par, 2 * i + par)

            def lows(stage):
                for k in range(1, KT, 2):
                    pool.wait_ge(s_xhi, X_HI[stage] + k + 1)
                    pool.tensor_tensor(xlo[:, k, :], mix[:, k, :], xhi[:, k, :].bitcast(F32), ALU.subtract).then_inc(s_xp, 1)

            lows("out0")
            for par in range(2):
                out_proj(1, N_OUT0, 0, par)
            with pool.Fori(1, KT // 2 - 1) as i:
                for par in range(2):
                    out_proj(1, N_OUT0, i, par)
            out_proj(1, N_OUT0, KT // 2 - 1, 0)
            out_proj(1, N_OUT0, KT // 2 - 1, 1, narrow=True)
            for k in range(KT):
                if k in (8, 12):
                    lo(2 * N_HEAD + (k == 12), (2 * N_HEAD + (k == 12)) % 4)
                pool.wait_ge(s_yt, k + 1)
                pool.wait_ge(s_hld, 16)
                pool.tensor_tensor(mix[:, k, :], mix[:, k, :], hbuf[:, k, :], ALU.add).then_inc(s_hn, 1)
            with pool.Fori(0, GH) as s:
                for c in range(24):
                    lo(24 * s + 2 * N_HEAD + c + 2, (2 * N_HEAD + c + 2) % 4)
            lows("out1")
            for par in range(2):
                out_proj(3, N_OUT1, 0, par)
            with pool.Fori(1, KT // 2 - 1) as i:
                for par in range(2):
                    out_proj(3, N_OUT1, i, par)
            out_proj(3, N_OUT1, KT // 2 - 1, 0)
            out_proj(3, N_OUT1, KT // 2 - 1, 1, last=True)
            for k in [k for k in range(KT) if k % 3 < 2]:
                pool.wait_ge(s_yt, KT + k + 1)
                pool.wait_ge(s_hld, 32)
                pool.tensor_tensor(mix[:, k, :], mix[:, k, :], hbuf[:, k, :], ALU.add).then_inc(s_hn, 1)

        @block.scalar
        def _(act):
            chain = Chain(s_a, act)

            def split(n, kc, par, width=P):
                act.wait_ge(s_raw[kc], n * 16 + 16)
                act.wait_ge(s_tile, n + 1)
                act.activation(whi[:, 2 * par + kc, :, 0:width], wraw[:, kc, :, 0:width], ACT.Copy).then_inc(s_hi, 1)

            def square(r, j, k, src, ready=None):
                if not (isinstance(k, int) and r == 1 and k < 2):
                    act.wait_ge(s_acc, (r - 1) * KT + k - 1)
                act.activation(sq_of[j] if src.shape[1] == T else (tz, te)[j][:], src, ACT.Square).then_inc(s_sq, 1)

            def finish_rms(r):
                act.wait_ge(s_ss, r + 1)
                chain.link(act.activation(rstd[:], score2[:, :, 0:TH], ACT.Ln, scale=1.0 / D, bias=eps))
                act.activation(rstd[:], rstd[:], ACT.Exp, scale=-0.5).then_inc(s_rstd, 1)

            act.preload_act_table_set("natural_log_exp_and_others")
            act.wait_ge(s_init, 1)
            act.sem_inc(s_tile, 2)
            act.sem_inc(s_fa, 2)
            for s_credit in (s_kout, s_qk, s_snr, *s_vout, s_uout, exp_done.sem, *s_sout, s_gout):
                act.sem_inc(s_credit, 1)
            squares = [x[:].rearrange("p k t -> p (k t)")[:, a:a + D] for x, a in ((xhi, 0), (xhi, D), (xhi, 2 * D), (xhi, 3 * D), (xlo, 0))]
            for i in range(1, 20, 2):
                tt, kq = TILE_ORDER[i // 4], i % 4
                w = P if tt < TT else TB
                if kq == 1:
                    act.wait_ge(s_xin[tt], 32 if tt in (0, 4) else 16)
                    act.activation(squares[tt][0:w], xin[tt][0:w, :], ACT.Square, accum_out=stat[0:w, 2 + tt:3 + tt]).then_inc(s_tok, 1)
                act.wait_ge(s_xt, i + 1)
                act.copy(mix[:, 4 * kq:4 * kq + 4, tt * P:tt * P + w],
                         banks[i % 8].rearrange("p (k t) -> p k t", k=4)[:, :, 0:w]).then_inc(s_xa, 1)
                if i == 17:
                    act.wait_ge(s_tok, 5)
                    chain.link(act.activation(stat[:, 2:7], stat[:, 2:7], ACT.Ln, scale=1.0 / D, bias=eps))
                    act.activation(stat[:, 8:13], stat[:, 2:7], ACT.Exp, scale=-0.5).then_inc(s_tok, 1)
            split(0, 0, 0)
            act.wait_ge(s_xd, 10)
            act.wait_ge(s_xa, 10)
            act.wait_ge(s_cols, 1)
            for k in range(KT):
                act.activation(xhi[:, k, :], mix[:, k, :], ACT.Copy, scale=cols[:, PRE0 + k:PRE0 + k + 1]).then_inc(s_xhi, 1)
                if k == HC - 1:
                    split(0, 1, 0)
            act.wait_ge(s_lam, 1)
            act.activation(lam[:, 6:8], lam[:, 4:6], ACT.Exp).then_inc(s_lam, 1)

            def sigmoid(phase, name, n, i):
                act.wait_ge(s_evac, n + 3)
                chain.link(act.activation(te[:], tz[:], ACT.Exp, scale=-1.0))
                chain.link(act.activation(te[:], te[:], ACT.Ln, bias=one))
                act.activation(te[:], te[:], ACT.Exp, scale=-1.0).then_inc(sigmoid_ready.sem, 1)

            def pair(g):
                n0 = 12 * g

                def k_rows(hb):
                    h, x = 2 * g + hb, "AB"[hb]
                    act.wait_ge(*full.at("pair", "KT0" + x, g))
                    act.wait_ge(s_kout, 32 * g + (16 * hb + 1))
                    act.copy(ktok[:], bank_of("pair", "KT0" + x)[:].rearrange("p (t e) -> p t e", t=TT)).then_inc(s_fa, 1)
                    act.wait_ge(*full.at("pair", "KT1" + x, g))
                    act.wait_ge(s_qk, 96 * g + (48 * hb + 1))
                    act.wait_ge(s_snr, g + 1)
                    act.copy(qk_tok[0:TB, :, hb, :], bank_of("pair", "KT1" + x)[0:TB, 0:2 * P].rearrange("p (a e) -> p a e", a=2)).then_inc(s_fa, 1)
                    act.wait_ge(*free_a.at("pair", "KT1" + x, g))
                    act.dma_start(k_prompt[0, 0:TT * P, bass.ds(h, 1), :].rearrange("(t p) o e -> p (t o) e", p=P), ktok[:]).then_inc(s_kout, 16)
                    act.dma_start(k_prompt[0, TT * P:TP, bass.ds(h, 1), :].rearrange("t o e -> t (o e)"), qk_tok[0:TAIL, 1, hb, :]).then_inc(s_qk, 16)
                    act.dma_start(k_sample[:, 0, bass.ds(h, 1), :].rearrange("b o e -> b (o e)"), qk_tok[TAIL:TB, 1, hb, :]).then_inc(s_qk, 16)
                    act.dma_start(q_dram[bass.ds(g, 1), :, hb * P:(hb + 1) * P].rearrange("o b e -> (o b) e"), qk_tok[TAIL:TB, 0, hb, :]).then_inc(s_qk, 16)

                def v_rows(hb):
                    h, x = 2 * g + hb, "AB"[hb]
                    act.wait_ge(s_vout[hb], 48 * g + 1)
                    act.wait_ge(*full.at("pair", "VT0" + x, g))
                    act.copy(vtok[hb][:, 0:TT, :], bank_of("pair", "VT0" + x)[:].rearrange("p (t e) -> p t e", t=TT)).then_inc(s_fa, 1)
                    act.wait_ge(*full.at("pair", "VT1" + x, g))
                    act.copy(vtok[hb][0:TB, TT, :], bank_of("pair", "VT1" + x)[0:TB, 0:P]).then_inc(s_fa, 1)
                    act.wait_ge(*free_a.at("pair", "VT1" + x, g))
                    act.dma_start(v_prompt[0, 0:TT * P, bass.ds(h, 1), :].rearrange("(t p) o e -> p (t o) e", p=P), vtok[hb][:, 0:TT, :]).then_inc(s_vout[hb], 16)
                    act.dma_start(v_prompt[0, TT * P:TP, bass.ds(h, 1), :].rearrange("t o e -> t (o e)"), vtok[hb][0:TAIL, TT, :]).then_inc(s_vout[hb], 16)
                    act.dma_start(v_sample[:, 0, bass.ds(h, 1), :].rearrange("b o e -> b (o e)"), vtok[hb][TAIL:TB, TT, :]).then_inc(s_vout[hb], 16)

                def exps(t, hb):
                    act.wait_ge(*max_ready.at("pair", f"{t}{'AB'[hb]}", g))
                    if t < TT:
                        n = (t + 1) * P
                        for m in range(2):
                            last = act.activation(prob[:, m, 0:n], score2[:, m, 0:n], ACT.Exp, bias=small[:, 2 + m:3 + m],
                                                  scale=SCALE, accum_out=small[:, 4 + m:5 + m])
                    else:
                        last = act.activation(probw[0:2 * TAIL, 0:TP], score[0:2 * TAIL, 0:TP], ACT.Exp,
                                              bias=small[0:2 * TAIL, 2:3], scale=SCALE, accum_out=small[0:2 * TAIL, 4:5])
                    last.then_inc(exp_done.sem, 1)

                def o_square(hb):
                    act.wait_ge(*free_d.at("pair", f"O{TT}{'AB'[hb]}", g))
                    act.activation(pd[:, 0:TP], oT[:, 0:TP], ACT.Square).then_inc(osq_ready.sem, 1)

                def o_rstd(hb):
                    x, half = "AB"[hb], TP // 2
                    for a in range(2):
                        act.wait_ge(*full.at("pair", f"SS{a}{x}", g))
                        act.activation(pd[:, a * half:(a + 1) * half], bank_of("pair", f"SS{a}{x}")[:, 0:half], ACT.Ln,
                                       scale=1.0 / P, bias=eps).then_inc(s_fa, 1)
                    act.wait_ge(*free_a.at("pair", f"SS1{x}", g))
                    act.activation(pd[:, 0:TP], pd[:, 0:TP], ACT.Exp, scale=-0.5).then_inc(ro_ready.sem, 1)

                def fetch(cache, b, ready):
                    page = [act.value_load(pages[0:1, b * NPG + pg:b * NPG + pg + 1], min_val=0, max_val=PHYS - 1) for pg in range(NPG)]
                    src = [cache[bass.ds(p, 1), :, bass.ds(g * 256, 256)].rearrange("o p d -> p (o d)") for p in page]
                    act.wait_ge(*ready)
                    for pg in range(NPG):
                        act.dma_start(kv[b % 2][:, pg, :], src[pg]).then_inc(s_kv[b % 2], 16)

                def fetch_q(b):
                    act.dma_start(qb[b % 2][:], q_dram[bass.ds(g, 1), b, :].to_broadcast([P, 2 * P])).then_inc(s_qb[b % 2], 16)

                ck = A["cache_k"].rearrange("n p h e -> n p (h e)")
                cv = A["cache_v"].rearrange("n p h e -> n p (h e)")
                for s in range(24):
                    tile = (s + 2) // 2
                    split(n0 + tile, s % 2, tile % 2)
                    if s == 3:
                        act.wait_ge(*free_d.before("pair", BY_DVE["pair"][0], g))
                        act.dma_start(spool[:], A["state_pool"][:, :, bass.ds(g * 256, 256)].rearrange("b r c -> (b r) c")).then_inc(s_sg, 16)
                        act.dma_start(pw[:], A["pool_w_0"][bass.ds(g, 1)].rearrange("o (c p) d -> p (o c) d", p=P)).then_inc(s_pw, 16)
                    if s == 5: k_rows(0)
                    if s == 8:
                        used = free_d.before("pair", BY_DVE["pair"][0], g)
                        fetch(ck, 0, used)
                        fetch(ck, 1, used)
                    if s == 9: k_rows(1)
                    if s == 10: v_rows(0)
                    if s == 12: sigmoid("pair", "gA", n0 + 5, g)
                    if s == 14:
                        v_rows(1)
                        o_square(0)
                    if s == 15: o_rstd(0)
                    if s == 16: sigmoid("pair", "gB", n0 + 7, g)
                    if 8 <= s < 13: exps(s - 8, 0)
                    if 16 <= s < 21: exps(s - 16, 1)
                    for b in KEY_FETCH.get(s, ()):
                        act.wait_ge(s_prod, 8 * g + b - 1)
                        fetch_q(b)
                        fetch(ck, b, (s_kred, 8 * g + b - 1))
                    if s == 10:
                        act.wait_ge(s_qk, 96 * g + 97)
                        fetch_q(0)
                        fetch_q(1)
                    for b in (0, 1):
                        if NB - 2 + b in KEY_SUM.get(s, ()):
                            fetch(cv, b, (s_kred, 8 * g + 7 + b))
                    if s == 17:
                        act.wait_ge(*max_ready.at("pair", "s", g))
                        act.activation(sprob[:], sprob[:], ACT.Exp, bias=small2[0:32, 34:35], scale=SCALE, accum_out=small2[0:32, 35:36])
                        act.activation(small2[0:32, 36:37], small2[0:32, 40:41], ACT.Exp, bias=small2[0:32, 34:35], scale=SCALE).then_inc(exp_done.sem, 1)
                    if s == 21:
                        act.wait_ge(*full.at("pair", "UT", g))
                        act.wait_ge(s_uout, 32 * g + 1)
                        act.copy(utok[0:TB, :], bank_of("pair", "UT")[0:TB, 0:256]).then_inc(s_fa, 1)
                        act.wait_ge(*free_a.at("pair", "UT", g))
                        act.dma_start(pool_prompt[0, :, bass.ds(g * 256, 256)], utok[1:TAIL, :]).then_inc(s_uout, 16)
                        act.dma_start(pool_sample[:, CTX - 1, bass.ds(g * 256, 256)], utok[TAIL:TB, :]).then_inc(s_uout, 16)
                    if 19 <= s < 22:
                        for b in (2 * (s - 18), 2 * (s - 18) + 1):
                            fetch(cv, b, full.at("pair", f"V{s - 19}", g))
                    if s == 22:
                        sigmoid("pair", "p0", n0 + 10, g)
                        act.wait_ge(*free_d.at("pair", "V3", g))
                        act.activation(small2[:, 0:16], small[:, 32:48], ACT.Square).then_inc(osq_ready.sem, 1)
                        o_square(1)
                    if s == 23:
                        act.wait_ge(*full.at("pair", "SN", g))
                        act.activation(small2[:, 16:32], bank_of("pair", "SN")[:, 0:16], ACT.Ln, scale=1.0 / P, bias=eps).then_inc(s_fa, 1)
                        act.wait_ge(*free_a.at("pair", "SN", g))
                        act.activation(small2[:, 16:32], small2[:, 16:32], ACT.Exp, scale=-0.5).then_inc(ro_ready.sem, 1)
                        o_rstd(1)
                sigmoid("pair", "p1", n0 + 11, g)

            with act.Fori(0, PAIRS) as g:
                chain.enter(g, PAIR_LINKS_ACT)
                pair(g)
                chain.leave(PAIRS)
            for s_out, n in ((s_kout, 32), (s_qk, 96), (s_vout[0], 48), (s_vout[1], 48), (s_uout, 32)):
                act.wait_ge(s_out, n * PAIRS + 1)

            def mix_hi(phase):
                act.wait_ge(s_tile, (N_OUT0 if phase == 0 else N_OUT1) + 2)
                early = ((2 * PAIRS - 2, free_d.at("pair", "PO11", PAIRS - 2)), (4 * GH - 4, (s_head, GH - 1)))[phase]
                act.wait_ge(*early[1])
                for k in range(KT):
                    if k == early[0]:
                        act.wait_ge(s_mix, phase + 1)
                    act.activation(xhi[:, k, :], mix[:, k, :], ACT.Copy).then_inc(s_xhi, 1)

            def out_proj(r, n0, i, par, last=False, narrow=False):
                n = n0 + 2 * i + par
                if not last:
                    for kc in range(2):
                        split(n + 1, kc, (n0 + par + 1) % 2, RANK if narrow else P)
                act.wait_ge(s_tile, n + 3)
                square(r, par, 2 * i + par, proj[(n0 + par) % 2][:, :, 0:TH])

            def out_stage(r, n0, narrow):
                for par in range(2):
                    out_proj(r, n0, 0, par)
                with act.Fori(1, KT // 2 - 1) as i:
                    for par in range(2):
                        out_proj(r, n0, i, par)
                out_proj(r, n0, KT // 2 - 1, 0)
                out_proj(r, n0, KT // 2 - 1, 1, last=not narrow, narrow=narrow)

            def fetch_h(layer):
                act.dma_start(hbuf[:], h_dram[layer].rearrange("k p t -> p k t")).then_inc(s_hld, 16)

            mix_hi(0)
            fetch_h(0)
            out_stage(1, N_OUT0, True)
            finish_rms(1)
            split(N_HEAD, 0, 1)
            split(N_HEAD, 1, 1)
            for k in range(KT):
                act.wait_ge(s_hn, k + 1)
                act.dma_start(h_dram[1, k], mix[:, k, :]).then_inc(s_hst, 16)
                act.activation(xhi[:, k, :], mix[:, k, :], ACT.Copy, scale=cols[:, PRE1 + k:PRE1 + k + 1]).then_inc(s_xhi, 1)
                square(2, k % 2, k, mix[:, k, :])
            act.dma_start(lower[:], A["lower"]).then_inc(s_c1, 16)
            finish_rms(2)
            act.wait_ge(s_hst, 16 + 16 * KT)

            def head(s):
                n0 = N_HEAD + 12 * s

                def decay_logs(j):
                    act.wait_ge(s_zg, 2 * s + j + 1)
                    if j:
                        act.wait_ge(s_g, 2 * s + 1)
                    chain.link(act.activation(tef, gb[:, j, :], ACT.Abs))
                    chain.link(act.activation(tef, tef, ACT.Exp, scale=-1.0))
                    act.activation(tef, tef, ACT.Ln, bias=one).then_inc(s_ga, 1)

                def decays(c):
                    c0, w = c * P, P if c < TT else TAIL
                    act.wait_ge(*dq_ready.at("head", str(c), s))
                    act.activation(eq[:, :, 0:w], eq[:, :, 0:w], ACT.Exp, scale=1.0 / TAU)
                    for j in range(2):
                        for i in range(4 if c < TT else 1):
                            m, ref = (SUB * (i + 1), 4 * c + i) if c < TT else (TAIL, 16)
                            act.activation(ek[:, j, KOFF[i]:KOFF[i] + m], gb[:, j, c0:c0 + m], ACT.Exp,
                                           scale=-1.0 / TAU, bias=refs[:, j, ref:ref + 1])
                        last = act.activation(el[:, j, 0:w], gb[:, j, c0:c0 + w], ACT.Exp, scale=-1.0 / TAU, bias=lastr[:, j, c:c + 1])
                    last.then_inc(dec_ready.sem, 1)

                def decay_start(c):
                    c0, w = c * P, P if c < TT else TAIL
                    act.activation(ed[:, :, 0:w], gb[:, :, c0:c0 + w], ACT.Exp, scale=1.0 / TAU).then_inc(ed_exp.sem, 1)

                def o_rows(c):
                    c0, w = c * P, P if c < TT else TAIL
                    act.wait_ge(*full.at("head", f"OC{c}", s))
                    act.copy(og[:, :, c0:c0 + w], bank_of("head", f"OC{c}")[:, 0:4 * w].rearrange("p (v t) -> p v t", v=4)).then_inc(s_fa, 1)

                def v_rows(j):
                    act.wait_ge(*full.at("head", f"VT0{j}", s))
                    act.copy(gv[:, 0:TT, j * P:(j + 1) * P], bank_of("head", f"VT0{j}")[:].rearrange("p (t e) -> p t e", t=TT)).then_inc(s_fa, 1)
                    act.wait_ge(*full.at("head", f"VT1{j}", s))
                    act.copy(gv[0:TB, TT, j * P:(j + 1) * P], bank_of("head", f"VT1{j}")[0:TB, 0:P]).then_inc(s_fa, 1)

                def fetch_s(b):
                    i = b % 2
                    act.wait_ge(s_so, 8 * s + b - 1) if b >= 2 else None
                    act.wait_ge(s_sout[i], 64 * s + (16 * (b // 2) + 1))
                    act.dma_start(sst[i][:], A["state_gla"][b, bass.ds(s, 1)].rearrange("o (j p) v -> p (o j) v", p=P)).then_inc(s_st[i], 16)
                    act.dma_start(vb[i][:], vs_dram[bass.ds(s, 1), b, :].to_broadcast([P, GV])).then_inc(s_vb[i], 16)

                def decay_s(b):
                    i = b % 2
                    act.wait_ge(s_st[i], 64 * s + 16 * (b // 2 + 1))
                    for j in range(2):
                        last = act.activation(sst[i][:, j, :], sst[i][:, j, :], ACT.Copy, scale=eg[:, j, b:b + 1])
                    last.then_inc(s_sdec, 1)

                def store_s(b):
                    i = b % 2
                    act.wait_ge(s_snew, 8 * s + b + 1)
                    act.dma_start(gla_sample[b, bass.ds(s, 1)].rearrange("o (j p) v -> p (o j) v", p=P), sst[i][:]).then_inc(s_sout[i], 16)

                for c in range(24):
                    tile = (c + 2) // 2
                    split(n0 + tile, c % 2, (tile + 1) % 2)
                    if c == 2: decay_logs(0)
                    if c == 3: decay_logs(1)
                    if c == 4:
                        act.wait_ge(s_refs, s + 1)
                        act.activation(elast[:], lastr[:], ACT.Exp)
                        act.activation(eg[:], gb[:, :, TP:T], ACT.Exp, scale=1.0 / TAU).then_inc(s_last, 1)
                    if c in (2, 4, 6, 8): v_rows((c - 2) // 2)
                    if c == 9:
                        act.wait_ge(*free_a.at("head", "VT13", s))
                        act.dma_start(vs_dram[bass.ds(s, 1)].rearrange("o b v -> (o b) v"), gv[TAIL:TB, TT, :]).then_inc(s_vs, 16)
                        decays(0)
                    if c == 10:
                        act.wait_ge(s_vs, 16 * s + 16)
                        fetch_s(0)
                        fetch_s(1)
                    if c == 12:
                        decay_s(0)
                        decay_s(1)
                    if c in (18, 20, 22):
                        decay_s(c - 16)
                        decay_s(c - 15)
                    if c == 16: decays(1)
                    if c in (17, 19, 21, 23):
                        for b in (c - 17, c - 16):
                            store_s(b)
                        for b in (c - 15, c - 14) if c < 23 else ():
                            fetch_s(b)
                    if c in (18, 20, 22): sigmoid("head", f"g{(c - 18) // 2}", n0 + 8 + (c - 18) // 2, s)
                    if 17 <= c < 22:
                        o_rows(c - 17)
                        if c < 21:
                            decay_start(c - 16)
                        if c < 20:
                            decays(c - 15)
                    if c == 22:
                        act.wait_ge(*free_d.at("head", "SU41", s))
                        act.dma_start(gla_prompt[0, bass.ds(s, 1)].rearrange("o (j p) v -> p (o j) v", p=P), state[:]).then_inc(s_gout, 16)
                        act.wait_ge(s_so, 8 * s + 8)
                        for v in range(4):
                            last = act.activation((gq, gk)[v // 2][:, v % 2, 0:TP], og[:, v, 0:TP], ACT.Square)
                        last.then_inc(s_gsq, 1)
                act.wait_ge(*free_d.at("head", "SO", s))
                for v in range(4):
                    last = act.activation((gq, gk)[v // 2][:, v % 2, TP:T], og[:, v, TP:T], ACT.Square)
                last.then_inc(s_gsq, 1)
                sigmoid("head", "g3", n0 + 11, s)
                r = ek[:].rearrange("p j t -> p (j t)")[:, 0:T]
                for a, (lo_t, hi_t) in enumerate(SS_COLS):
                    act.wait_ge(*full.at("head", f"SS{a}", s))
                    act.activation(r[:, lo_t:hi_t], bank_of("head", f"SS{a}")[:, 0:hi_t - lo_t], ACT.Ln, scale=1.0 / GV, bias=eps).then_inc(s_fa, 1)
                act.wait_ge(*free_a.at("head", "SS2", s))
                act.activation(r, r, ACT.Exp, scale=-0.5).then_inc(ro_ready.sem, 1)

            with act.Fori(0, GH) as s:
                chain.enter(s, HEAD_LINKS_ACT)
                head(s)
                chain.leave(GH)
            act.wait_ge(s_gout, 16 * GH + 1)
            act.wait_ge(s_sout[0], 64 * GH + 1)
            act.wait_ge(s_sout[1], 64 * GH + 1)
            mix_hi(1)
            fetch_h(1)
            out_stage(3, N_OUT1, False)
            finish_rms(3)
            for i in RESULT_ACT:
                w = P if i % 5 < TT else TB
                act.wait_ge(s_fT, i + 1)
                if i >= 15:
                    act.wait_ge(s_yout[1], 16 * 6)
                act.copy(y_buffer(i)[0:w], banks[i % 8].rearrange("p (k e) -> p k e", k=4)[0:w]).then_inc(s_fa2, 1)

        @block.tensor
        def _(pe):
            def matmul(out, lhsT, rhs, start=True, stop=True):
                return pe.matmul(out, lhsT, rhs, start=start, stop=stop, skip_group_check=True)

            def transpose(out, x):
                return pe.transpose(out, x, ident[0:x.shape[0], 0:x.shape[0]])

            def chunk(n, par, kc, stage):
                if kc == 0:
                    pe.wait_ge(s_evac, n + 1)
                pe.wait_ge(s_lo, 2 * n + kc + 3)
                for s_part, (start, step) in zip((s_x, s_xp), X_LO[stage]):
                    if step:
                        pe.wait_ge(s_part, start + step * (kc + 1))
                slot = 2 * par + kc
                for a in range(2):
                    for k in range(HC):
                        x = slice(a * TH, (a + 1) * TH)
                        kt = kc * HC + k
                        out = proj[par][:, a, 0:TH]
                        matmul(out, wlo[:, slot, k, :], xhi[:, kt, x], start=kt == 0, stop=False)
                        matmul(out, whi[:, slot, k, :], xlo[:, kt, x], start=False, stop=False)
                        last = matmul(out, whi[:, slot, k, :], xhi[:, kt, x], start=False, stop=kt == KT - 1)
                if kc == 1:
                    last.then_inc(s_tile, 1)

            def sum_squares(r):
                pe.wait_ge(s_acc, KT * r)
                for a in range(2):
                    last = matmul(score2[:, a, 0:TH], ones, acc[:, a * TH:(a + 1) * TH])
                last.then_inc(s_ss, 1)

            pe.wait_ge(s_const, 16)
            for i in range(20):
                tt, kq = TILE_ORDER[i // 4], i % 4
                w = P if tt < TT else TB
                if kq == 0:
                    pe.wait_ge(s_xin[tt], 32 if tt in (0, 4) else 16)
                if i == 7:
                    pe.wait_ge(s_rows, 16 * 8)
                    transpose(banks[7][:, 0:85], rows[:, :]).then_inc(s_v, 1)
                    pe.wait_ge(s_cols, 1)
                if i >= 8:
                    pe.wait_ge((s_xd, s_xa)[i % 2], (i - 8) // 2 + 1)
                for k in range(4):
                    last = transpose(banks[i % 8][:, k * P:k * P + w], xin[tt][0:w, (4 * kq + k) * P:(4 * kq + k + 1) * P])
                last.then_inc(s_xt, 1)
            pe.wait_ge(s_diag, 1)
            pe.wait_ge(s_xd, 9)
            pe.wait_ge(s_xa, 9)
            for a in range(2):
                last = matmul(score2[:, a, 0:TH], ones, tz[:, a, :])
            last.then_inc(s_ss, 1)

            def pair(g):
                n0 = 12 * g

                def job(name):
                    k = PAIR_JOBS.index(name)
                    prev = PAIR_JOBS[k - 2]
                    if k < 2:
                        pe.wait_ge(*freed_back("pair", prev, g))
                    else:
                        pe.wait_ge(*freed("pair", prev, g))
                    return scratch[k % 2]

                def done(last):
                    last.then_inc(s_full, 1)

                def run(op):
                    kind, x = op[:2], op[-1]
                    hb = "AB".find(x)
                    if op[0] == "S" and op[1] in "01234":
                        t = int(op[1])
                        pe.wait_ge(*exp_done.before("pair", f"{t}{x}", g))
                        pe.wait_ge(*rope_ready.at("pair", "k" + x, g))
                        if t < TT:
                            n = (t + 1) * P
                            for m in range(2):
                                d = slice(64 * m, 64 * m + 64)
                                matmul(score2[:, m, 0:n], qT[hb][d, t * P:(t + 1) * P], kT[hb][d, 0:n], stop=False)
                                last = matmul(score2[:, m, n - P:n], ident, causal, start=False)
                        else:
                            pe.wait_ge(s_qblk, 2 * g + hb + 1)
                            r = 2 * TAIL
                            matmul(score[0:r, 0:TT * P], qblk[:], kT[hb][:, 0:TT * P])
                            matmul(score[0:r, TT * P:TP], qblk[:], kT[hb][:, TT * P:TP], stop=False)
                            last = matmul(score[0:r, TT * P:TP], ident[0:r, 0:r], tmask[0:r, :], start=False)
                        last.then_inc(score_ready.sem, 1)
                        return
                    out = job(op)
                    if kind in ("RQ", "RK"):
                        a = int(op[2])
                        pe.wait_ge(s_evac, n0 + 2 * hb + (kind == "RK") + 3)
                        done(matmul(out[:, 0:TH], rot, tz[:, a, :]))
                    elif kind == "KT":
                        if op[2] == "0":
                            pe.wait_ge(*rope_ready.at("pair", "k" + x, g))
                            for t in range(TT):
                                last = transpose(out[:, t * P:(t + 1) * P], kT[hb][:, t * P:(t + 1) * P])
                        else:
                            transpose(out[0:TB, 0:P], qT[hb][:, TT * P:T])
                            last = transpose(out[0:TB, P:2 * P], kT[hb][:, TT * P:T])
                        done(last)
                    elif kind == "VT":
                        pe.wait_ge(s_evac, n0 + 4 + 2 * hb + 3)
                        if op[2] == "0":
                            for t in range(TT):
                                last = transpose(out[:, t * P:(t + 1) * P], tzf[:, t * P:(t + 1) * P])
                        else:
                            last = transpose(out[0:TB, 0:P], tzf[:, TT * P:T])
                        done(last)
                    elif kind == "PT":
                        t = int(op[2])
                        pe.wait_ge(*pd_ready.at("pair", f"{t}{x}", g))
                        if t < TT:
                            for k in range(t + 1):
                                last = transpose(out[:, k * P:(k + 1) * P], pd[:, k * P:(k + 1) * P])
                        else:
                            for k in range(TT + 1):
                                m = P if k < TT else TAIL
                                last = matmul(out[0:m, k * TAIL:(k + 1) * TAIL], probw[0:2 * TAIL, k * P:k * P + m], tsel[0:2 * TAIL, :])
                        done(last)
                    elif op[0] == "O":
                        t = int(op[1])
                        w = P if t < TT else TAIL
                        pe.wait_ge(*free_d.at("pair", f"PT{t}{x}", g))
                        pe.wait_ge(*free_a.at("pair", f"VT1{x}", g))
                        for k in range(t + 1):
                            m = P if k < TT else TAIL
                            last = matmul(out[:, 0:w], vtok[hb][0:m, k, :], pdT[(5 * hb + t) % 2][0:m, k * w:(k + 1) * w],
                                          start=k == 0, stop=k == t)
                        done(last)
                    elif kind == "SS":
                        a, half = int(op[2]), TP // 2
                        pe.wait_ge(*osq_ready.at("pair", x, g))
                        done(matmul(out[:, 0:half], ones, pd[:, a * half:(a + 1) * half]))
                    elif op == "SG":
                        pe.wait_ge(s_sg, g * 16 + 16)
                        r = NB * CTX
                        for j in range(2):
                            last = transpose(out[:, j * r:(j + 1) * r], spool[:, j * P:(j + 1) * P])
                        done(last)
                    elif op == "UT":
                        pe.wait_ge(s_evac, n0 + 9 + 3)
                        for j in range(2):
                            last = transpose(out[0:TB, j * P:(j + 1) * P], ub[:, j, META + TT * P:META + T])
                        done(last)
                    elif op == "ST":
                        pe.wait_ge(s_kred, 8 * g + 8)
                        for k in range(NPG):
                            last = transpose(out[0:4 * NB, k * P:(k + 1) * P], sall[:, k, :])
                        done(last)
                    elif op == "SD":
                        pe.wait_ge(*pd_ready.at("pair", "s", g))
                        for k in range(NPG):
                            matmul(out[:, 16 * k:16 * k + 16], sprob[:, k * P:(k + 1) * P], ssel[0:4 * NB, :])
                        done(matmul(out[:, 64:80], ones[0:4 * NB, :], enew[:]))
                    elif kind == "PO":
                        j, a = int(op[2]), int(op[3])
                        pe.wait_ge(s_d, g + 1)
                        pe.wait_ge(s_pw, g * 16 + 16)
                        for k in range(2):
                            last = matmul(out[:, 0:TH], pw[:, k, j * P:(j + 1) * P], ub[:, k, META + a * TH:META + (a + 1) * TH],
                                          start=k == 0, stop=k == 1)
                        done(last)
                    elif op[0] == "V":
                        if op == "V0":
                            pe.wait_ge(*free_d.at("pair", "SD", g))
                        for b in (2 * int(op[1]), 2 * int(op[1]) + 1):
                            pe.wait_ge(s_kv[b % 2], 512 * g + 256 + 64 * (b // 2 + 1))
                            for j in range(2):
                                for k in range(NPG):
                                    c = 2 * b + j
                                    last = matmul(out[:, c:c + 1], kv[b % 2][:, k, j * P:(j + 1) * P], pds[:, 16 * k + c:16 * k + c + 1],
                                                  start=k == 0, stop=k == NPG - 1)
                        done(last)
                    elif op == "SN":
                        pe.wait_ge(*osq_ready.at("pair", "s", g))
                        done(matmul(out[:, 0:16], ones, small2[:, 0:16]))
                    else:
                        raise ValueError(op)

                for s in range(24):
                    chunk(n0 + s // 2, (s // 2) % 2, s % 2, "in0")
                    for op in PAIR_PLAN.get(s, "").split():
                        run(op)

            pe.wait_ge(s_c0, 96)
            with pe.Fori(0, PAIRS) as g:
                pair(g)

            def out_proj(n0, stage):
                with pe.Fori(0, KT // 2) as i:
                    for par in range(2):
                        for kc in range(2):
                            chunk(2 * i + (n0 + par), (n0 + par) % 2, kc, stage)

            out_proj(N_OUT0, "out0")
            sum_squares(1)
            pe.wait_ge(s_rstd, 2)
            pe.wait_ge(s_evac, N_LR + 1)
            pe.wait_ge(s_lo, 2 * N_LR + 4)
            for k in range(KT):
                pe.wait_ge(s_sq, KT + k + 1)
                for a in range(2):
                    last = matmul(score2[:, a, 0:TH], ones, (tz, te)[k % 2][:, a, :], start=k == 0, stop=k == KT - 1)
                last.then_inc(s_acc, 1)
                pe.wait_ge(s_x, X_LO["in1"][0][0] + k + 1)
                for a in range(2):
                    w, x = (k // HC, k % HC), slice(a * TH, (a + 1) * TH)
                    out = proj[0][:, a, 0:TH]
                    matmul(out, wlo[:, w[0], w[1], :], xhi[:, k, x], start=k == 0, stop=False)
                    matmul(out, whi[:, w[0], w[1], :], xlo[:, k, x], start=False, stop=False)
                    last = matmul(out, whi[:, w[0], w[1], :], xhi[:, k, x], start=False, stop=k == KT - 1)
            last.then_inc(s_tile, 1)
            pe.wait_ge(s_acc, 2 * KT)
            pe.sem_inc(s_ss, 1)

            def head(s):
                n0 = N_HEAD + 12 * s

                def job(name):
                    k = HEAD_JOBS.index(name)
                    prev = HEAD_JOBS[k - 2]
                    if k < 2:
                        pe.wait_ge(*freed_back("head", prev, s))
                    else:
                        pe.wait_ge(*freed("head", prev, s))
                    return scratch[k % 2]

                def done(last):
                    last.then_inc(s_full, 1)

                def run(op):
                    kind = op[:2]
                    if op[0] == "B":
                        b = int(op[1])
                        pe.wait_ge(s_snew, 8 * s + b + 1)
                        for j in range(2):
                            last = matmul(score[0:NB, 0:GV], qd[:, j, b * NB:(b + 1) * NB], sst[b % 2][:, j, :], start=b + j == 0, stop=b + j == NB)
                        last.then_inc(s_so, 1)
                        return
                    out = job(op)
                    if op[0] == "G":
                        j, a = int(op[1]), int(op[2])
                        pe.wait_ge(s_lr, 1)
                        pe.wait_ge(s_wa2, s * 16 + 16)
                        done(matmul(out[:, 0:TH], wa2[:, j * P:(j + 1) * P], lrT[:, a * TH:(a + 1) * TH]))
                    elif kind == "VT":
                        j = int(op[3])
                        pe.wait_ge(s_evac, n0 + j + 3)
                        if op[2] == "0":
                            for t in range(TT):
                                last = transpose(out[:, t * P:(t + 1) * P], tzf[:, t * P:(t + 1) * P])
                        else:
                            last = transpose(out[0:TB, 0:P], tzf[:, TT * P:T])
                        done(last)
                    elif kind == "SK":
                        c = int(op[2])
                        pe.wait_ge(*fac_ready.at("head", str(c), s))
                        for i in range(4 if c < TT else 1):
                            m, w = (SUB * (i + 1), SUB) if c < TT else (TAIL, TAIL)
                            for j in range(2):
                                matmul(out[0:m, SUB * i:SUB * i + w], ek[:, j, KOFF[i]:KOFF[i] + m], eq[:, j, SUB * i:SUB * i + w],
                                       start=j == 0, stop=j == 1)
                        w = P if c < TT else TAIL
                        for j in range(2):
                            last = transpose(out[0:w, P * (j + 1):P * (j + 2)], el[:, j, 0:w])
                        done(last)
                    elif kind == "OC":
                        c = int(op[2])
                        w = P if c < TT else TAIL
                        pe.wait_ge(*free_d.at("head", f"SK{c}", s))
                        pe.wait_ge(*free_a.at("head", "VT13", s))
                        if c:
                            pe.wait_ge(*ed_ready.at("head", str(c), s))
                            pe.wait_ge(*free_d.at("head", f"SU{c - 1}1", s))
                        for v in range(4):
                            o, vc = out[:, v * w:(v + 1) * w], slice(v * P, (v + 1) * P)
                            if c:
                                for j in range(2):
                                    matmul(o, state[:, j, vc], ed[:, j, 0:w], start=j == 0, stop=False)
                            last = matmul(o, gv[0:w, c, vc], st[0:w, 0:w], start=c == 0, stop=True)
                        done(last)
                    elif kind == "SU":
                        c, j = int(op[2]), int(op[3])
                        w = P if c < TT else TAIL
                        done(matmul(out[:, 0:GV], kd[0:w, j * P:(j + 1) * P], gv[0:w, c, :]))
                    elif op == "SO":
                        pe.wait_ge(s_srow, s + 1)
                        for v in range(4):
                            last = matmul(out[:, v * NB:(v + 1) * NB], srow[:, v * P:(v + 1) * P], ident[0:NB, 0:NB])
                        done(last)
                    elif kind == "SS":
                        lo_t, hi_t = SS_COLS[int(op[2])]
                        pe.wait_ge(s_gsq, 2 * s + (2 if op == "SS2" else 1))
                        for v in range(4):
                            last = matmul(out[:, 0:hi_t - lo_t], ones, (gq, gk)[v // 2][:, v % 2, lo_t:hi_t], start=v == 0, stop=v == 3)
                        done(last)
                    else:
                        raise ValueError(op)

                for c in range(24):
                    chunk(n0 + c // 2, (1 + c // 2) % 2, c % 2, "in1")
                    for op in HEAD_PLAN.get(c, "").split():
                        run(op)

            with pe.Fori(0, GH) as s:
                head(s)
            out_proj(N_OUT1, "out1")
            sum_squares(3)
            for i in range(20):
                kq, tt = i // 5, i % 5
                w = P if tt < TT else TB
                if tt == 0:
                    for k in range(4 * kq, 4 * kq + 4):
                        pe.wait_ge(*residual_added(k))
                if i == 0:
                    pe.wait_ge(s_rstd, 4)
                if i >= 8:
                    pe.wait_ge(*result_read(i - 8))
                for k in range(4):
                    last = transpose(banks[i % 8][0:w, k * P:(k + 1) * P], mix[:, 4 * kq + k, tt * P:tt * P + w])
                last.then_inc(s_fT, 1)

        @block.vector
        def _(dve):
            chain = Chain(s_vc, dve)
            link = chain.link

            def evac(n, par, dst, scale=None):
                dve.wait_ge(s_tile, n + 3)
                src = proj[par][:, :, 0:TH]
                if scale is None:
                    dve.tensor_tensor(dst, src, rstd[:], ALU.mult).then_inc(s_evac, 1)
                else:
                    dve.scalar_tensor_tensor(out=dst, in0=src, scalar=scale, in1=rstd[:], op0=ALU.mult, op1=ALU.mult).then_inc(s_evac, 1)
                dve.wait_ge(s_evac, n + 3)

            def lows(stage, scale_col=None):
                for k in range(0, KT, 2 if scale_col is None else 1):
                    dve.wait_ge(s_xhi, X_HI[stage] + k + 1)
                    if scale_col is None:
                        dve.tensor_tensor(xlo[:, k, :], mix[:, k, :], xhi[:, k, :].bitcast(F32), ALU.subtract).then_inc(s_x, 1)
                    else:
                        dve.scalar_tensor_tensor(out=xlo[:, k, :], in0=mix[:, k, :], scalar=cols[:, scale_col + k:scale_col + k + 1],
                                                 in1=xhi[:, k, :].bitcast(F32), op0=ALU.mult, op1=ALU.subtract).then_inc(s_x, 1)

            dve.sem_inc(s_evac, 2)
            dve.sem_inc(s_fd, 2)
            dve.memset(stat[:, 1:], 1.0)
            link(dve.memset(stat[:, 0:1], EPS))
            dve.sem_inc(s_init, 1)
            for i in range(0, 20, 2):
                tt, kq = TILE_ORDER[i // 4], i % 4
                w = P if tt < TT else TB
                dve.wait_ge(s_xt, i + 1)
                dve.tensor_copy(mix[:, 4 * kq:4 * kq + 4, tt * P:tt * P + w],
                                banks[i % 8].rearrange("p (k t) -> p k t", k=4)[:, :, 0:w]).then_inc(s_xd, 1)
                if i == 4:
                    dve.wait_ge(s_v, 1)
                    link(dve.tensor_copy(cols[:, 0:85], banks[7][:, 0:85]))
                    dve.tensor_scalar(cols[:, SUBG8:SUBG8 + 1], cols[:, SUBG:SUBG + 1], 1.0 - LAM_INIT, None, ALU.mult).then_inc(s_cols, 1)
                    dve.wait_ge(s_cols, 1)
            dve.wait_ge(s_tok, 6)
            for tt in range(TT + 1):
                w = P if tt < TT else TB
                last = dve.tensor_scalar(tzf[:, tt * P:tt * P + w], ident[:, 0:w], stat[:, 8 + tt:9 + tt], None, ALU.mult)
            last.then_inc(s_diag, 1)
            dve.wait_ge(s_ss, 1)
            dve.tensor_copy(rstd[:], score2[:, :, 0:TH]).then_inc(s_rstd, 1)
            lows("in0", PRE0)
            dve.wait_ge(s_c0, 96)
            link(dve.tensor_tensor(lam4[:, 0:3:2, :], lam4[:, 0:3:2, :], lam4[:, 1:4:2, :], ALU.mult))
            dve.tensor_reduce(lam[:, 4:6], lam4[:, 0:3:2, :], AX.X, ALU.add).then_inc(s_lam, 1)
            dve.memset(qblk[:], 0.0)
            dve.memset(ub[:, :, 0:META], 0.0)
            dve.wait_ge(s_lam, 2)
            link(dve.tensor_tensor(lam[:, 0:1], lam[:, 6:7], lam[:, 7:8], ALU.subtract))
            link(dve.tensor_scalar(lam[:, 1:2], lam[:, 0:1], LAM_INIT, -1.0, ALU.add, ALU.mult))
            dve.scalar_tensor_tensor(out=lam[:, 2:3], in0=tmap[:, 1:2], scalar=lam[:, 1:2], in1=tmap[:, 0:1], op0=ALU.mult, op1=ALU.add)
            dve.scalar_tensor_tensor(out=lam[:, 3:4], in0=smap[:, 1:2], scalar=lam[:, 1:2], in1=smap[:, 0:1], op0=ALU.mult, op1=ALU.add)
            link(dve.memset(lam[:, 0:1], 1.0))
            dve.wait_ge(s_rstd, 1)

            def pair(g):
                n0 = 12 * g
                os = small[:, 32:48]

                def gate(name, dst):
                    dve.wait_ge(*sigmoid_ready.at("pair", name, g))
                    link(dve.tensor_tensor(dst, tzf, tef, ALU.mult))

                def rope_start(n, dst):
                    evac(n, n % 2, tz[:])
                    link(dve.tensor_tensor(dst[:], tzf, cos, ALU.mult))

                def rope_end(op, x, dst):
                    for a in range(2):
                        c = slice(a * TH, (a + 1) * TH)
                        dve.wait_ge(*full.at("pair", f"{op}{a}{x}", g))
                        dve.tensor_tensor(te[:, a, :], bank_of("pair", f"{op}{a}{x}")[:, 0:TH], sin[:, c], ALU.mult).then_inc(s_fd, 1)
                        dve.wait_ge(*free_d.at("pair", f"{op}{a}{x}", g))
                        last = dve.tensor_tensor(dst[:, c], dst[:, c], te[:, a, :], ALU.add)
                    last.then_inc(rope_ready.sem, 1)

                def tail_queries(hb):
                    dve.wait_ge(*rope_ready.at("pair", "q" + "AB"[hb], g))
                    dve.tensor_copy(qblk[0:64, 0:TAIL], qT[hb][0:64, TT * P:TP])
                    dve.tensor_copy(qblk[64:P, TAIL:2 * TAIL], qT[hb][64:P, TT * P:TP]).then_inc(s_qblk, 1)

                def maxima(t, hb):
                    dve.wait_ge(*score_ready.at("pair", f"{t}{'AB'[hb]}", g))
                    if t < TT:
                        link(dve.tensor_reduce(small[:, 0:2], score2[:, :, 0:(t + 1) * P], AX.X, ALU.max))
                        dve.tensor_scalar(small[:, 2:4], small[:, 0:2], -SCALE, None, ALU.mult).then_inc(max_ready.sem, 1)
                    else:
                        r = 2 * TAIL
                        link(dve.tensor_reduce(small[0:r, 0:1], score[0:r, 0:TP], AX.X, ALU.max))
                        dve.tensor_scalar(small[0:r, 2:3], small[0:r, 0:1], -SCALE, None, ALU.mult).then_inc(max_ready.sem, 1)

                def combine(t, hb):
                    dve.wait_ge(*exp_done.at("pair", f"{t}{'AB'[hb]}", g))
                    if t < TT:
                        n = (t + 1) * P
                        link(dve.reciprocal(small[:, 6:8], small[:, 4:6]))
                        link(dve.tensor_tensor(small[:, 8:10], small[:, 6:8], lam[:, 0:2], ALU.mult))
                        link(dve.tensor_scalar(prob[:, 0, 0:n], prob[:, 0, 0:n], small[:, 8:9], None, ALU.mult))
                        dve.scalar_tensor_tensor(out=pd[:, 0:n], in0=prob[:, 1, 0:n], scalar=small[:, 9:10], in1=prob[:, 0, 0:n],
                                                 op0=ALU.mult, op1=ALU.add).then_inc(pd_ready.sem, 1)
                    else:
                        r = 2 * TAIL
                        link(dve.reciprocal(small[0:r, 6:7], small[0:r, 4:5]))
                        link(dve.tensor_tensor(small[0:r, 8:9], small[0:r, 6:7], lam[0:r, 2:3], ALU.mult))
                        dve.tensor_scalar(probw[0:r, 0:TP], probw[0:r, 0:TP], small[0:r, 8:9], None, ALU.mult).then_inc(pd_ready.sem, 1)

                def probs_out(t, hb):
                    x, buf = "AB"[hb], pdT[(5 * hb + t) % 2]
                    dve.wait_ge(*full.at("pair", f"PT{t}{x}", g))
                    src = bank_of("pair", f"PT{t}{x}")
                    if t < TT:
                        dve.tensor_copy(buf[:, 0:(t + 1) * P], src[:, 0:(t + 1) * P]).then_inc(s_fd, 1)
                    else:
                        dve.tensor_copy(buf[:, 0:TT * TAIL], src[:, 0:TT * TAIL])
                        dve.tensor_copy(buf[0:TAIL, TT * TAIL:(TT + 1) * TAIL], src[0:TAIL, TT * TAIL:(TT + 1) * TAIL]).then_inc(s_fd, 1)

                def output(t, hb):
                    x, w = "AB"[hb], P if t < TT else TAIL
                    dve.wait_ge(*full.at("pair", f"O{t}{x}", g))
                    dve.tensor_copy(oT[:, t * P:t * P + w], bank_of("pair", f"O{t}{x}")[:, 0:w]).then_inc(s_fd, 1)

                def mix_head(hb):
                    dve.wait_ge(*ro_ready.at("pair", "AB"[hb], g))
                    dve.wait_ge(*free_d.at("pair", f"O{TT}{'AB'[hb]}", g))
                    link(dve.scalar_tensor_tensor(out=oT[:, 0:TP], in0=oT[:, 0:TP], scalar=cols[:, SUBG8:SUBG8 + 1], in1=pd[:, 0:TP],
                                                  op0=ALU.mult, op1=ALU.mult))
                    m = mix[:, HC + 2 * g + hb, 0:TP]
                    link(dve.tensor_tensor(m, m, oT[:, 0:TP], ALU.mult))

                def key_sums(b):
                    dve.wait_ge(s_prod, 8 * g + b + 1)
                    dve.tensor_reduce(sall[:, :, 4 * b:4 * b + 4], kv[b % 2][:].rearrange("p k (m d) -> p k m d", d=64),
                                      AX.X, ALU.add).then_inc(s_kred, 1)

                def own_key_scores():
                    dve.wait_ge(*free_a.at("pair", "KT1B", g))
                    link(dve.tensor_tensor(tef[0:TB, 0:2 * P], qk_tok[0:TB, 0].rearrange("p h e -> p (h e)"),
                                           qk_tok[0:TB, 1].rearrange("p h e -> p (h e)"), ALU.mult))
                    dve.tensor_reduce(small2[0:TB, 0:4], tef[0:TB, 0:2 * P].rearrange("p (m d) -> p m d", d=64), AX.X, ALU.add).then_inc(s_snr, 1)

                def pooled_rows():
                    w = 2 << g
                    dve.wait_ge(*full.at("pair", "SG", g))
                    src = bank_of("pair", "SG")[:, 0:2 * NB * CTX].rearrange("p (b r) -> p b r", r=CTX)
                    dve.tensor_reduce(small[:, 16:32], src[:, :, CTX - (w - 1):CTX], AX.X, ALU.add).then_inc(s_fd, 1)

                def window_means():
                    w = 2 << g
                    dve.wait_ge(*full.at("pair", "UT", g))
                    for j in range(2):
                        u = ub[:, j, 0:META + TP]
                        src, x = u, 1
                        for step in range(g + 1):
                            dst = win[step % 2]
                            link(dve.tensor_tensor(dst[:, 16:], src[:, 16:], src[:, 16 - x:META + TP - x], ALU.add))
                            if step < g:
                                link(dve.memset(dst[:, 0:16], 0.0))
                            src, x = dst, 2 * x
                        link(dve.tensor_tensor(small2[:, 16:32], src[:, 16:32], counts[:, g, :], ALU.mult))
                        link(dve.tensor_tensor(small2[:, 16:32], small2[:, 16:32], u[:, 16:32], ALU.subtract))
                        link(dve.scalar_tensor_tensor(out=u[:, 32:], in0=src[:, 32:], scalar=1.0 / w, in1=u[:, 32:], op0=ALU.mult, op1=ALU.subtract))
                        dve.tensor_copy(u[:, 16:32], small2[:, 16:32])
                        us, t8 = ub[:, j, META + TP:META + T], small[:, 16 + 8 * j:24 + 8 * j]
                        link(dve.tensor_tensor(t8, t8, us, ALU.add))
                        last = dve.scalar_tensor_tensor(out=us, in0=t8, scalar=1.0 / w, in1=us, op0=ALU.mult, op1=ALU.subtract)
                        if j == 0:
                            link(last)
                    last.then_inc(s_d, 1)

                def sample_scores():
                    dve.wait_ge(*full.at("pair", "ST", g))
                    dve.tensor_copy(sprob[:], bank_of("pair", "ST")[0:4 * NB, :]).then_inc(s_fd, 1)

                def sample_softmax():
                    dve.wait_ge(*free_d.at("pair", "ST", g))
                    link(dve.tensor_reduce(small2[0:32, 32:33], sprob[:], AX.X, ALU.max))
                    dve.wait_ge(s_sn, g * 16 + 16)
                    link(dve.tensor_tensor(small2[0:32, 33:34], small2[0:32, 32:33], small2[0:32, 40:41], ALU.max))
                    dve.tensor_scalar(small2[0:32, 34:35], small2[0:32, 33:34], -SCALE, None, ALU.mult).then_inc(max_ready.sem, 1)
                    dve.wait_ge(*exp_done.at("pair", "s", g))
                    link(dve.tensor_tensor(small2[0:32, 37:38], small2[0:32, 35:36], small2[0:32, 36:37], ALU.add))
                    link(dve.reciprocal(small2[0:32, 37:38], small2[0:32, 37:38]))
                    link(dve.tensor_tensor(small2[0:32, 38:39], small2[0:32, 37:38], lam[0:32, 3:4], ALU.mult))
                    link(dve.tensor_tensor(small2[0:32, 39:40], small2[0:32, 38:39], small2[0:32, 36:37], ALU.mult))
                    dve.tensor_scalar(sprob[:], sprob[:], small2[0:32, 38:39], None, ALU.mult)
                    dve.tensor_scalar(enew[:], ssel[0:32, :], small2[0:32, 39:40], None, ALU.mult).then_inc(pd_ready.sem, 1)

                def sample_probs():
                    dve.wait_ge(*full.at("pair", "SD", g))
                    dve.tensor_copy(pds[:], bank_of("pair", "SD")[:, 0:80]).then_inc(s_fd, 1)
                    dve.wait_ge(*free_d.at("pair", "SD", g))
                    link(dve.tensor_tensor(os.rearrange("p (b h) -> p b h", h=2), pds[:, 64:80].rearrange("p (b h) -> p b h", h=2),
                                           vs[:].rearrange("p h b -> p b h"), ALU.mult))

                def sample_values(i):
                    c = slice(4 * i, 4 * i + 4)
                    dve.wait_ge(*full.at("pair", f"V{i}", g))
                    dve.tensor_tensor(os[:, c], os[:, c], bank_of("pair", f"V{i}")[:, c], ALU.add).then_inc(s_fd, 1)
                    dve.wait_ge(*free_d.at("pair", f"V{i}", g))

                def pooled_out(j):
                    k = 2 * g + j
                    for a in range(2):
                        dve.wait_ge(*full.at("pair", f"PO{j}{a}", g))
                        m = mix[:, k, a * TH:(a + 1) * TH]
                        dve.scalar_tensor_tensor(out=m, in0=bank_of("pair", f"PO{j}{a}")[:, 0:TH], scalar=cols[:, PSC + k:PSC + k + 1],
                                                 in1=m, op0=ALU.mult, op1=ALU.mult).then_inc(s_fd, 1)

                def sample_mix():
                    dve.wait_ge(*ro_ready.at("pair", "s", g))
                    link(dve.scalar_tensor_tensor(out=os, in0=os, scalar=cols[:, SUBG8:SUBG8 + 1], in1=small2[:, 16:32], op0=ALU.mult, op1=ALU.mult))
                    m = mix[:, HC + 2 * g:HC + 2 * g + 2, TP:T]
                    link(dve.tensor_tensor(m, m, os.rearrange("p (b h) -> p h b", h=2), ALU.mult))

                for s in range(24):
                    if s in (1, 3, 5, 7):
                        rope_start(n0 + s // 2, (qT, kT)[s // 2 % 2][s // 4])
                    if s in (2, 4, 6, 8):
                        i = s // 2 - 1
                        rope_end(("RQ", "RK")[i % 2], "AB"[i // 2], (qT, kT)[i % 2][i // 2])
                    if s == 9:
                        evac(n0 + 4, 0, tz[:])
                        link(dve.tensor_copy(vs[:, 0, :], tzf[:, TP:T]))
                    if s == 11:
                        dve.wait_ge(*full.at("pair", "VT1A", g))
                        evac(n0 + 5, 1, tz[:])
                    if s == 12:
                        dve.wait_ge(s_hst, 16)
                        gate("gA", mix[:, HC + 2 * g, :])
                    if s == 13:
                        evac(n0 + 6, 0, tz[:])
                        link(dve.tensor_copy(vs[:, 1, :], tzf[:, TP:T]))
                    if s == 15:
                        dve.wait_ge(*full.at("pair", "VT1B", g))
                        evac(n0 + 7, 1, tz[:])
                        mix_head(0)
                    if s in (17, 19):
                        evac(n0 + 8 + (s - 17) // 2, (s - 17) // 2, ub[:, (s - 17) // 2, META:].rearrange("p (a t) -> p a t", a=2))
                    if s in (21, 23):
                        evac(n0 + 10 + (s - 21) // 2, (s - 21) // 2, tz[:])
                    for hb, s0 in ((0, 8), (1, 16)):
                        t = s - s0
                        if 1 <= t <= 5: probs_out(t - 1, hb)
                        if 2 <= t <= 6: output(t - 2, hb)
                        if t == 3: tail_queries(hb)
                        if 0 <= t <= 4:
                            maxima(t, hb)
                            combine(t, hb)
                    if s == 10: own_key_scores()
                    if s == 16:
                        pooled_rows()
                        gate("gB", mix[:, HC + 2 * g + 1, :])
                    for b in KEY_SUM.get(s, ()):
                        key_sums(b)
                    if s == 17:
                        sample_scores()
                        sample_softmax()
                    if s == 18: sample_probs()
                    if 19 <= s < 23: sample_values(s - 19)
                    if s == 21: window_means()
                    if s == 22:
                        gate("p0", mix[:, 2 * g, :])
                        pooled_out(0)
                    if s == 23:
                        sample_mix()
                        mix_head(1)
                        gate("p1", mix[:, 2 * g + 1, :])
                        pooled_out(1)

            for g in range(PAIRS):
                pair(g)
            dve.wait_ge(*free_d.at("pair", "PO11", PAIRS - 1))
            dve.sem_inc(s_mix, 1)
            lows("out0")

            def out_stage(r, n0, post):
                with dve.Fori(0, KT // 2) as i:
                    for par in range(2):
                        k = 2 * i + par
                        dst = tile_at(mix, k).rearrange("p (a t) -> p a t", a=2)
                        gain = cols[:, bass.ds(2 * i + (post + par), 1)]
                        dve.wait_ge(s_sq, 2 * i + ((r - 1) * KT + par + 1))
                        dve.tensor_scalar(dst, proj[(n0 + par) % 2][:, :, 0:TH], gain, None, ALU.mult).then_inc(s_evac, 1)
                dve.wait_ge(s_evac, n0 + KT + 2)

            def add_residual(k):
                dve.tensor_tensor(mix[:, k, :], mix[:, k, :], rstdf, ALU.mult).then_inc(s_yt, 1)

            out_stage(1, N_OUT0, POST0)
            dve.wait_ge(s_rstd, 2)

            def lows_1(k):
                dve.wait_ge(s_xhi, X_HI["in1"] + k + 1)
                dve.scalar_tensor_tensor(out=xlo[:, k, :], in0=mix[:, k, :], scalar=cols[:, PRE1 + k:PRE1 + k + 1],
                                         in1=xhi[:, k, :].bitcast(F32), op0=ALU.mult, op1=ALU.subtract).then_inc(s_x, 1)

            for k in range(KT):
                add_residual(k)
                if k >= 2:
                    lows_1(k - 2)
            lows_1(KT - 2)
            lows_1(KT - 1)
            dve.wait_ge(s_rstd, 3)
            dve.memset(st[:], 0.0)
            link(dve.memset(qd[:], 0.0))
            dve.wait_ge(s_tile, N_LR + 3)
            dve.tensor_tensor(lrT[:].rearrange("p (a t) -> p a t", a=2), proj[0][0:RANK, :, 0:TH], rstd[0:RANK], ALU.mult).then_inc(s_evac, 1)
            dve.wait_ge(s_evac, N_LR + 3)
            dve.sem_inc(s_lr, 1)
            dve.wait_ge(s_c1, 16)
            dve.wait_ge(s_hst, 16 + 16 * KT)

            def head(s):
                n0 = N_HEAD + 12 * s

                def two(buf, j):
                    return buf[:, j, :].rearrange("p (a t) -> p a t", a=2)

                def gate(v):
                    dve.wait_ge(*sigmoid_ready.at("head", f"g{v}", s))
                    link(dve.tensor_tensor(tile_at(mix, 4 * s + v), tzf, tef, ALU.mult))

                def decay_logits(j):
                    for a in range(2):
                        dve.wait_ge(*full.at("head", f"G{j}{a}", s))
                        dve.tensor_scalar(gb[:, j, a * TH:(a + 1) * TH], bank_of("head", f"G{j}{a}")[:, 0:TH],
                                          ba_col(s, j), None, ALU.add).then_inc(s_fd, 1)
                    dve.wait_ge(*free_d.at("head", f"G{j}1", s))
                    dve.sem_inc(s_zg, 1)

                def ba_col(s, j):
                    return cols[:, bass.ds(2 * s + (BA + j), 1)]

                def running_sums(j):
                    dve.wait_ge(s_ga, 2 * s + j + 1)
                    dve.scalar_tensor_tensor(out=gb[:, j, :], in0=gb[:, j, :], scalar=0.0, in1=tef, op0=ALU.min, op1=ALU.subtract).then_inc(s_g, 1)
                    dve.wait_ge(s_g, 2 * s + j + 1)
                    for c in range(TT + 1):
                        w = P if c < TT else TAIL
                        x = gb[:, j, c * P:c * P + w]
                        last = dve.tensor_tensor_scan(x, ones[:, 0:w], x, 0.0, ALU.mult, ALU.add)
                    link(last)

                def references():
                    k = 1.0 / TAU
                    dve.tensor_scalar(refs[:, :, 0:16], gb[:, :, 15:TT * P:SUB], k, None, ALU.mult)
                    dve.tensor_scalar(refs[:, :, 16:17], gb[:, :, TT * P + 7:TT * P + 8], k, None, ALU.mult)
                    dve.tensor_scalar(lastr[:, :, 0:4], gb[:, :, P - 1:TT * P:P], k, None, ALU.mult)
                    dve.tensor_scalar(lastr[:, :, 4:5], gb[:, :, TP - 1:TP], k, None, ALU.mult).then_inc(s_refs, 1)
                    dve.wait_ge(s_refs, s + 1)

                def distances(c):
                    if c < TT:
                        x = gb[:, :, c * P:(c + 1) * P].rearrange("p j (i t) -> p j i t", t=SUB)
                        dve.tensor_tensor(eq[:].rearrange("p j (i t) -> p j i t", t=SUB), x, x[:, :, :, 15:16].to_broadcast([P, 2, 4, SUB]),
                                          ALU.subtract).then_inc(dq_ready.sem, 1)
                    else:
                        x = gb[:, :, TT * P:TP]
                        dve.tensor_tensor(eq[:, :, 0:TAIL], x, x[:, :, 7:8].to_broadcast([P, 2, TAIL]), ALU.subtract).then_inc(dq_ready.sem, 1)

                def factors(c):
                    c0, w = c * P, P if c < TT else TAIL
                    dve.wait_ge(*dec_ready.at("head", str(c), s))
                    dve.tensor_tensor(eq[:, :, 0:w], eq[:, :, 0:w], gq[:, :, c0:c0 + w], ALU.mult)
                    dve.tensor_tensor(el[:, :, 0:w], el[:, :, 0:w], gk[:, :, c0:c0 + w], ALU.mult)
                    for i in range(4 if c < TT else 1):
                        m = SUB * (i + 1) if c < TT else TAIL
                        x = ek[:, :, KOFF[i]:KOFF[i] + m]
                        last = dve.tensor_tensor(x, x, gk[:, :, c0:c0 + m], ALU.mult)
                    last.then_inc(fac_ready.sem, 1)

                def query_decay(c):
                    c0, w = c * P, P if c < TT else TAIL
                    dve.wait_ge(*ed_exp.at("head", str(c), s))
                    dve.tensor_tensor(ed[:, :, 0:w], ed[:, :, 0:w], gq[:, :, c0:c0 + w], ALU.mult).then_inc(ed_ready.sem, 1)

                def masked(c):
                    w = P if c < TT else TAIL
                    src = bank_of("head", f"SK{c}")
                    dve.wait_ge(*full.at("head", f"SK{c}", s))
                    for i in range(4 if c < TT else 1):
                        m, n = (SUB * (i + 1), SUB) if c < TT else (TAIL, TAIL)
                        x = slice(SUB * i, SUB * i + n)
                        dve.tensor_tensor(st[0:m, x], src[0:m, x], lower[0:m, x], ALU.mult)
                    dve.tensor_copy(kd[0:w, :], src[0:w, P:3 * P]).then_inc(s_fd, 1)

                def update(c):
                    for j in range(2):
                        dve.wait_ge(*full.at("head", f"SU{c}{j}", s))
                        src = bank_of("head", f"SU{c}{j}")
                        if c == 0:
                            dve.tensor_copy(state[:, j, :], src[:]).then_inc(s_fd, 1)
                        else:
                            dve.scalar_tensor_tensor(out=state[:, j, :], in0=state[:, j, :], scalar=elast[:, j, c:c + 1], in1=src[:],
                                                     op0=ALU.mult, op1=ALU.add).then_inc(s_fd, 1)

                def new_state(b):
                    i = b % 2
                    dve.wait_ge(s_sdec, 8 * s + b + 1)
                    dve.wait_ge(s_vb[i], 64 * s + 16 * (b // 2 + 1))
                    for j in range(2):
                        last = dve.scalar_tensor_tensor(out=sst[i][:, j, :], in0=vb[i][:], scalar=gk[:, j, TP + b:TP + b + 1], in1=sst[i][:, j, :],
                                                        op0=ALU.mult, op1=ALU.add)
                    last.then_inc(s_snew, 1)

                for c in range(24):
                    tile, done_tile = c // 2, c % 2 == 1
                    kind = HEAD_TILES[tile]
                    if done_tile:
                        par = (1 + tile) % 2
                        if kind[0] == "q": evac(n0 + tile, par, two(gq, int(kind[1])), 1.0 / TAU)
                        elif kind[0] == "k": evac(n0 + tile, par, two(gk, int(kind[1])))
                        else:
                            if kind in ("v1", "v2", "v3"):
                                dve.wait_ge(*full.at("head", f"VT1{int(kind[1]) - 1}", s))
                            if kind == "g0":
                                dve.wait_ge(*full.at("head", "VT13", s))
                            evac(n0 + tile, par, tz[:])
                    if c == 1: decay_logits(0)
                    if c == 2:
                        running_sums(0)
                        decay_logits(1)
                    if c == 3:
                        running_sums(1)
                        references()
                    if c == 8: distances(0)
                    if c == 16:
                        factors(0)
                        link(dve.tensor_copy(qd[:, :, 0:NB * NB:NB + 1], gq[:, :, TP:T]))
                        new_state(0)
                        new_state(1)
                        masked(0)
                        distances(1)
                        factors(1)
                    if c in (18, 20, 22):
                        new_state(c - 16)
                        new_state(c - 15)
                    if 17 <= c < 22:
                        k = c - 17
                        if k == 0:
                            dve.wait_ge(s_last, s + 1)
                            dve.wait_ge(s_gout, 16 * s + 1)
                        update(k)
                        if k < 4:
                            query_decay(k + 1)
                            masked(k + 1)
                        if k < 3:
                            distances(k + 2)
                    if 17 <= c < 20: factors(c - 15)
                    if c in (18, 20, 22): gate((c - 18) // 2)
                    if c == 23:
                        dve.wait_ge(s_so, 8 * s + 8)
                        dve.tensor_copy(srow, score[0:NB, 0:GV]).then_inc(s_srow, 1)
                        dve.wait_ge(*full.at("head", "SO", s))
                        dve.wait_ge(*free_a.at("head", "OC4", s))
                        dve.tensor_copy(og[:, :, TP:T], bank_of("head", "SO")[:, 0:4 * NB].rearrange("p (v b) -> p v b", v=4)).then_inc(s_fd, 1)
                gate(3)
                dve.wait_ge(*ro_ready.at("head", "o", s))
                r = ek[:].rearrange("p j t -> p (j t)")[:, 0:T]
                for v in range(4):
                    link(dve.scalar_tensor_tensor(out=og[:, v, :], in0=og[:, v, :], scalar=cols[:, GN + v:GN + v + 1], in1=r, op0=ALU.mult, op1=ALU.mult))
                    m = tile_at(mix, 4 * s + v)
                    last = dve.tensor_tensor(m, m, og[:, v, :], ALU.mult)
                    if v < 3:
                        link(last)
                last.then_inc(s_head, 1)
                dve.wait_ge(s_head, s + 1)

            with dve.Fori(0, GH) as s:
                chain.enter(s, HEAD_LINKS)
                head(s)
                chain.leave(GH)
            dve.sem_inc(s_mix, 1)
            lows("out1")
            out_stage(3, N_OUT1, POST1)
            dve.wait_ge(s_rstd, 4)
            for k in range(KT):
                add_residual(k)
                if k % 3 == 2:
                    dve.wait_ge(s_yt, KT + k + 1)
                    dve.wait_ge(s_hld, 32)
                    dve.tensor_tensor(mix[:, k, :], mix[:, k, :], hbuf[:, k, :], ALU.add).then_inc(s_hd, 1)
            for i in RESULT_DVE:
                w = P if i % 5 < TT else TB
                dve.wait_ge(s_fT, i + 1)
                if i >= 15:
                    dve.wait_ge(s_yout[1], 16 * 6)
                dve.tensor_copy(y_buffer(i)[0:w], banks[i % 8].rearrange("p (k e) -> p k e", k=4)[0:w]).then_inc(s_fd2, 1)


_INS = ["x_prompt", "x_sample", "cache_k", "cache_v", "state_pool", "state_gla", "page_table", "meta_tokens",
        "pre_norm_0", "post_norm_0", "w_in_0", "pool_w_0", "pool_scale_0", "lambda_q1_0", "lambda_k1_0",
        "lambda_q2_0", "lambda_k2_0", "subln_0", "w_out_0", "pre_norm_1", "post_norm_1", "w_in_1",
        "gla_wa2_1", "gla_ba_1", "gla_norm_1", "w_out_1"]
_OUTS = [(1, SEQ, D), (NB, 1, D), (1, TP, NH, P), (1, TP, NH, P), (1, CTX, 1024), (1, GH, GK, GV),
         (NB, 1, NH, P), (NB, 1, NH, P), (NB, CTX, 1024), (NB, GH, GK, GV)]


def kernel(**inputs):
    import numpy as _np
    import concourse.bacc as _bacc
    from concourse.bass_utils import run_bass_kernel_spmd as _run

    nc = _bacc.Bacc("TRN2", target_bir_lowering=False, num_devices=1)
    arrays, aps = {}, {}
    tables = constants()
    for name, a in [(n, inputs[n]) for n in _INS] + list(zip(("both", "first", "lower"), tables)):
        a = _np.ascontiguousarray(a)
        arrays[f"in_{name}"] = a
        aps[name] = nc.dram_tensor(f"in_{name}", a.shape, mybir.dt.from_np(a.dtype), kind="ExternalInput").ap()
    outs = [nc.dram_tensor(f"out_{i}", s, F32, kind="ExternalOutput").ap() for i, s in enumerate(_OUTS)]
    build(nc, aps, outs, *[t.shape[1] for t in tables])
    r = _run(nc, [arrays], core_ids=[0])
    return tuple(r.results[0][f"out_{i}"] for i in range(len(_OUTS)))
```
